# Optimizing a Trainium2 kernel written in Bass

```python
import jax, jax.numpy as jnp
from jax import lax
import numpy as np

D_MODEL = 1024
BATCH = 1
SEQ = 256
DEPTH = 1
DEC_BATCH = 8
DEC_SEQ = 1
PAST_LEN = 2048
PAGE_SIZE = 128

BRANCH_W = D_MODEL // 2
SWA_HEAD_DIM = 64
SWA_HEADS = BRANCH_W // SWA_HEAD_DIM
SWA_KV_HEADS = 2
WINDOW = 128
SWA_BLOCK = 128
GDN_HEAD_DIM = 128
GDN_HEADS = BRANCH_W // GDN_HEAD_DIM
CONV_WIDTH = 4
GDN_CHUNK = 64
MEM_LEN = 256
MEM_HEADS = 4
MEM_HEAD_DIM = BRANCH_W // MEM_HEADS
N_BRANCH = 3
N_EXPERTS = 32
TOP_K = 4
D_FF = D_MODEL
SWIGLU_LIMIT = 7.0
SWIGLU_ALPHA = 1.702
MOE_BLOCK = 128
EPS = 1e-6

SWA_Q_W = SWA_HEADS * SWA_HEAD_DIM
SWA_KV_W = SWA_KV_HEADS * SWA_HEAD_DIM
GDN_W = GDN_HEADS * GDN_HEAD_DIM
GDN_CONV_W = 3 * GDN_W
MEM_W = MEM_HEADS * MEM_HEAD_DIM
GATE_W = N_BRANCH * D_MODEL
IN_SPLITS = (SWA_Q_W, SWA_KV_W, SWA_KV_W, GDN_W, GDN_W, GDN_W, GDN_W, GDN_HEADS, GDN_HEADS, MEM_W, GATE_W)
IN_WIDTH = sum(IN_SPLITS)
IN_OFFSETS = tuple(int(o) for o in np.cumsum(IN_SPLITS)[:-1])

kernel_name = 'hybrid_swa_gdn_mem_moe_step'

F32 = jnp.float32

def rms_norm(x, gain):
    xf = x.astype(F32)
    y = xf * lax.rsqrt(jnp.mean(xf * xf, axis=-1, keepdims=True) + EPS) * gain.astype(F32)
    return y.astype(x.dtype)

def l2_norm(x):
    xf = x.astype(F32)
    return xf * lax.rsqrt(jnp.sum(xf * xf, axis=-1, keepdims=True) + EPS)

def alibi_slopes(n):
    return jnp.asarray(2.0 ** (-8.0 * np.arange(1, n + 1) / n), F32)

def sliding_window_attention(q, k_all, v_all, pos0, sinks):
    B, L, H, Dh = q.shape
    KVH = k_all.shape[2]
    G = H // KVH
    QB = SWA_BLOCK if L % SWA_BLOCK == 0 else L
    NB = L // QB
    KS = QB + WINDOW
    idx = np.arange(NB)[:, None] * QB + np.arange(KS)[None, :]
    kb = k_all[:, idx]
    vb = v_all[:, idx]
    qb = q.reshape(B, NB, QB, KVH, G, Dh)
    q_pos = pos0 + np.arange(L).reshape(NB, QB)
    k_pos = pos0 - WINDOW + idx
    dist = q_pos[:, :, None] - k_pos[:, None, :]
    valid = (dist >= 0) & (dist <= WINDOW) & (k_pos[:, None, :] >= 0)
    slopes = alibi_slopes(H).reshape(KVH, G)
    s = jnp.einsum('bnqkgd,bnskd->bnkgqs', qb, kb).astype(F32) * (Dh ** -0.5)
    s = s - slopes[None, None, :, :, None, None] * dist.astype(np.float32)[None, :, None, None, :, :]
    s = jnp.where(valid[None, :, None, None, :, :], s, -jnp.inf)
    sink = jnp.broadcast_to(sinks.astype(F32).reshape(1, 1, KVH, G, 1, 1), s.shape[:-1] + (1,))
    p = jax.nn.softmax(jnp.concatenate([s, sink], axis=-1), axis=-1)[..., :-1]
    o = jnp.einsum('bnkgqs,bnskd->bnqkgd', p.astype(vb.dtype), vb)
    return o.reshape(B, L, H * Dh)

def causal_conv_silu(x, prev, w):
    L = x.shape[1]
    xp = jnp.concatenate([prev.astype(x.dtype), x], axis=1)
    y = xp[:, 0:L] * w[0]
    for j in range(1, CONV_WIDTH):
        y = y + xp[:, j:j + L] * w[j]
    return jax.nn.silu(y), xp[:, -(CONV_WIDTH - 1):]

def _to_chunks(a, n, c):
    b, h = a.shape[0], a.shape[2]
    a = a.reshape((b, n, c, h) + a.shape[3:])
    return jnp.swapaxes(jnp.swapaxes(a, 0, 1), 2, 3)

def gated_delta_rule(q, k, v, g, beta, s0):
    B, L, H, DK = q.shape
    DV = v.shape[-1]
    C = GDN_CHUNK
    pad = (-L) % C
    n = (L + pad) // C

    def prep(a):
        a = a.astype(F32)
        a = jnp.pad(a, [(0, 0), (0, pad)] + [(0, 0)] * (a.ndim - 2))
        return _to_chunks(a, n, C)

    qc = prep(q) * (DK ** -0.5)
    kc, vc, gc, bc = prep(k), prep(v), prep(g), prep(beta)
    gcum = jnp.cumsum(gc, axis=-1)
    incl = np.tril(np.ones((C, C), bool))
    strict = np.tril(np.ones((C, C), bool), -1)
    gdiff = gcum[..., :, None] - gcum[..., None, :]
    decay = jnp.where(incl, jnp.exp(jnp.where(incl, gdiff, 0.0)), 0.0)
    kb = kc * bc[..., None]
    a_mat = jnp.where(strict, jnp.einsum('nbhik,nbhjk->nbhij', kb, kc) * decay, 0.0)
    eye = jnp.eye(C, dtype=F32)
    t_mat = lax.linalg.triangular_solve(eye + a_mat, jnp.broadcast_to(eye, a_mat.shape),
                                        left_side=True, lower=True, unit_diagonal=True)
    u = jnp.einsum('nbhij,nbhjv->nbhiv', t_mat, vc * bc[..., None])
    w = jnp.einsum('nbhij,nbhjk->nbhik', t_mat, kb * jnp.exp(gcum)[..., None])
    intra = jnp.where(incl, jnp.einsum('nbhik,nbhjk->nbhij', qc, kc) * decay, 0.0)

    def step(s, inp):
        q_i, k_i, u_i, w_i, g_i, a_i = inp
        v_new = u_i - jnp.einsum('bhck,bhkv->bhcv', w_i, s)
        o = (jnp.einsum('bhck,bhkv->bhcv', q_i * jnp.exp(g_i)[..., None], s)
             + jnp.einsum('bhij,bhjv->bhiv', a_i, v_new))
        g_last = g_i[..., -1:]
        s = (s * jnp.exp(g_last)[..., None]
             + jnp.einsum('bhck,bhcv->bhkv', k_i * jnp.exp(g_last - g_i)[..., None], v_new))
        return s, o

    s_fin, o = lax.scan(step, s0.astype(F32), (qc, kc, u, w, gcum, intra))
    o = jnp.transpose(o, (1, 0, 3, 2, 4)).reshape(B, n * C, H, DV)[:, :L]
    return o, s_fin

def memory_kv(mem, mem_norm, w_mem_kv, k_norm_mem):
    B, M, _ = mem.shape
    kv = rms_norm(mem, mem_norm) @ w_mem_kv
    k, v = jnp.split(kv, 2, axis=-1)
    k = rms_norm(k.reshape(B, M, MEM_HEADS, MEM_HEAD_DIM), k_norm_mem)
    return k, v.reshape(B, M, MEM_HEADS, MEM_HEAD_DIM)

def memory_attention(q, mem_k, mem_v):
    s = jnp.einsum('blhd,bmhd->bhlm', q, mem_k.astype(q.dtype)).astype(F32) * (q.shape[-1] ** -0.5)
    p = jax.nn.softmax(s, axis=-1)
    o = jnp.einsum('bhlm,bmhd->blhd', p.astype(q.dtype), mem_v.astype(q.dtype))
    return o.reshape(q.shape[0], q.shape[1], -1)

def moe_ffn(x2, w_router, b_router, w_mlp1, b_mlp1, w_mlp2, b_mlp2):
    T, D = x2.shape
    logits = x2.astype(F32) @ w_router.astype(F32) + b_router.astype(F32)
    top_val, top_idx = lax.top_k(logits, TOP_K)
    gate = jax.nn.softmax(top_val, axis=-1)
    n_rows = T * TOP_K
    flat_e = top_idx.reshape(-1).astype(jnp.int32)
    flat_tok = jnp.repeat(jnp.arange(T, dtype=jnp.int32), TOP_K)
    flat_g = gate.reshape(-1)
    order = jnp.argsort(flat_e)
    se, stok, sg = flat_e[order], flat_tok[order], flat_g[order]
    counts = jax.ops.segment_sum(jnp.ones((n_rows,), jnp.int32), flat_e, num_segments=N_EXPERTS)
    starts = jnp.cumsum(counts) - counts
    padded = (counts + MOE_BLOCK - 1) // MOE_BLOCK * MOE_BLOCK
    pends = jnp.cumsum(padded)
    pstarts = pends - padded
    dest = pstarts[se] + jnp.arange(n_rows, dtype=jnp.int32) - starts[se]
    n_blocks = -(-n_rows // MOE_BLOCK) + N_EXPERTS
    n_slots = n_blocks * MOE_BLOCK
    slot_tok = jnp.zeros((n_slots,), jnp.int32).at[dest].set(stok)
    slot_gate = jnp.zeros((n_slots,), F32).at[dest].set(sg)
    block_e = jnp.minimum(jnp.searchsorted(pends, jnp.arange(n_blocks, dtype=jnp.int32) * MOE_BLOCK, side='right'),
                          N_EXPERTS - 1)

    def expert_block(args):
        tok, gb, e = args
        hmid = x2[tok] @ w_mlp1[e] + b_mlp1[e]
        glu = jnp.minimum(hmid[:, :D_FF], SWIGLU_LIMIT)
        lin = jnp.clip(hmid[:, D_FF:], -SWIGLU_LIMIT, SWIGLU_LIMIT)
        act = glu * jax.nn.sigmoid(SWIGLU_ALPHA * glu) * (lin + 1.0)
        y = act @ w_mlp2[e] + b_mlp2[e]
        return y.astype(F32) * gb[:, None]

    ys = lax.map(expert_block, (slot_tok.reshape(n_blocks, MOE_BLOCK), slot_gate.reshape(n_blocks, MOE_BLOCK), block_e))
    out = jnp.zeros((T, D), F32).at[slot_tok].add(ys.reshape(n_slots, D))
    return out.astype(x2.dtype)

def hybrid_layer(x, pos0, win_k, win_v, gdn_state, conv_state, mem_k, mem_v,
                 ln1_gain, w_in, q_norm_swa, k_norm_swa, swa_sinks, conv_w, a_log, dt_bias, gdn_norm,
                 q_norm_mem, w_branch, w_out, ln2_gain, w_router, b_router, w_mlp1, b_mlp1, w_mlp2, b_mlp2):
    B, L, D = x.shape
    h = rms_norm(x, ln1_gain)
    proj = h @ w_in
    (q_s, k_s, v_s, q_g, k_g, v_g, z_g, a_g, b_g, q_m, gate_logits) = jnp.split(proj, IN_OFFSETS, axis=-1)

    q_s = rms_norm(q_s.reshape(B, L, SWA_HEADS, SWA_HEAD_DIM), q_norm_swa)
    k_s = rms_norm(k_s.reshape(B, L, SWA_KV_HEADS, SWA_HEAD_DIM), k_norm_swa)
    v_s = v_s.reshape(B, L, SWA_KV_HEADS, SWA_HEAD_DIM)
    k_all = jnp.concatenate([win_k.astype(k_s.dtype), k_s], axis=1)
    v_all = jnp.concatenate([win_v.astype(v_s.dtype), v_s], axis=1)
    o_swa = sliding_window_attention(q_s, k_all, v_all, pos0, swa_sinks)
    new_win_k, new_win_v = k_all[:, -WINDOW:], v_all[:, -WINDOW:]

    qkv, new_conv = causal_conv_silu(jnp.concatenate([q_g, k_g, v_g], axis=-1), conv_state, conv_w)
    qg, kg, vg = jnp.split(qkv, [GDN_W, 2 * GDN_W], axis=-1)
    qg = l2_norm(qg.reshape(B, L, GDN_HEADS, GDN_HEAD_DIM))
    kg = l2_norm(kg.reshape(B, L, GDN_HEADS, GDN_HEAD_DIM))
    vg = vg.reshape(B, L, GDN_HEADS, GDN_HEAD_DIM)
    beta = jax.nn.sigmoid(b_g.astype(F32))
    g = -jnp.exp(a_log.astype(F32)) * jax.nn.softplus(a_g.astype(F32) + dt_bias.astype(F32))
    o_g, new_s = gated_delta_rule(qg, kg, vg, g, beta, gdn_state)
    o_g = rms_norm(o_g.astype(x.dtype), gdn_norm) * jax.nn.silu(z_g.reshape(B, L, GDN_HEADS, GDN_HEAD_DIM))

    q_m = rms_norm(q_m.reshape(B, L, MEM_HEADS, MEM_HEAD_DIM), q_norm_mem)
    o_m = memory_attention(q_m, mem_k, mem_v)

    branches = jnp.stack([o_swa, o_g.reshape(B, L, GDN_W), o_m], axis=2)
    gates = jax.nn.sigmoid(gate_logits.reshape(B, L, N_BRANCH, D))
    mixed = jnp.einsum('blnc,ncd->blnd', branches, w_branch)
    x = x + jnp.sum(gates * mixed, axis=2) @ w_out

    h2 = rms_norm(x, ln2_gain)
    x = x + moe_ffn(h2.reshape(B * L, D), w_router, b_router, w_mlp1, b_mlp1, w_mlp2, b_mlp2).reshape(B, L, D)
    return x, new_win_k, new_win_v, new_s.astype(gdn_state.dtype), new_conv

def setup_inputs(seed: int = 0) -> dict:
    key = jax.random.key(seed)
    ks = iter(jax.random.split(key, 40))

    def nrm(shape, scale):
        return scale * jax.random.normal(next(ks), shape, F32)

    def gain(shape):
        return 1.0 + nrm(shape, 0.02)

    a_log = jnp.log(jax.random.uniform(next(ks), (DEPTH, GDN_HEADS), F32, 1.0, 16.0))
    dt = jnp.exp(jax.random.uniform(next(ks), (DEPTH, GDN_HEADS), F32, float(np.log(1e-3)), float(np.log(1e-1))))
    dt_bias = dt + jnp.log(-jnp.expm1(-dt))
    return {
        'x_prompt': nrm((BATCH, SEQ, D_MODEL), 1.0),
        'x_sample': nrm((DEC_BATCH, DEC_SEQ, D_MODEL), 1.0),
        'cache_swa_k': nrm((DEPTH, DEC_BATCH, WINDOW, SWA_KV_HEADS, SWA_HEAD_DIM), 1.0),
        'cache_swa_v': nrm((DEPTH, DEC_BATCH, WINDOW, SWA_KV_HEADS, SWA_HEAD_DIM), 1.0),
        'state_gdn': nrm((DEPTH, DEC_BATCH, GDN_HEADS, GDN_HEAD_DIM, GDN_HEAD_DIM), 0.1),
        'state_conv': nrm((DEPTH, DEC_BATCH, CONV_WIDTH - 1, GDN_CONV_W), 1.0),
        'cache_mem_k': nrm((DEPTH, DEC_BATCH, MEM_LEN, MEM_HEADS, MEM_HEAD_DIM), 1.0),
        'cache_mem_v': nrm((DEPTH, DEC_BATCH, MEM_LEN, MEM_HEADS, MEM_HEAD_DIM), 1.0),
        'mem_prompt': nrm((BATCH, MEM_LEN, D_MODEL), 1.0),
        'ln1_gain': gain((DEPTH, D_MODEL)),
        'w_in': nrm((DEPTH, D_MODEL, IN_WIDTH), D_MODEL ** -0.5),
        'q_norm_swa': gain((DEPTH, SWA_HEAD_DIM)),
        'k_norm_swa': gain((DEPTH, SWA_HEAD_DIM)),
        'swa_sinks': nrm((DEPTH, SWA_HEADS), 0.5),
        'conv_w': nrm((DEPTH, CONV_WIDTH, GDN_CONV_W), CONV_WIDTH ** -0.5),
        'a_log': a_log,
        'dt_bias': dt_bias,
        'gdn_norm': gain((DEPTH, GDN_HEAD_DIM)),
        'q_norm_mem': gain((DEPTH, MEM_HEAD_DIM)),
        'k_norm_mem': gain((DEPTH, MEM_HEAD_DIM)),
        'mem_norm': gain((DEPTH, D_MODEL)),
        'w_mem_kv': nrm((DEPTH, D_MODEL, 2 * MEM_W), D_MODEL ** -0.5),
        'w_branch': nrm((DEPTH, N_BRANCH, BRANCH_W, D_MODEL), BRANCH_W ** -0.5),
        'w_out': nrm((DEPTH, D_MODEL, D_MODEL), D_MODEL ** -0.5),
        'ln2_gain': gain((DEPTH, D_MODEL)),
        'w_router': nrm((DEPTH, D_MODEL, N_EXPERTS), D_MODEL ** -0.5),
        'b_router': nrm((DEPTH, N_EXPERTS), 0.01),
        'w_mlp1': nrm((DEPTH, N_EXPERTS, D_MODEL, 2 * D_FF), D_MODEL ** -0.5),
        'b_mlp1': nrm((DEPTH, N_EXPERTS, 2 * D_FF), 0.01),
        'w_mlp2': nrm((DEPTH, N_EXPERTS, D_FF, D_MODEL), D_FF ** -0.5),
        'b_mlp2': nrm((DEPTH, N_EXPERTS, D_MODEL), 0.01),
    }

def reference(x_prompt, x_sample, cache_swa_k, cache_swa_v, state_gdn, state_conv, cache_mem_k, cache_mem_v,
              mem_prompt, ln1_gain, w_in, q_norm_swa, k_norm_swa, swa_sinks, conv_w, a_log, dt_bias, gdn_norm,
              q_norm_mem, k_norm_mem, mem_norm, w_mem_kv, w_branch, w_out, ln2_gain, w_router, b_router,
              w_mlp1, b_mlp1, w_mlp2, b_mlp2):
    xp, xs = x_prompt, x_sample
    Bp = xp.shape[0]
    swa_kp, swa_vp, swa_ks, swa_vs = [], [], [], []
    gdn_p, gdn_s, conv_p, conv_s, mem_kp, mem_vp = [], [], [], [], [], []
    for l in range(DEPTH):
        lw = (ln1_gain[l], w_in[l], q_norm_swa[l], k_norm_swa[l], swa_sinks[l], conv_w[l], a_log[l], dt_bias[l],
              gdn_norm[l], q_norm_mem[l], w_branch[l], w_out[l], ln2_gain[l], w_router[l], b_router[l],
              w_mlp1[l], b_mlp1[l], w_mlp2[l], b_mlp2[l])
        mk, mv = memory_kv(mem_prompt, mem_norm[l], w_mem_kv[l], k_norm_mem[l])
        zero_win = jnp.zeros((Bp, WINDOW, SWA_KV_HEADS, SWA_HEAD_DIM), xp.dtype)
        zero_s = jnp.zeros((Bp, GDN_HEADS, GDN_HEAD_DIM, GDN_HEAD_DIM), xp.dtype)
        zero_conv = jnp.zeros((Bp, CONV_WIDTH - 1, GDN_CONV_W), xp.dtype)
        xp, pk, pv, ps, pc = hybrid_layer(xp, 0, zero_win, zero_win, zero_s, zero_conv, mk, mv, *lw)
        xs, sk, sv, ss, sc = hybrid_layer(xs, PAST_LEN, cache_swa_k[l], cache_swa_v[l], state_gdn[l], state_conv[l],
                                          cache_mem_k[l], cache_mem_v[l], *lw)
        swa_kp.append(pk); swa_vp.append(pv); swa_ks.append(sk); swa_vs.append(sv)
        gdn_p.append(ps); gdn_s.append(ss); conv_p.append(pc); conv_s.append(sc)
        mem_kp.append(mk); mem_vp.append(mv)
    return (xp, xs,
            jnp.stack(swa_kp), jnp.stack(swa_vp), jnp.stack(swa_ks), jnp.stack(swa_vs),
            jnp.stack(gdn_p), jnp.stack(gdn_s), jnp.stack(conv_p), jnp.stack(conv_s),
            jnp.stack(mem_kp), jnp.stack(mem_vp))


_drawn_inputs = setup_inputs


def setup_inputs(seed=0):
    import zlib

    import numpy as np

    out = dict(_drawn_inputs(seed))
    spreads = {}
    factors = {'q_norm_swa': 17.095,
     'k_norm_swa': 2.918,
     'q_norm_mem': 8.0,
     'k_norm_mem': 2.913,
     'mem_norm': 2.931,
     'b_mlp1': 8.0,
     'b_mlp2': 23.529,
     'swa_sinks': 52.443,
     'gdn_norm': 16.294,
     'b_router': 3.923,
     'ln2_gain': 3.119}
    for name, (base, spread) in spreads.items():
        noise = np.random.default_rng([zlib.crc32(name.encode()), seed]).standard_normal(out[name].shape)
        drawn = base * np.exp(spread * noise) if base else spread * noise
        out[name] = __import__('jax').numpy.asarray(drawn.astype(out[name].dtype))
    for name, factor in factors.items():
        out[name] = (out[name] * factor).astype(out[name].dtype)
    return out
```

```python
from contextlib import ExitStack

import concourse.bass as bass
from concourse import mybir

F32 = mybir.dt.float32
BF16 = mybir.dt.bfloat16
I32 = mybir.dt.int32
U32 = mybir.dt.uint32
ALU = mybir.AluOpType
ACT = mybir.ActivationFunctionType
AX = mybir.AxisListType.X
PE_ENGINE = mybir.EngineType.PE

P = 128
D = 1024
KD = D // P
NP_TOK = 256
NB = 8
T = NP_TOK + NB
EPS = 1e-6
NEG = -1e30
HD_S, H_S, KV_S, WIN = 64, 8, 2, 128
HD_G, H_G = 128, 4
HD_M, H_M, MEM = 128, 4, 256
N_EXP, TOP_K = 32, 4
LIMIT, ALPHA = 7.0, 1.702
SLOTS, SLOT = 12, 2048
BLK = 64
EXTRA = 16
N_ITEM = N_EXP + EXTRA + 1
CONV_FLAT = 3 + NP_TOK + 4 * NB
OFF_QS, OFF_QG, OFF_AB, OFF_QM, OFF_GATE = 0, 768, 2816, 2824, 3336
TOK = [(0, P), (P, P), (2 * P, NB)]


INVERSE = [
    ("turn", 0, None, ("parts",)),
    ("mult", 0, 1, ("copy", 4)),
    ("turn", 4, None, ("copy", 5)),
    ("mult", 5, 4, ("copy", 0)),
    ("turn", 0, None, ("copy", 1)),
    ("mult", 1, 0, ("copy", 4)),
    ("turn", 4, None, ("copy", 4)),
    ("mult", 5, 3, ("add", 3)),
    ("mult", 1, 3, ("add", 3)),
    ("mult", 4, 3, ("add", 3)),
    ("turn", 3, None, ("copy", 4)),
    ("mult", 4, 2, ("copy", 0)),
    ("turn", 0, None, ("copy", 1)),
    ("mult", 1, 0, ("copy", 2)),
    ("turn", 2, None, ("copy", 4)),
    ("mult", 4, 2, ("copy", 5)),
    ("turn", 5, None, ("copy", 5)),
    ("mult", 5, 3, ("add", 3)),
    ("mult", 4, 3, ("add", 3)),
    ("mult", 1, 3, ("subtract", 3)),
    ("turn", 3, None, ("copy", 3)),
]


CHAINS = {
    "pe_load": [("x_T", 16), ("prm_T", 1), ("cst_T", 1)],
    "pe_small": [("ab_ps", 1), ("ab_nT", 1), ("kmT_ps", 2), ("conv_rows_ps", 3)],
    "pe_scores": [("mm_s", 8), ("swa_nat", 2), ("sw_s", 8)],
    "pe_turned": [("mm_pT_ps", 8), ("sw_pT_ps", 8)],
    "pe_outputs": [("mm_o_ps", 8), ("sw_o_ps", 8)],
    "pe_window": [("ss_kT_ps", 2), ("ss_new", 1), ("ss_s", 1), ("ss_rows", 1), ("ss_pT_ps", 1), ("ss_o_ps", 1)],
    "pe_delta": [("gd_cum", 1), ("gd_row", 2), ("gd_brow", 2), ("gd_kk", 2), ("gd_qk", 2), ("gd_kn", 2), ("gd_vn", 2),
                 ("inv_ps", 2 * len(INVERSE)), ("gd_v0", 1), ("gd_s1", 1), ("gd_o0", 1), ("gd_ks", 1), ("gd_v1", 1),
                 ("gd_o1", 1), ("gd_s2", 1), ("gs_ps", 1), ("gs_rows", 1), ("gs_outer", 8)],
    "pe_memory": [("ms_q_ps", 1), ("ms_qb", 8), ("ms_rows", 1), ("ms_pT_ps", 1), ("ms_o_ps", 8), ("ms_oT", 2)],
    "pe_router": [("out_ps", 8), ("lg_ps", 1), ("h2_nat_ps", 6), ("lg_nat", 1), ("rank", 1), ("gateT_ps", 1),
                  ("posT_ps", 1), ("more_ps", 1), ("hot_ps", 1), ("tables", 1), ("b1_ps", 2), ("b2_ps", 8)],
    "act_small": [("tr_evac_act", 8), ("kn_sq", 1), ("kn_rt", 1), ("ab_T", 1), ("z_sg", 1), ("dc_act", 1),
                  ("KmT_ready", 2), ("conv_rows_ready", 3)],
    "act_attend": [("mm_e", 1), ("mm_pT", 8), ("sw_e", 1), ("sw_pT", 8), ("ss_kT", 2), ("ss_e", 1)],
    "act_delta": [("gd_exp", 1), ("gs_eg", 1), ("gd_erow", 1), ("gd_dec_e", 1), ("gd_kdec", 2), ("gd_vbeta", 2),
                  ("gd_v0_evac", 1), ("gd_v1_evac", 1)],
    "act_late": [("ms_e", 1), ("ms_o_evac", 2), ("lgT", 1), ("top_e", 1)],
    "dve_load": [("eps", 1), ("tr_evac_dve", 8), ("colp_ready", 1), ("cst_done", 1), ("cin_ready", 1),
                 ("hT_ready", 8), ("memTn_ready", 8), ("kn_ss", 1), ("memkv_ready", 1)],
    "dve_small": [("conv_saved", 1), ("ab_done", 1), ("dc", 1), ("decay_ready", 1)],
    "dve_attend": [("mm_s_evac", 8), ("mm_m", 1), ("mm_p", 1), ("mm_o", 4), ("k_dup", 1), ("swa_rows_ready", 2),
                   ("sw_s_evac", 8), ("sw_m", 1), ("sw_p", 1), ("sw_o", 4)],
    "dve_window": [("ss_q", 1), ("ss_sT", 1), ("ss_m", 1), ("ss_p", 1), ("ss_pT", 1), ("ss_done", 1)],
    "dve_delta": [("gd_cum_evac", 1), ("gd_small", 1), ("gd_min", 1), ("gd_dec", 2), ("gd_at", 2), ("gd_qk_done", 2),
                  ("inv", 2 * len(INVERSE)), ("gd_s1_evac", 1), ("gd_r", 1), ("gdn_state_ready", 1), ("gs_kq", 1),
                  ("gs_v", 1)],
    "dve_memory": [("ms_q", 1), ("ms_m", 1), ("ms_p", 1), ("ms_pT", 1), ("ms_done", 1), ("o_ready", 1)],
    "dve_router": [("x1", 8), ("h2_ready", 8), ("top", 1), ("sel", 1), ("pos_ready", 1),
                   ("more", 1), ("hot", 1), ("items_ready", 1), ("gateT", 1), ("tables_done", 1)],
}


PRIMED = ("put_ps", "part_ready", "put", "y_evac", "h_sum", "acc_done")


def build_layer(nc, A, O):
    with ExitStack() as ctx:
        build_program(nc, ctx, A, O)


def build_program(nc, ctx, A, O):
    sems, signalled = {}, {}
    where = {name: (chain, i) for chain, steps in CHAINS.items() for i, (name, _) in enumerate(steps)}

    def handle(name):
        if name not in sems:
            sems[name] = ctx.enter_context(nc.semaphore(name))
        return sems[name]

    def sem(name):
        if name not in where:
            return handle(name)
        chain, i = where[name]
        signalled[name] = signalled.get(name, 0) + 1
        for before_it, count in CHAINS[chain][:i]:
            assert signalled.get(before_it, 0) == count, (name, before_it)
        assert signalled[name] <= CHAINS[chain][i][1], name
        return handle(chain)

    def at(name, n):
        if name not in where:
            return handle(name), n + (name in PRIMED)
        chain, i = where[name]
        return handle(chain), sum(count for _, count in CHAINS[chain][:i]) + n

    made = {}

    def link(eng, name, ins):
        made[name] = made.get(name, 0) + 1
        ins.then_inc(sem(name), 1)
        eng.wait_ge(*at(name, made[name]))

    ring = ctx.enter_context(nc.sbuf_tensor("ring", [P, SLOTS, SLOT], F32))
    ARENA = 28600
    arena = ctx.enter_context(nc.sbuf_tensor("arena", [P, ARENA], F32))
    top = [0]

    def take(n):
        top[0] += n
        assert top[0] <= ARENA, top[0]
        return arena[:, top[0] - n:top[0]]

    def cols(region, a, n):
        return region[:, a:a + n]

    def grid(v, n):
        return v.rearrange("p (k n) -> p k n", n=n)

    ident, ones, blk64 = take(P), take(P), take(P)
    tri_incl, tri_strict, diag16 = take(P), take(P), take(P)
    neg_dist = take(3 * P)
    neg_dist_s = take(P)
    slot_iota = take(P)
    iota32 = take(32)
    colp = take(80)
    sink_b, alog_b, dt_b, brow_b = take(8), take(4), take(4), take(32)
    eps_col, thr_col, e_col = take(1), take(1), take(1)
    w_ab = grid(take(64), 8)
    w_rt = grid(take(256), 32)
    ab_T = take(T)
    ab_n = grid(take(24), 8)
    g_n, beta_n, gt0, gt1 = (grid(take(12), 4) for _ in range(4))
    conv_save = take(12 * 27)
    stat = take(160)
    xT_flat, hT_flat = take(KD * T), take(KD * T)
    xT, hT = grid(xT_flat, T), grid(hT_flat, T)
    at_qsk = top[0]
    qsk_flat = take(5 * T)
    vsT = take(T)
    qsk = grid(qsk_flat, T)
    region_q = arena[:, at_qsk:at_qsk + 6 * T]
    at_cv = top[0]
    cv_flat, zT_flat, qm_flat = take(12 * T), take(4 * T), take(4 * T)
    cv, zT, qm = grid(cv_flat, T), grid(zT_flat, T), grid(qm_flat, T)
    int_tmp, prm = cols(zT_flat, 0, 3 * P).bitcast(I32), cols(zT_flat, 3 * P, P)
    region_cv = arena[:, at_cv:at_cv + 20 * T]
    G_flat = take(KD * T)
    G = grid(G_flat, T)
    oT_flat = take(12 * T)
    oT = grid(oT_flat, T)
    at_mem = top[0]
    Kn_flat, Vm_flat, KmT_flat = take(1024), take(1024), take(1024)
    knorm_b = cols(KmT_flat, 0, P)
    region_mem = arena[:, at_mem:at_mem + 3072]
    scr = take(6400)

    x_nat = grid(cols(scr, 0, 2048), D)
    xs_nat = cols(scr, 2048, 1024)
    mem_nat = grid(cols(scr, 3072, 2048), D)
    memT = grid(cols(oT_flat, 0, 2048), NP_TOK)
    memTn = grid(cols(cv_flat, 0, 2048), NP_TOK)
    rsx, rsm = cols(Kn_flat, 0, T), cols(Kn_flat, 512, NP_TOK)
    cst_nat = cols(region_q, 0, 1536)
    cin = grid(cols(scr, 0, 12 * CONV_FLAT), CONV_FLAT)
    conv_y = grid(cols(scr, 3492, 576), 288)
    conv_sg = grid(cols(oT_flat, 2112, 576), 288)
    rt = grid(cols(scr, 4288, KD * T), T)
    cso = cols(oT_flat, 0, 1536)
    Kn, Vm = grid(Kn_flat, 512), grid(Vm_flat, 512)
    KmT = grid(KmT_flat, NP_TOK)

    B = [ctx.enter_context(nc.psum_tensor(f"bank{i}", [P, 512], F32)) for i in range(8)]

    LN1, LN2, LNM, C_GDN, C_QM, C_QS, C_KS, C_CONV = 0, 8, 16, 24, 25, 26, 27, 28

    w_in, w_mkv, w_br, w_out = A["w_in"][0], A["w_mem_kv"][0], A["w_branch"][0], A["w_out"][0]

    def columns(w, a):
        return [(0, SLOT, 256, w[:, a:a + 256].rearrange("(k p) n -> p k n", p=P))]

    pieces = [columns(w_mkv, 256 * i) for i in range(4)]
    PC_QM = len(pieces)
    pieces += [columns(w_in, OFF_QM + 256 * i) for i in range(2)]
    PC_IN = len(pieces)
    pieces += [columns(w_in, 256 * i) for i in range(OFF_AB // 256)]
    PC_SWA = len(pieces)
    pieces.append([(0, 1024, P, A["cache_swa_k"][0].rearrange("b w k d -> w b (k d)")),
                   (1024, 1024, P, A["cache_swa_v"][0].rearrange("b w k d -> w b (k d)"))])
    PC_STATE = len(pieces)
    state = A["state_gdn"][0].rearrange("b h k v -> k (b h) v")
    pieces += [[(0, SLOT, HD_G, state[:, 16 * i:16 * i + 16, :])] for i in range(2)]
    PC_MK = len(pieces)
    for name in ("cache_mem_k", "cache_mem_v"):
        v = A[name][0].rearrange("b (c m) h d -> m (b c) (h d)", m=P)
        pieces += [[(0, SLOT, 512, v[:, 4 * i:4 * i + 4, :])] for i in range(4)]
    PC_MV = PC_MK + 4
    PC_GATE = []
    for n in range(3):
        PC_GATE.append(len(pieces))
        pieces += [columns(w_in, OFF_GATE + D * n + 256 * i) for i in range(4)]
        v = w_br[n].rearrange("(c p) d -> p c d", p=P)
        pieces += [[(0, SLOT, 512, v[:, :, 512 * i:512 * i + 512])] for i in range(2)]
    PC_OUT = len(pieces)
    pieces += [columns(w_out, 256 * i) for i in range(4)]
    N_PRE = len(pieces)
    landed_at, before = [], [0] * SLOTS
    for i, dmas in enumerate(pieces):
        before[i % SLOTS] += 16 * len(dmas)
        landed_at.append(before[i % SLOTS])
    landed_pre = list(before)
    landed = [sem(f"landed{s}") for s in range(SLOTS)]

    release = [("proj", 2 * i + 2) for i in range(PC_SWA)]
    release += [("ss_o_ps", 1), ("state_used", 1), ("state_used", 2)]
    release += [("ms_mul", 2 * i + 2) for i in range(4)] + [("ms_o_ps", 2 * i + 2) for i in range(4)]
    for n in range(3):
        release += [("proj", 34 + 8 * n + 2 * i + 2) for i in range(4)] + [("branch", 8 * n + 4 * i + 4) for i in range(2)]
    release += [("out_ps", 2 * i + 2) for i in range(4)]

    def slot(i):
        return ring[:, i % SLOTS, :]

    def has_landed(eng, i):
        eng.wait_ge(landed[i % SLOTS], landed_at[i])

    def expert_slot(p):
        return (N_PRE + p) % SLOTS

    n_store = [0]

    HN = [4, 5, 8, 4]
    HN_BASE = [0, 4, 9, 17]

    block = ctx.enter_context(nc.Block())

    sw_s = cols(scr, 0, H_S * 3 * P)
    sw_s3 = grid(sw_s, 3 * P)
    sw_pT = grid(cols(scr, 3072, 2 * 3 * P), 3 * P)
    k_dup = grid(cols(scr, 3840, 2 * T), T)
    kv_nat = cols(scr, 4368, 3 * P)
    kv_s = cols(scr, 4752, 2 * P)
    mm_s = grid(cols(scr, 0, 8 * NP_TOK), NP_TOK)
    mm_pT = grid(cols(scr, 2048, 2 * NP_TOK), NP_TOK)
    sw_kT = grid(cols(scr, 0, 1024), P)
    q_bd = cols(scr, 1024, 64)
    q_bd3 = q_bd.rearrange("p (b h) -> p b h", h=H_S)
    ss_prod = cols(scr, 1088, 64)
    ss_prod3 = ss_prod.rearrange("p (b h) -> p b h", h=H_S)
    rows64 = cols(scr, 1664, 128)
    ss_T = cols(scr, 1152, 64)
    ss = cols(scr, 1216, P + 1)
    ss_pT = cols(scr, 1408, 64)
    ss_pb = cols(scr, 1472, P)
    ss_o = cols(scr, 1600, 64)
    ss_o3 = ss_o.rearrange("p (b h) -> p b h", h=H_S)
    inv = [grid(cols(scr, 1024 * i, 1024), P) for i in range(6)]
    inv_flat = [cols(scr, 1024 * i, 1024) for i in range(6)]
    dec_flat, intra_flat = cols(G_flat, 0, 1024), cols(G_flat, 1024, 1024)
    dec, intra = grid(dec_flat, P), grid(intra_flat, P)
    k_dec, v_beta = grid(Kn_flat, P), grid(Vm_flat, P)
    v_new = grid(cols(KmT_flat, 0, 512), P)
    s_one = grid(cols(KmT_flat, 512, 512), P)
    q_dec, r_new, e_row = (grid(cols(region_q, 512 * i, 512), P) for i in range(3))
    g_sm = cols(scr, 6144, 64)
    s_out = cols(scr, 0, 4096)
    s_out3 = grid(s_out, P)
    vn_mask = [grid(cols(scr, 4096 + 1024 * i, 1024), P) for i in range(2)]
    gs = cols(scr, 6144, 256)
    gs_kq = gs[:, 0:64].rearrange("p (n c) -> p n c", c=2)
    gs_qk, gs_bc = gs[:, 64:96], gs[:, 96:192]
    gs_vn, gs_t = gs[:, 192:224], gs[:, 224:256]
    gs_nat = cols(region_q, 0, 2 * P)
    gs_dg = cols(region_q, 256, 64)
    pick8 = grid(cols(scr, 0, 1024), P)
    q_nat8 = cols(scr, 1024, 512)
    mk_prod = grid(cols(scr, 1536, 1024), P)
    ms_T = cols(scr, 2560, 64)
    ms = cols(scr, 2624, NP_TOK)
    ms_pT = cols(scr, 2880, 64)
    ms_pv = grid(cols(scr, 2944, 1024), 512)
    mT = grid(cols(cv_flat, 0, KD * T), T)
    mtmp = grid(cols(scr, 0, 2 * T), T)
    h2_nat = grid(cols(oT_flat, 0, 3 * D), D)
    h2_parts = cols(region_cv, 0, 4608).bitcast(BF16).rearrange("p (s c d) -> p s c d", s=3, d=D)
    h2_tmp = cols(scr, 4096, 2048)
    b1_nat, b2_nat = cols(scr, 0, 2048), cols(scr, 2048, 1024)
    rr = cols(scr, 3072, 1024)
    lgT, gateT, posT = rr[:, 0:T], rr[:, T:2 * T], rr[:, 2 * T:3 * T]
    lg_n = grid(rr[:, 800:896], 32)
    rr_b = rr[:, 896:1024]
    top_v, top_f, top_p = grid(cols(G_flat, 1400, 24), 8), grid(cols(G_flat, 1424, 24), 8), grid(cols(G_flat, 1448, 12), 4)
    top_i = cols(G_flat, 1472, 24).bitcast(U32).rearrange("p (c n) -> p c n", n=8)
    gate_n, sel_n, pos_n = (grid(cols(G_flat, 96 * i, 96), 32) for i in range(3))
    sel4 = cols(G_flat, 288, 384).rearrange("p (c r e) -> p c r e", c=3, r=4)
    rtmp = cols(G_flat, 672, 32)
    more_f, more_pos = cols(G_flat, 704, 1), cols(G_flat, 705, 1)
    item_hot = cols(G_flat, 706, 16)
    thr_b = cols(G_flat, 722, P)
    e_mod = cols(G_flat, 850, 32)
    item_oh = cols(G_flat, 882, N_ITEM)
    item_off = cols(G_flat, 931, 16)
    top_s = cols(G_flat, 1480 + 16, 12)
    item_f = cols(G_flat, 1510, 20)
    used_cols = [0]

    def moe(n):
        used_cols[0] += n
        assert used_cols[0] <= 3072
        return cols(region_mem, used_cols[0] - n, n)

    item_pos, item_gate = (grid(moe(3 * N_ITEM), N_ITEM) for _ in range(2))
    item_b1 = grid(moe(16 * N_ITEM), 16)
    item_int = moe(18).bitcast(I32)
    item_count, item_expert = item_int[:, 0:1], item_int[:, 2:18]
    pick = moe(96).bitcast(BF16).rearrange("p (c n) -> p c n", n=BLK)
    gpick = grid(moe(3 * P), P)
    xg = grid(moe(512), BLK)
    put = moe(T)
    h_odd, h_sum = cols(scr, 0, 2048), cols(scr, 2048, 2048)
    glu, lin, sg, act_e = (cols(scr, 4096 + 512 * i, 512) for i in range(4))
    y_e = cols(region_q, 0, 1024)
    part_flat = hT_flat
    part = hT
    y_out = h2_nat

    def bc(v, n):
        return v.unsqueeze(len(v.shape)).broadcast_to([*v.shape, n])

    def mid(v, n):
        return v.unsqueeze(1).broadcast_to([v.shape[0], n, v.shape[1]])

    @block.sync
    def _(sp):
        sp.dma_start(x_nat, A["x_prompt"][0].rearrange("(c p) d -> p c d", p=P)).then_inc(sem("x_landed"), 16)
        sp.dma_start(mem_nat, A["mem_prompt"][0].rearrange("(c p) d -> p c d", p=P)).then_inc(sem("mem_landed"), 16)
        for i, dmas in enumerate(pieces):
            if i >= SLOTS:
                sp.wait_ge(*at(*release[i - SLOTS]))
            for a, n, w, src in dmas:
                sp.dma_start(grid(slot(i)[:, a:a + n], w), src).then_inc(landed[i % SLOTS], 16)

        w1 = A["w_mlp1"][0].rearrange("e (k p) n -> e k p n", p=P)
        w2 = A["w_mlp2"][0].rearrange("e (j k p) n -> e j p k n", p=P, k=2)

        def load_expert(e, item):
            for p in range(SLOTS):
                s = expert_slot(p)
                if item is None:
                    sp.wait_ge(*at(*release[N_PRE - SLOTS + p]))
                elif p < 8:
                    sp.wait_ge(*at("mm1", item * 7 - 7 + (p // 2 + 1 if p < 6 else 7)))
                else:
                    sp.wait_ge(*at("mm2", item * 4 - 4 + (p - 7)))
                if p < 8:
                    src = w1[bass.ds(e, 1), p, :, :].rearrange("e p n -> p (e n)")
                    dst = ring[:, s, :]
                else:
                    src = w2[bass.ds(e, 1), p - 8, :, :, :].rearrange("e p k n -> p (e k) n")
                    dst = grid(ring[:, s, :], D)
                sp.dma_start(dst, src).then_inc(landed[s], 16)

        load_expert(0, None)
        with sp.Fori(1, N_EXP) as e:
            load_expert(e, e)
        sp.wait_ge(*at("items_ready", 1))
        n_items = sp.value_load(item_count[0:1, 0:1], min_val=N_EXP, max_val=N_EXP + EXTRA)
        with sp.If(n_items > N_EXP):
            with sp.Fori(N_EXP, n_items) as item:
                e = sp.value_load(item_expert[0:1, bass.ds(item - N_EXP, 1)], min_val=0, max_val=N_EXP - 1)
                load_expert(e, item)
        sp.wait_ge(*at("y_ready", 3))
        sp.dma_start(O["y_p"][0].rearrange("(c p) d -> p c d", p=P), y_out[:, 0:2, :]).then_inc(sem("y_stored"), 16)
        sp.dma_start(O["y_s"].rearrange("b l d -> (b l) d"), y_out[0:NB, 2, :]).then_inc(sem("y_stored"), 16)
        sp.wait_ge(*at("y_stored", 32))

    @block.gpsimd
    def _(pool):
        def step(ins):
            link(pool, "pool_step", ins)

        step(pool.memset(arena[:, 0:6 * P], 1.0))
        step(pool.affine_select(out=ident, in_=ident, compare_op=ALU.is_equal, fill=0.0, base=0,
                                pattern=[[-1, P]], channel_multiplier=1))
        pool.nop().then_inc(sem("const_ready"), 1)
        step(pool.affine_select(out=tri_incl, in_=tri_incl, compare_op=ALU.is_ge, fill=0.0, base=0,
                                pattern=[[1, P]], channel_multiplier=-1))
        step(pool.affine_select(out=tri_strict, in_=tri_strict, compare_op=ALU.is_gt, fill=0.0, base=0,
                                pattern=[[1, P]], channel_multiplier=-1))
        d16 = diag16.rearrange("p (a b) -> p a b", b=16)
        step(pool.affine_select(out=d16, in_=d16, compare_op=ALU.is_ge, fill=0.0, base=0,
                                pattern=[[-16, 8], [0, 16]], channel_multiplier=1))
        step(pool.affine_select(out=d16, in_=d16, compare_op=ALU.is_ge, fill=0.0, base=15,
                                pattern=[[16, 8], [0, 16]], channel_multiplier=-1))
        b64 = blk64.rearrange("p (a b) -> p a b", b=64)
        step(pool.affine_select(out=b64, in_=b64, compare_op=ALU.is_ge, fill=0.0, base=0,
                                pattern=[[-64, 2], [0, 64]], channel_multiplier=1))
        pool.affine_select(out=b64, in_=b64, compare_op=ALU.is_ge, fill=0.0, base=63,
                           pattern=[[64, 2], [0, 64]], channel_multiplier=-1).then_inc(sem("const_ready"), 1)

        step(pool.iota(int_tmp[:, 0:P], pattern=[[1, P]], base=0, channel_multiplier=-1))
        step(pool.iota(int_tmp[:, P:3 * P], pattern=[[1, 2 * P]], base=-P, channel_multiplier=-1))
        step(pool.tensor_copy(neg_dist, int_tmp))
        step(pool.affine_select(out=neg_dist[:, 0:P], in_=neg_dist[:, 0:P], compare_op=ALU.is_ge, fill=NEG, base=0,
                                pattern=[[-1, P]], channel_multiplier=1))
        step(pool.affine_select(out=neg_dist[:, P:3 * P], in_=neg_dist[:, P:3 * P], compare_op=ALU.is_ge, fill=NEG,
                                base=P, pattern=[[-1, 2 * P]], channel_multiplier=1))
        step(pool.affine_select(out=neg_dist[:, P:3 * P], in_=neg_dist[:, P:3 * P], compare_op=ALU.is_ge, fill=NEG,
                                base=0, pattern=[[1, 2 * P]], channel_multiplier=-1))
        step(pool.iota(int_tmp[:, 0:P], pattern=[[1, P]], base=-P, channel_multiplier=0))
        step(pool.iota(int_tmp[:, P:2 * P], pattern=[[0, 2], [1, BLK]], base=0, channel_multiplier=0))
        step(pool.iota(int_tmp[:, 2 * P:2 * P + 32], pattern=[[1, 32]], base=0, channel_multiplier=0))
        step(pool.iota(int_tmp[:, 2 * P + 32:2 * P + 33], pattern=[[0, 1]], base=0, channel_multiplier=1))
        step(pool.tensor_copy(neg_dist_s, int_tmp[:, 0:P]))
        step(pool.tensor_copy(slot_iota, int_tmp[:, P:2 * P]))
        step(pool.tensor_copy(iota32, int_tmp[:, 2 * P:2 * P + 32]))
        pool.tensor_copy(e_col, int_tmp[:, 2 * P + 32:2 * P + 33]).then_inc(sem("const_ready"), 1)

        def spread(v, n):
            return v.broadcast_to([P, n])
        pool.dma_start(knorm_b, spread(A["k_norm_mem"], P)).then_inc(sem("rowp_landed"), 16)
        pool.dma_start(sink_b, spread(A["swa_sinks"], 8)).then_inc(sem("rowp_landed"), 16)
        pool.dma_start(alog_b, spread(A["a_log"], 4)).then_inc(sem("rowp_landed"), 16)
        pool.dma_start(dt_b, spread(A["dt_bias"], 4)).then_inc(sem("rowp_landed"), 16)
        pool.dma_start(brow_b, spread(A["b_router"], 32)).then_inc(sem("rowp_landed"), 16)
        pool.dma_start(w_ab, w_in[:, OFF_AB:OFF_AB + 8].rearrange("(k p) n -> p k n", p=P)).then_inc(sem("wab_landed"), 16)
        pool.dma_start(w_rt, A["w_router"][0].rearrange("(k p) n -> p k n", p=P)).then_inc(sem("wrt_landed"), 16)

        def store(dst, src):
            pool.dma_start(dst, src).then_inc(sem("stored"), 16)
            n_store[0] += 1

        store(O["swa_ks"][0, :, 0:WIN - 1].rearrange("b w k d -> b w (k d)"),
              A["cache_swa_k"][0, :, 1:WIN].rearrange("b w k d -> b w (k d)"))
        store(O["swa_vs"][0, :, 0:WIN - 1].rearrange("b w k d -> b w (k d)"),
              A["cache_swa_v"][0, :, 1:WIN].rearrange("b w k d -> b w (k d)"))
        pool.wait_ge(*at("memkv_ready", 1))
        store(O["mem_k"][0, 0].rearrange("(c m) h d -> m c (h d)", m=P), Kn)
        store(O["mem_v"][0, 0].rearrange("(c m) h d -> m c (h d)", m=P), Vm)
        pool.wait_ge(*at("stored", 16 * n_store[0]))
        pool.nop().then_inc(sem("memkv_stored"), 1)
        pool.wait_ge(*at("conv_rows_ready", 3))
        store(O["conv_p"][0, 0], cso[0:3, :])
        store(O["conv_s"][0].rearrange("b j n -> (b j) n"), cso[3:27, :])
        pool.wait_ge(*at("stored", 16 * n_store[0]))
        pool.nop().then_inc(sem("conv_stored"), 1)
        pool.wait_ge(*at("swa_rows_ready", 2))
        store(O["swa_kp"][0, 0].rearrange("w k d -> w (k d)"), kv_nat[:, 2 * P:3 * P])
        store(O["swa_vp"][0, 0].rearrange("w k d -> w (k d)"), kv_nat[:, P:2 * P])
        store(O["swa_ks"][0, :, WIN - 1].rearrange("b k d -> b (k d)"), kv_s[0:NB, 0:P])
        store(O["swa_vs"][0, :, WIN - 1].rearrange("b k d -> b (k d)"), kv_s[0:NB, P:2 * P])
        pool.wait_ge(*at("stored", 16 * n_store[0]))
        pool.nop().then_inc(sem("swa_stored"), 1)
        pool.wait_ge(*at("gdn_state_ready", 1))
        store(O["gdn_p"][0, 0].rearrange("h k v -> k h v"), s_one)
        pool.wait_ge(*at("gs_state_ready", 8))
        for j in range(2):
            store(O["gdn_s"][0].rearrange("b h k v -> k (b h) v")[:, 16 * j:16 * j + 16, :], s_out3[:, 16 * j:16 * j + 16, :])
        pool.wait_ge(*at("stored", 16 * n_store[0]))
        pool.nop().then_inc(sem("gdn_stored"), 1)
        pool.wait_ge(*at("merged", 24))
        pool.dma_start(b1_nat[0:N_EXP, :], A["b_mlp1"][0]).then_inc(sem("b_landed"), 16)
        pool.dma_start(b2_nat[0:N_EXP, :], A["b_mlp2"][0]).then_inc(sem("b_landed"), 16)

        pool.wait_ge(*at("items_ready", 1))
        pool.wait_ge(*at("acc_ready", 8))
        n_items = pool.value_load(item_count[0:1, 0:1], min_val=N_EXP, max_val=N_EXP + EXTRA)
        pool.nop().then_inc(sem("acc_done"), 1)
        with pool.Fori(0, n_items) as item:
            pool.wait_ge(*at("part_ready", (item + 1) * 8))
            pool.tensor_tensor(xT_flat, xT_flat, part_flat, ALU.add).then_inc(sem("acc_done"), 1)
            pool.wait_ge(*at("acc_done", item + 1))
        pool.wait_ge(*at("part_ready", (n_items + 1) * 8))
        pool.tensor_tensor(xT_flat, xT_flat, part_flat, ALU.add).then_inc(sem("acc_last"), 1)

    @block.tensor
    def _(pe):
        def mm(out, lhsT, rhs, start=True, stop=True):
            return nc.tensor.matmul(out, lhsT, rhs, start=start, stop=stop, skip_group_check=True)

        def tr(out, in_):
            n = in_.shape[0]
            return nc.tensor.transpose(out, in_, ident[0:n, 0:n])

        pe.wait_ge(*at("const_ready", 1))
        pe.wait_ge(*at("x_landed", 16))
        pe.wait_ge(*at("xs_landed", 16))
        for g in range(16):
            k = g % 8
            if g == 8:
                pe.wait_ge(*at("mem_landed", 16))
            if g >= 4:
                pe.wait_ge(*at("tr_evac_dve" if g % 2 else "tr_evac_act", (g - 4) // 2 + 1))
            src = x_nat if g < 8 else mem_nat
            for c in range(2):
                ins = tr(B[g % 4][:, P * c:P * c + P], src[:, c, P * k:P * k + P])
            if g < 8:
                ins = tr(B[g % 4][:, 2 * P:T], xs_nat[0:NB, P * k:P * k + P])
            ins.then_inc(sem("x_T"), 1)
        pe.wait_ge(*at("prm_landed", 160))
        tr(B[7][:, 0:76], prm[0:76, :]).then_inc(sem("prm_T"), 1)
        pe.wait_ge(*at("cst_landed", 16))
        for c in range(12):
            ins = tr(B[6][:, 24 * c:24 * c + 24], cst_nat[0:24, P * c:P * c + P])
        ins.then_inc(sem("cst_T"), 1)
        for i, n in ((0, T), (1, NP_TOK)):
            pe.wait_ge(*at("ln_sq", i + 1))
            for k in range(KD):
                ins = mm(B[4 + i][:, 0:n], ones, G_flat[:, n * k:n * k + n], start=(k == 0), stop=(k == KD - 1))
            ins.then_inc(sem("ln_ss"), 1)

        pe.wait_ge(*at("memTn_ready", 8))
        for n in range(8):
            i, c = n // 2, n % 2
            if n % 2 == 0:
                has_landed(pe, i)
            if n >= 4:
                pe.wait_ge(*at("proj_evac", n - 3))
            w = grid(slot(i), 256)
            for k in range(KD):
                ins = mm(B[n % 4][:, 0:256], memTn[:, k, P * c:P * c + P], w[:, k, :], start=(k == 0), stop=(k == KD - 1))
            ins.then_inc(sem("proj"), 1)

        def project(i, half, n, rhs):
            if half == 0:
                has_landed(pe, i)
            pe.wait_ge(*at("proj_evac", n - 3))
            w = grid(slot(i), 256)
            for k in range(KD):
                ins = mm(B[n % 4][:, 0:T], w[:, k, P * half:P * half + P], rhs[:, k, :], start=(k == 0), stop=(k == KD - 1))
            ins.then_inc(sem("proj"), 1)

        def norm_sums(s, lhsT):
            pe.wait_ge(*at("hn_sq", s + 1))
            for i in range(HN[s]):
                if i >= 4 or s:
                    pe.wait_ge(*at("hn_rt", max(HN_BASE[s], HN_BASE[s] + i - 3) if i >= 4 else HN_BASE[s]))
                mm(B[4 + i % 4][:, 0:T], lhsT, G_flat[:, T * i:T * i + T]).then_inc(sem("hn_ss"), 1)

        pe.wait_ge(*at("const_ready", 3))
        pe.wait_ge(*at("hT_ready", 8))
        for n in range(8, 12):
            project(PC_QM + (n - 8) // 2, n % 2, n, hT)
        pe.wait_ge(*at("cst_done", 1))
        pe.wait_ge(*at("colp_ready", 1))
        norm_sums(0, ones)
        for n in range(12, 34):
            project(PC_IN + (n - 12) // 2, n % 2, n, hT)
        pe.wait_ge(*at("wab_landed", 16))
        pe.wait_ge(*at("hn_rt", 4))
        for k in range(KD):
            ins = mm(B[4][0:8, 0:T], w_ab[:, k, :], hT[:, k, :], start=(k == 0), stop=(k == KD - 1))
        ins.then_inc(sem("ab_ps"), 1)
        pe.wait_ge(*at("ab_T", 1))
        for c, (a, n) in enumerate(TOK):
            ins = tr(B[5][0:n, 8 * c:8 * c + 8], ab_T[0:8, a:a + n])
        ins.then_inc(sem("ab_nT"), 1)
        pe.wait_ge(*at("ab_done", 1))
        norm_sums(1, blk64)
        norm_sums(2, ones)
        pe.wait_ge(*at("memkv_ready", 1))
        pe.wait_ge(*at("hn_rt", HN_BASE[3]))
        for c in range(2):
            for h in range(H_M):
                ins = tr(B[6 + c][:, P * h:P * h + P], Kn[:, c, P * h:P * h + P])
            ins.then_inc(sem("kmT_ps"), 1)
        pe.wait_ge(*at("conv_saved", 1))
        pe.wait_ge(*at("proj_evac", 34))
        cs = grid(conv_save, 27)
        for c in range(12):
            ins = tr(B[c // 4][0:27, P * (c % 4):P * (c % 4) + P], cs[:, c, :])
            if c % 4 == 3:
                ins.then_inc(sem("conv_rows_ps"), 1)

        def attend(tag, n, n_keys, scores, values, part_n):
            for i in range(n):
                if i >= 2:
                    pe.wait_ge(*at(tag + "_s_evac", i - 1))
                scores(i, B[i % 2]).then_inc(sem(tag + "_s"), 1)
            for i in range(n):
                pe.wait_ge(*at(tag + "_p", 1))
                if i >= 2:
                    pe.wait_ge(*at(tag + "_pT", i - 1))
                part_n(i, B[2 + i % 2]).then_inc(sem(tag + "_pT_ps"), 1)
                if i:
                    values(i - 1)
            values(n - 1)

        pe.wait_ge(*at("hn_done", HN_BASE[3]))
        pe.wait_ge(*at("KmT_ready", 2))
        pe.wait_ge(*at("conv_rows_ready", 3))

        def mm_scores(i, bank):
            h, q = i // 2, i % 2
            return mm(bank[:, 0:256], qm[:, h, P * q:P * q + P], KmT[:, h, :])

        def mm_turn(i, bank):
            tr(bank[:, 0:P], mm_s[:, i, 0:P])
            return tr(bank[:, P:2 * P], mm_s[:, i, P:2 * P])

        def mm_values(i):
            h, q = i // 2, i % 2
            pe.wait_ge(*at("mm_pT", i + 1))
            if q == 0 and h >= 2:
                pe.wait_ge(*at("mm_o", h - 1))
            for c in range(2):
                ins = mm(B[4 + h % 2][:, P * q:P * q + P], Vm[:, c, P * h:P * h + P], mm_pT[:, i % 2, P * c:P * c + P],
                         start=(c == 0), stop=(c == 1))
            ins.then_inc(sem("mm_o_ps"), 1)

        attend("mm", 8, 256, mm_scores, mm_values, mm_turn)

        pe.wait_ge(*at("mm_o", 4))
        for j in range(2):
            tr(B[6][:, P * j:P * j + P], vsT[:, P * j:P * j + P])
        tr(B[6][:, 2 * P:3 * P], qsk[:, 4, P:2 * P]).then_inc(sem("swa_nat"), 1)
        tr(B[7][0:NB, 0:P], qsk[:, 4, 2 * P:T])
        tr(B[7][0:NB, P:2 * P], vsT[:, 2 * P:T]).then_inc(sem("swa_nat"), 1)
        pe.wait_ge(*at("k_dup", 1))
        pe.wait_ge(*at("swa_rows_ready", 2))

        def sw_scores(i, bank):
            r = HD_S * (i % 2)
            q, k = qsk[r:r + HD_S, i // 2, :], k_dup[r:r + HD_S, i // 4, :]
            mm(bank[:, 0:P], q[:, 0:P], k[:, 0:P])
            return mm(bank[:, P:3 * P], q[:, P:2 * P], k[:, 0:2 * P])

        def sw_turn(i, bank):
            for c in range(3):
                ins = tr(bank[:, P * c:P * c + P], sw_s3[:, i, P * c:P * c + P])
            return ins

        def sw_values(i):
            r, v = HD_S * (i % 2), HD_S * (i // 4)
            pe.wait_ge(*at("sw_pT", i + 1))
            if i % 2 == 0 and i >= 4:
                pe.wait_ge(*at("sw_o", i // 2 - 1))
            out = B[4 + (i // 2) % 2][r:r + HD_S, :]
            mm(out[:, 0:P], kv_nat[:, v:v + HD_S], sw_pT[:, i % 2, 0:P])
            mm(out[:, P:2 * P], kv_nat[:, v:v + HD_S], sw_pT[:, i % 2, P:2 * P], stop=False)
            mm(out[:, P:2 * P], kv_nat[:, P + v:P + v + HD_S], sw_pT[:, i % 2, 2 * P:3 * P],
               start=False).then_inc(sem("sw_o_ps"), 1)

        attend("sw", 8, 384, sw_scores, sw_values, sw_turn)

        pe.wait_ge(*at("sw_o", 4))
        has_landed(pe, PC_SWA)
        kc, vc = grid(slot(PC_SWA)[:, 0:1024], P), grid(slot(PC_SWA)[:, 1024:2048], P)
        for b in range(NB):
            ins = tr(B[b // 4][:, P * (b % 4):P * (b % 4) + P], kc[:, b, :])
            if b % 4 == 3:
                ins.then_inc(sem("ss_kT_ps"), 1)
        pe.wait_ge(*at("ss_q", 1))
        mm(B[3][0:64, 0:1], ss_prod, ones[:, 0:1])
        mm(B[3][0:64, 1:2], rows64[0:1, 0:64], ones[0:1, 0:1])
        mm(B[3][0:64, 2:3], rows64[0:1, 64:128], ones[0:1, 0:1]).then_inc(sem("ss_new"), 1)
        for b in range(NB):
            pe.wait_ge(*at("ss_kT", b // 4 + 1))
            ins = mm(B[2][:, 8 * b:8 * b + 8], sw_kT[:, b, :], q_bd[:, 8 * b:8 * b + 8])
        ins.then_inc(sem("ss_s"), 1)
        pe.wait_ge(*at("ss_sT", 1))
        tr(B[4][0:64, 0:P], ss_T).then_inc(sem("ss_rows"), 1)
        pe.wait_ge(*at("ss_p", 1))
        mm(B[3][:, 0:64], ss_pb[0:64, :], ident[0:64, 0:64])
        tr(B[5][:, 0:64], ss[0:64, 0:P]).then_inc(sem("ss_pT_ps"), 1)
        pe.wait_ge(*at("ss_pT", 1))
        for b in range(NB):
            ins = mm(B[2][:, 8 * b:8 * b + 8], vc[:, b, :], ss_pT[:, 8 * b:8 * b + 8])
        ins.then_inc(sem("ss_o_ps"), 1)

        pe.wait_ge(*at("ss_done", 1))
        pe.wait_ge(*at("decay_ready", 1))
        for c in range(2):
            mm(B[0][:, 4 * c:4 * c + 4], tri_incl, g_n[:, c, :])
            ins = mm(B[0][:, 8 + 4 * c:12 + 4 * c], ones, g_n[:, c, :])
        ins.then_inc(sem("gd_cum"), 1)
        for c in range(2):
            for h in range(H_G):
                ins = mm(B[1 + c][:, P * h:P * h + P], g_n[:, c, h:h + 1].broadcast_to([P, P]), tri_incl)
            ins.then_inc(sem("gd_row"), 1)
        for c in range(2):
            for h in range(H_G):
                ins = mm(B[3 + c][:, P * h:P * h + P], beta_n[:, c, h:h + 1].broadcast_to([P, P]), ident)
            ins.then_inc(sem("gd_brow"), 1)
        for c in range(2):
            for h in range(H_G):
                k = cv[:, 4 + h, P * c:P * c + P]
                ins = mm(B[5 + c][:, P * h:P * h + P], k, k)
            ins.then_inc(sem("gd_kk"), 1)
        for c in range(2):
            if c:
                pe.wait_ge(*at("gd_cum_evac", 1))
            for h in range(H_G):
                ins = mm(B[7 if c == 0 else 0][:, P * h:P * h + P], cv[:, 4 + h, P * c:P * c + P], cv[:, h, P * c:P * c + P])
            ins.then_inc(sem("gd_qk"), 1)
        pe.wait_ge(*at("gd_dec", 2))
        for c in range(2):
            for h in range(H_G):
                ins = tr(B[1 + c][:, P * h:P * h + P], cv[:, 4 + h, P * c:P * c + P])
            ins.then_inc(sem("gd_kn"), 1)
        pe.wait_ge(*at("gd_at", 2))
        for c in range(2):
            for h in range(H_G):
                ins = tr(B[3 + c][:, P * h:P * h + P], cv[:, 8 + h, P * c:P * c + P])
            ins.then_inc(sem("gd_vn"), 1)

        pe.wait_ge(*at("gd_qk_done", 2))
        for s, (kind, a, b, _) in enumerate(INVERSE):
            for c in range(2):
                if s:
                    pe.wait_ge(*at("inv", 2 * s - 1 + c))
                bank = B[(5, 6, 7, 0)[2 * (s % 2) + c]]
                for h in range(H_G):
                    m = 4 * c + h
                    out = bank[:, P * h:P * h + P]
                    ins = tr(out, inv[a][:, m, :]) if kind == "turn" else mm(out, inv[a][:, m, :], inv[b][:, m, :])
                ins.then_inc(sem("inv_ps"), 1)
        pe.wait_ge(*at("inv", 2 * len(INVERSE)))
        pe.wait_ge(*at("gd_vbeta", 2))

        def per_head(bank, left, right, name, **kw):
            for h in range(H_G):
                ins = mm(bank[:, P * h:P * h + P], left(h), right(h), **kw)
            if name:
                ins.then_inc(sem(name), 1)

        T_inv = inv[3]
        per_head(B[1], lambda h: T_inv[:, h, :], lambda h: v_beta[:, h, :], "gd_v0")
        pe.wait_ge(*at("gd_v0_evac", 1))
        per_head(B[2], lambda h: k_dec[:, h, :], lambda h: v_new[:, h, :], "gd_s1")
        per_head(B[3], lambda h: v_new[:, h, :], lambda h: intra[:, h, :], "gd_o0")
        pe.wait_ge(*at("gd_s1_evac", 1))
        per_head(B[4], lambda h: cv[:, 4 + h, P:2 * P], lambda h: s_one[:, h, :], "gd_ks")
        pe.wait_ge(*at("gd_r", 1))
        per_head(B[1], lambda h: T_inv[:, 4 + h, :], lambda h: r_new[:, h, :], "gd_v1")
        pe.wait_ge(*at("gd_v1_evac", 1))
        for h in range(H_G):
            mm(B[5][:, P * h:P * h + P], s_one[:, h, :], q_dec[:, h, :], stop=False)
            ins = mm(B[5][:, P * h:P * h + P], v_new[:, h, :], intra[:, 4 + h, :], start=False)
        ins.then_inc(sem("gd_o1"), 1)
        per_head(B[2], lambda h: k_dec[:, 4 + h, :], lambda h: v_new[:, h, :], "gd_s2")

        pe.wait_ge(*at("gdn_state_ready", 1))
        pe.wait_ge(*at("gs_kq", 1))
        for i in range(32):
            if i % 16 == 0:
                has_landed(pe, PC_STATE + i // 16)
            ins = mm(B[0][:, 2 * i:2 * i + 2], slot(PC_STATE + i // 16)[:, P * (i % 16):P * (i % 16) + P], gs_kq[:, i, :])
        mm(B[1][:, 0:32], ones, gs_qk)
        mm(B[1][:, 32:96], ones[0:8, :], gs_dg[0:8, :]).then_inc(sem("gs_ps"), 1)
        pe.wait_ge(*at("gs_v", 1))
        tr(B[2][0:32, 0:P], gs_vn)
        tr(B[2][0:32, P:2 * P], gs_t).then_inc(sem("gs_rows"), 1)
        for j in range(8):
            pe.wait_ge(*at("gs_mask", j // 2 + 1))
            if j >= 4:
                pe.wait_ge(*at("gs_state_ready", j - 3))
            mm(B[4 + j % 4][:, :], gs_nat[0:32, P:2 * P],
               vn_mask[(j // 2) % 2][0:32, 4 * (j % 2):4 * (j % 2) + 4, :].rearrange("p a b -> p (a b)")).then_inc(sem("gs_outer"), 1)

        pe.wait_ge(*at("gdn_stored", 1))
        for h in range(H_M):
            ins = tr(B[0][0:NB, P * h:P * h + P], qm[:, h, 2 * P:T])
        ins.then_inc(sem("ms_q_ps"), 1)
        pe.wait_ge(*at("ms_q", 1))
        for b in range(NB):
            if b >= 2:
                pe.wait_ge(*at("ms_mul", b - 1))
            mm(B[1 + b % 2][:, :], pick8[0:8, b, :], q_nat8[0:8, :]).then_inc(sem("ms_qb"), 1)
        pe.wait_ge(*at("ms_s", 8))
        for c in range(2):
            ins = tr(B[3][0:32, P * c:P * c + P], ms_T[:, 32 * c:32 * c + 32])
        ins.then_inc(sem("ms_rows"), 1)
        pe.wait_ge(*at("ms_p", 1))
        for c in range(2):
            ins = tr(B[4][:, 32 * c:32 * c + 32], ms[0:32, P * c:P * c + P])
        ins.then_inc(sem("ms_pT_ps"), 1)
        pe.wait_ge(*at("ms_pT", 1))
        pe.wait_ge(*at("gs_state_ready", 8))
        for b in range(NB):
            i = PC_MV + b // 2
            has_landed(pe, i)
            v = grid(slot(i), 512)
            for c in range(2):
                ins = mm(B[5 + b // 4][32 * (b % 4):32 * (b % 4) + 32, :], ms_pT[:, 32 * c:32 * c + 32],
                         v[:, 2 * (b % 2) + c, :], start=(c == 0), stop=(c == 1))
            ins.then_inc(sem("ms_o_ps"), 1)
        for j in range(2):
            pe.wait_ge(*at("ms_o_evac", j + 1))
            for h in range(H_M):
                ins = tr(B[(0, 7)[j]][:, P * h:P * h + P], ms_pv[:, j, P * h:P * h + P])
            ins.then_inc(sem("ms_oT"), 1)
        pe.wait_ge(*at("ms_done", 1))
        norm_sums(3, ones)

        pe.wait_ge(*at("hn_rt", 21))
        pe.wait_ge(*at("o_ready", 1))
        for n in range(3):
            for d in range(8):
                project(PC_GATE[n] + d // 2, d % 2, 34 + 8 * n + d, hT)
            for d in range(8):
                i = PC_GATE[n] + 4 + d // 4
                has_landed(pe, i)
                w = grid(slot(i), 512)
                j = 8 * n + d
                if j >= 4:
                    pe.wait_ge(*at("merged", j - 3))
                for c in range(4):
                    ins = mm(B[4 + j % 4][:, 0:T], w[:, c, P * (d % 4):P * (d % 4) + P], oT[:, 4 * n + c, :],
                             start=(c == 0), stop=(c == 3))
                ins.then_inc(sem("branch"), 1)
        pe.wait_ge(*at("merged", 24))
        for d in range(8):
            i = PC_OUT + d // 2
            has_landed(pe, i)
            w = grid(slot(i), 256)
            if d < 4:
                pe.wait_ge(*at("proj_evac", 58))
            else:
                pe.wait_ge(*at("x1", d - 3))
            for k in range(KD):
                ins = mm(B[d % 4][:, 0:T], w[:, k, P * (d % 2):P * (d % 2) + P], mT[:, k, :], start=(k == 0), stop=(k == KD - 1))
            ins.then_inc(sem("out_ps"), 1)
        for k in range(KD):
            pe.wait_ge(*at("ln_sq", 3 + k))
            ins = mm(B[4][:, 0:T], ones, G[:, k, :], start=(k == 0), stop=(k == KD - 1))
        ins.then_inc(sem("ln_ss"), 1)
        pe.wait_ge(*at("h2_ready", 8))
        pe.wait_ge(*at("wrt_landed", 16))
        for k in range(KD):
            ins = mm(B[5][0:32, 0:T], w_rt[:, k, :], hT[:, k, :], start=(k == 0), stop=(k == KD - 1))
        ins.then_inc(sem("lg_ps"), 1)
        for c, (a, n) in enumerate(TOK):
            for k in range(KD):
                bank = B[(0, 2, 6)[c] + k // 4]
                ins = tr(bank[0:n, P * (k % 4):P * (k % 4) + P], hT[:, k, a:a + n])
                if k % 4 == 3:
                    ins.then_inc(sem("h2_nat_ps"), 1)
        pe.wait_ge(*at("lgT", 1))
        for c, (a, n) in enumerate(TOK):
            ins = tr(B[4][0:n, 32 * c:32 * c + 32], lgT[0:32, a:a + n])
        ins.then_inc(sem("lg_nat"), 1)
        pe.wait_ge(*at("sel", 1))
        pe.wait_ge(*at("h2_nat", 6))
        for c, (a, n) in enumerate(TOK):
            for i in range(c):
                mm(B[5][0:n, 32 * c:32 * c + 32], ones[:, 0:n], sel_n[:, i, :], start=(i == 0), stop=False)
            mm(B[5][0:n, 32 * c:32 * c + 32], tri_strict[0:n, 0:n], sel_n[0:n, c, :], start=(c == 0), stop=True)
        for c, (a, n) in enumerate(TOK):
            ins = mm(B[7][:, 0:1], sel4[0:n, c, :, :].rearrange("p r e -> p (r e)"), ones[0:n, 0:1], start=(c == 0), stop=(c == 2))
        ins.then_inc(sem("rank"), 1)
        for c, (a, n) in enumerate(TOK):
            ins = tr(B[4][0:32, a:a + n], gate_n[0:n, c, :])
        ins.then_inc(sem("gateT_ps"), 1)
        pe.wait_ge(*at("pos_ready", 1))
        for c, (a, n) in enumerate(TOK):
            ins = tr(B[5][0:32, a:a + n], pos_n[0:n, c, :])
        ins.then_inc(sem("posT_ps"), 1)
        pe.wait_ge(*at("more", 1))
        mm(B[7][:, 8:9], tri_strict, more_f)
        mm(B[7][0:1, 12:13], more_f, ones[:, 0:1]).then_inc(sem("more_ps"), 1)
        pe.wait_ge(*at("hot", 1))
        mm(B[7][0:32, 16:32], e_mod, item_hot)
        mm(B[7][:, 32:48], thr_b, item_hot)
        mm(B[7][0:1, 48:64], e_col, item_hot).then_inc(sem("hot_ps"), 1)
        pe.wait_ge(*at("gateT", 1))
        for c, (a, n) in enumerate(TOK):
            mm(B[6][0:n, N_ITEM * c:N_ITEM * c + N_ITEM], posT[0:32, a:a + n], item_oh[0:32, :])
            ins = mm(B[6][0:n, 256 + N_ITEM * c:256 + N_ITEM * c + N_ITEM], gateT[0:32, a:a + n], item_oh[0:32, :])
        ins.then_inc(sem("tables"), 1)
        pe.wait_ge(*at("b_landed", 32))
        for f in range(16):
            ins = mm(B[f // 8][:, N_ITEM * (f % 8):N_ITEM * (f % 8) + N_ITEM], b1_nat[0:32, P * f:P * f + P], item_oh[0:32, :])
            if f % 8 == 7:
                ins.then_inc(sem("b1_ps"), 1)
        for d in range(8):
            if d >= 2:
                pe.wait_ge(*at("acc_ready", d - 1))
            mm(B[2 + d % 2][:, 0:T], b2_nat[0:32, P * d:P * d + P], gateT[0:32, :]).then_inc(sem("b2_ps"), 1)

        def gather():
            for k in range(KD):
                for s in range(3):
                    for c, (a, n) in enumerate(TOK):
                        ins = mm(B[6][:, BLK * k:BLK * k + BLK], h2_parts[0:n, s, c, P * k:P * k + P], pick[0:n, c, :],
                                 start=(s == 0 and c == 0), stop=(s == 2 and c == 2))
            ins.then_inc(sem("xg_ps"), 1)

        pe.wait_ge(*at("picks", 1))
        pe.wait_ge(*at("tables_done", 1))
        pe.wait_ge(*at("h2_split", 3))
        gather()
        pe.wait_ge(*at("acc_ready", 8))
        pe.wait_ge(*at("b1_done", 2))
        pe.wait_ge(*at("items_ready", 1))
        n_items = pe.value_load(item_count[0:1, 0:1], min_val=N_EXP, max_val=N_EXP + EXTRA)
        pe.nop().then_inc(sem("put_ps"), 1)
        with pe.Fori(0, n_items) as item:
            pe.wait_ge(*at("xg", item + 1))
            for j in range(4):
                for r in range(2):
                    s = expert_slot(2 * j + r)
                    pe.wait_ge(landed[s], (item + 1) * 16 + landed_pre[s])
                for n in range(4):
                    for r in range(2):
                        k = 2 * j + r
                        ins = mm(B[n][64 * r:64 * r + 64, :], xg[:, k, :], ring[:, expert_slot(k), 512 * n:512 * n + 512],
                                 start=(j == 0), stop=(j == 3))
                    if j == 3 or n == 3:
                        ins.then_inc(sem("mm1"), 1)
            pe.wait_ge(*at("picks", item + 2))
            pe.wait_ge(*at("part_ready", item * 8))
            gather()
            for n in range(4):
                pe.wait_ge(*at("h_sum", item * 4 + (n + 1)))
                pe.nop().then_inc(sem("turning"), 1)
                for i in range(4):
                    f = 4 * n + i
                    ins = tr(B[f // 8][:, BLK * (f % 8):BLK * (f % 8) + BLK], h_sum[0:BLK, P * f:P * f + P])
                if n % 2:
                    ins.then_inc(sem("hT_ps"), 1)
            pe.wait_ge(*at("y_evac", item * 2))
            pe.wait_ge(*at("put", item))
            pe.wait_ge(*at("xg", item + 2))
            for d in range(KD):
                if d >= 2:
                    pe.wait_ge(*at("part_ready", item * 8 + (d - 1)))
                mm(B[6 + d % 2][:, 0:T], y_e[:, P * d:P * d + P], put).then_inc(sem("scat_ps"), 1)
            pe.wait_ge(*at("part_ready", item * 8 + 8))
            pe.wait_ge(*at("gpicks", item + 1))
            for c, (a, n) in enumerate(TOK):
                ins = tr(B[7][:, a:a + n], gpick[0:n, c, :])
            ins.then_inc(sem("put_ps"), 1)
            pe.wait_ge(*at("act", item + 1))
            for j in range(4):
                s = expert_slot(8 + j)
                pe.wait_ge(landed[s], (item + 1) * 16 + landed_pre[s])
                for n in range(2):
                    for r in range(2):
                        k = 2 * j + r
                        ins = mm(B[4 + n][64 * r:64 * r + 64, :], act_e[:, BLK * k:BLK * k + BLK],
                                 ring[:, s, D * r + 512 * n:D * r + 512 * n + 512], start=(j == 0), stop=(j == 3))
                ins.then_inc(sem("mm2"), 1)
        pe.wait_ge(*at("y_evac", n_items * 2))
        pe.wait_ge(*at("put", n_items))
        for d in range(KD):
            if d >= 2:
                pe.wait_ge(*at("part_ready", n_items * 8 + (d - 1)))
            mm(B[6 + d % 2][:, 0:T], y_e[:, P * d:P * d + P], put).then_inc(sem("scat_ps"), 1)
        pe.wait_ge(*at("acc_last", 1))
        for c, (a, n) in enumerate(TOK):
            for k in range(KD):
                bank = B[2 * c + k // 4]
                ins = tr(bank[0:n, P * (k % 4):P * (k % 4) + P], xT[:, k, a:a + n])
                if k % 4 == 3:
                    ins.then_inc(sem("y_ps"), 1)

    @block.scalar
    def _(act):
        fn = nc.scalar.activation

        def step(ins):
            link(act, "act_step", ins)

        def norm_root(s, scale):
            for i in range(HN[s]):
                act.wait_ge(*at("hn_ss", HN_BASE[s] + i + 1))
                if i == 0 and s:
                    act.wait_ge(*at("hn_done", HN_BASE[s]))
                fn(rt[:, i, :], B[4 + i % 4][:, 0:T], ACT.Ln, bias=eps_col, scale=scale).then_inc(sem("hn_rt"), 1)
            act.wait_ge(*at("hn_rt", HN_BASE[s] + HN[s]))
            fn(rt[:, 0:HN[s], :], rt[:, 0:HN[s], :], ACT.Exp, scale=-0.5).then_inc(sem("hn_inv"), 1)

        act.dma_start(xs_nat[0:NB, :], A["x_sample"].rearrange("b l d -> (b l) d")).then_inc(sem("xs_landed"), 16)
        rows = [(LN1, 8, A["ln1_gain"][0].rearrange("(k p) -> k p", p=P)),
                (LN2, 8, A["ln2_gain"][0].rearrange("(k p) -> k p", p=P)),
                (LNM, 8, A["mem_norm"][0].rearrange("(k p) -> k p", p=P)),
                (C_GDN, 1, A["gdn_norm"]), (C_QM, 1, A["q_norm_mem"]),
                (C_CONV, 48, A["conv_w"][0].rearrange("j (c p) -> (j c) p", p=P))]
        for r, n, src in rows:
            act.dma_start(prm[r:r + n, :], src).then_inc(sem("prm_landed"), 16)
        for half in range(2):
            act.dma_start(prm[C_QS:C_QS + 1, 64 * half:64 * half + 64], A["q_norm_swa"]).then_inc(sem("prm_landed"), 16)
            act.dma_start(prm[C_KS:C_KS + 1, 64 * half:64 * half + 64], A["k_norm_swa"]).then_inc(sem("prm_landed"), 16)
        act.dma_start(cst_nat[0:24, :], A["state_conv"][0].rearrange("b j n -> (b j) n")).then_inc(sem("cst_landed"), 16)
        for i in range(8):
            g = 2 * i
            act.wait_ge(*at("x_T", g + 1))
            dst = xT[:, g, :] if g < 8 else memT[:, g - 8, :]
            fn(dst, B[g % 4][:, 0:T if g < 8 else NP_TOK], ACT.Copy).then_inc(sem("tr_evac_act"), 1)
        act.wait_ge(*at("tr_evac_act", 4))
        act.wait_ge(*at("tr_evac_dve", 4))
        fn(G_flat, xT_flat, ACT.Square).then_inc(sem("ln_sq"), 1)
        act.wait_ge(*at("ln_ss", 1))
        act.wait_ge(*at("eps", 1))
        step(fn(rsx, B[4][:, 0:T], ACT.Ln, bias=eps_col, scale=1.0 / D))
        fn(rsx, rsx, ACT.Exp, scale=-0.5).then_inc(sem("ln_rt"), 1)
        act.wait_ge(*at("tr_evac_act", 8))
        act.wait_ge(*at("tr_evac_dve", 8))
        fn(G_flat[:, 0:2048], memT.rearrange("p k n -> p (k n)"), ACT.Square).then_inc(sem("ln_sq"), 1)
        act.wait_ge(*at("ln_ss", 2))
        step(fn(rsm, B[5][:, 0:NP_TOK], ACT.Ln, bias=eps_col, scale=1.0 / D))
        fn(rsm, rsm, ACT.Exp, scale=-0.5).then_inc(sem("ln_rt"), 1)
        act.wait_ge(*at("memTn_ready", 8))
        act.wait_ge(*at("hT_ready", 8))
        for n in range(8):
            i, c = n // 2, n % 2
            act.wait_ge(*at("proj", n + 1))
            dst = (Kn if i < 2 else Vm)[:, c, 256 * (i % 2):256 * (i % 2) + 256]
            fn(dst, B[n % 4][:, 0:256], ACT.Copy).then_inc(sem("proj_evac"), 1)
        act.wait_ge(*at("proj_evac", 8))
        fn(G_flat[:, 0:1024], Kn_flat, ACT.Square).then_inc(sem("kn_sq"), 1)
        act.wait_ge(*at("kn_ss", 1))
        fn(stat[:, 8:16], stat[:, 0:8], ACT.Sqrt, bias=eps_col, scale=1.0 / HD_M).then_inc(sem("kn_rt"), 1)
        for n in range(8, 12):
            act.wait_ge(*at("proj", n + 1))
            fn(qm[:, n - 8, :], B[n % 4][:, 0:T], ACT.Copy).then_inc(sem("proj_evac"), 1)
        act.wait_ge(*at("proj_evac", 12))
        fn(G_flat[:, 0:4 * T], qm_flat, ACT.Square).then_inc(sem("hn_sq"), 1)
        norm_root(0, 1.0 / HD_M)
        act.wait_ge(*at("cin_ready", 1))
        for n in range(12, 34):
            act.wait_ge(*at("proj", n + 1))
            j = n - 12
            if j < 5:
                dst = qsk[:, j, :]
            elif j == 5:
                dst = vsT
            elif j < 18:
                c = j - 6
                fn(cin[:, c, 3:3 + NP_TOK], B[n % 4][:, 0:NP_TOK], ACT.Copy)
                fn(cin[:, c, 3 + NP_TOK:CONV_FLAT].rearrange("p (b j) -> p b j", j=4)[:, :, 3],
                   B[n % 4][:, NP_TOK:T], ACT.Copy).then_inc(sem("proj_evac"), 1)
            else:
                dst = zT[:, j - 18, :]
            if not 6 <= j < 18:
                fn(dst, B[n % 4][:, 0:T], ACT.Copy).then_inc(sem("proj_evac"), 1)
            c = j - 8
            if 0 <= c < 12:
                act.wait_ge(*at("conv_y", c + 1))
                if c >= 2:
                    act.wait_ge(*at("conv_done", c - 1))
                fn(conv_sg[:, c % 2, :], conv_y[:, c % 2, :], ACT.Sigmoid).then_inc(sem("conv_sg"), 1)
        act.wait_ge(*at("ab_ps", 1))
        fn(ab_T[0:8, :], B[4][0:8, 0:T], ACT.Copy).then_inc(sem("ab_T"), 1)
        act.wait_ge(*at("hn_done", 4))
        act.wait_ge(*at("proj_evac", 34))
        fn(G_flat[:, 0:5 * T], qsk_flat, ACT.Square).then_inc(sem("hn_sq"), 1)
        norm_root(1, 1.0 / HD_S)
        act.wait_ge(*at("conv_done", 12))
        act.wait_ge(*at("hn_ss", HN_BASE[2]))
        fn(G_flat, cv_flat[:, 0:KD * T], ACT.Square).then_inc(sem("hn_sq"), 1)
        norm_root(2, 1.0)
        act.wait_ge(*at("hn_ss", HN_BASE[3]))
        fn(G_flat[:, 0:4 * T], zT_flat, ACT.Sigmoid).then_inc(sem("z_sg"), 1)
        act.wait_ge(*at("dc", 1))
        step(fn(gt1, gt1, ACT.Exp))
        step(fn(gt1, gt1, ACT.Ln, bias=1.0))
        step(fn(beta_n, ab_n[:, :, 4:8], ACT.Exp, scale=-1.0))
        fn(alog_b, alog_b, ACT.Exp).then_inc(sem("dc_act"), 1)
        for c in range(2):
            act.wait_ge(*at("kmT_ps", c + 1))
            fn(KmT[:, :, P * c:P * c + P], grid(B[6 + c][:, :], P), ACT.Copy).then_inc(sem("KmT_ready"), 1)
        for c in range(3):
            act.wait_ge(*at("conv_rows_ps", c + 1))
            act.wait_ge(*at("conv_done", 12))
            fn(cso[0:27, 512 * c:512 * c + 512], B[c][0:27, :], ACT.Copy).then_inc(sem("conv_rows_ready"), 1)

        act.wait_ge(*at("mm_m", 1))
        for i in range(8):
            ins = fn(mm_s[:, i, :], mm_s[:, i, :], ACT.Exp, bias=stat[:, 8 + i:9 + i], scale=HD_M ** -0.5,
                     accum_out=stat[:, 16 + i:17 + i])
        ins.then_inc(sem("mm_e"), 1)
        for i in range(8):
            act.wait_ge(*at("mm_pT_ps", i + 1))
            if i >= 2:
                act.wait_ge(*at("mm_o_ps", i - 1))
            fn(mm_pT[:, i % 2, :], B[2 + i % 2][:, 0:2 * P], ACT.Copy).then_inc(sem("mm_pT"), 1)
        act.wait_ge(*at("sw_m", 1))
        for i in range(8):
            fn(sw_s3[:, i, 0:P], sw_s3[:, i, 0:P], ACT.Exp, bias=stat[:, 16 + i:17 + i], accum_out=stat[:, 32 + i:33 + i])
            fn(sw_s3[:, i, P:3 * P], sw_s3[:, i, P:3 * P], ACT.Exp, bias=stat[:, 24 + i:25 + i],
               accum_out=stat[:, 40 + i:41 + i])
        fn(stat[:, 48:64], stat[:, 48:64], ACT.Exp).then_inc(sem("sw_e"), 1)
        for i in range(8):
            act.wait_ge(*at("sw_pT_ps", i + 1))
            if i >= 2:
                act.wait_ge(*at("sw_o_ps", i - 1))
            fn(sw_pT[:, i % 2, :], B[2 + i % 2][:, 0:3 * P], ACT.Copy).then_inc(sem("sw_pT"), 1)
        act.wait_ge(*at("sw_o", 4))
        for j in range(2):
            act.wait_ge(*at("ss_kT_ps", j + 1))
            fn(grid(cols(scr, 512 * j, 512), P), grid(B[j][:, :], P), ACT.Copy).then_inc(sem("ss_kT"), 1)
        act.wait_ge(*at("ss_m", 1))
        fn(ss[0:64, :], ss[0:64, :], ACT.Exp, bias=stat[0:64, 1:2], accum_out=stat[0:64, 2:3])
        fn(stat[0:64, 3:4], stat[0:64, 5:6], ACT.Exp, bias=stat[0:64, 1:2]).then_inc(sem("ss_e"), 1)
        act.wait_ge(*at("gd_small", 1))
        fn(g_sm[:, 16:40], g_sm[:, 16:40], ACT.Exp).then_inc(sem("gd_exp"), 1)
        fn(gt1[0:NB, 2, :], g_n[0:NB, 2, :], ACT.Exp).then_inc(sem("gs_eg"), 1)
        act.wait_ge(*at("gd_row", 2))
        act.wait_ge(*at("ss_done", 1))
        act.wait_ge(*at("gd_min", 1))
        fn(e_row.rearrange("p k n -> p (k n)"), B[2][:, :], ACT.Exp).then_inc(sem("gd_erow"), 1)
        fn(dec_flat, dec_flat, ACT.Exp).then_inc(sem("gd_dec_e"), 1)
        act.wait_ge(*at("memkv_stored", 1))
        act.wait_ge(*at("gd_exp", 1))
        for c in range(2):
            act.wait_ge(*at("gd_kn", c + 1))
            for h in range(H_G):
                ins = fn(k_dec[:, 4 * c + h, :], B[1 + c][:, P * h:P * h + P], ACT.Copy, scale=g_sm[:, 32 + 4 * c + h:33 + 4 * c + h])
            ins.then_inc(sem("gd_kdec"), 1)
        for c in range(2):
            act.wait_ge(*at("gd_vn", c + 1))
            for h in range(H_G):
                ins = fn(v_beta[:, 4 * c + h, :], B[3 + c][:, P * h:P * h + P], ACT.Copy, scale=beta_n[:, c, h:h + 1])
            ins.then_inc(sem("gd_vbeta"), 1)
        act.wait_ge(*at("gd_v0", 1))
        act.wait_ge(*at("gd_kdec", 2))
        fn(cols(KmT_flat, 0, 512), B[1][:, :], ACT.Copy).then_inc(sem("gd_v0_evac"), 1)
        act.wait_ge(*at("gd_v1", 1))
        act.wait_ge(*at("gd_s1", 1))
        act.wait_ge(*at("gd_o0", 1))
        fn(cols(KmT_flat, 0, 512), B[1][:, :], ACT.Copy).then_inc(sem("gd_v1_evac"), 1)
        act.wait_ge(*at("ms_m", 1))
        fn(ms[0:32, :], ms[0:32, :], ACT.Exp, bias=stat[0:32, 1:2], scale=HD_M ** -0.5,
           accum_out=stat[0:32, 2:3]).then_inc(sem("ms_e"), 1)
        for j in range(2):
            act.wait_ge(*at("ms_o_ps", 4 * j + 4))
            fn(ms_pv[:, j, :], B[5 + j][:, :], ACT.Copy).then_inc(sem("ms_o_evac"), 1)
        act.wait_ge(*at("ms_done", 1))
        fn(G_flat[:, 0:4 * T], oT_flat[:, 4 * T:8 * T], ACT.Square).then_inc(sem("hn_sq"), 1)
        norm_root(3, 1.0 / HD_G)
        act.wait_ge(*at("hn_ss", 21))
        for n in range(24):
            act.wait_ge(*at("proj", 34 + n + 1))
            if n >= 8:
                act.wait_ge(*at("merged", n - 7))
            fn(G[:, n % 8, :], B[(34 + n) % 4][:, 0:T], ACT.Sigmoid).then_inc(sem("proj_evac"), 1)
        for k in range(KD):
            act.wait_ge(*at("x1", k + 1))
            fn(G[:, k, :], xT[:, k, :], ACT.Square).then_inc(sem("ln_sq"), 1)
        act.wait_ge(*at("ln_ss", 3))
        step(fn(rr[:, 0:T], B[4][:, 0:T], ACT.Ln, bias=eps_col, scale=1.0 / D))
        fn(rr[:, 0:T], rr[:, 0:T], ACT.Exp, scale=-0.5).then_inc(sem("ln_rt"), 1)
        act.wait_ge(*at("lg_ps", 1))
        fn(lgT[0:32, :], B[5][0:32, 0:T], ACT.Copy).then_inc(sem("lgT"), 1)
        for c, (a, n) in enumerate(TOK):
            for j in range(2):
                act.wait_ge(*at("h2_nat_ps", 2 * c + j + 1))
                ins = fn(h2_nat[0:n, c, 512 * j:512 * j + 512], B[(0, 2, 6)[c] + j][0:n, :], ACT.Copy)
                ins.then_inc(sem("h2_nat"), 1)
            act.wait_ge(*at("h2_nat", 2 * c + 2))
            fn(h2_parts[0:n, 0, c, :], h2_nat[0:n, c, :], ACT.Copy).then_inc(sem("h2_hi"), 1)
        act.wait_ge(*at("top", 1))
        for c, (a, n) in enumerate(TOK):
            ins = fn(top_p[0:n, c, :], top_v[0:n, c, 0:4], ACT.Exp, bias=top_s[0:n, c:c + 1],
                     accum_out=top_s[0:n, 4 + c:5 + c])
        ins.then_inc(sem("top_e"), 1)

        act.wait_ge(*at("xg_ps", 1))
        fn(xg.rearrange("p k n -> p (k n)"), B[6][:, :], ACT.Copy).then_inc(sem("xg"), 1)
        act.wait_ge(*at("items_ready", 1))
        n_items = act.value_load(item_count[0:1, 0:1], min_val=N_EXP, max_val=N_EXP + EXTRA)
        for name in ("part_ready", "put", "y_evac"):
            act.nop().then_inc(sem(name), 1)
        with act.Fori(0, n_items) as item:
            fn(stat[:, 101:102], eps_col, ACT.Sigmoid)
            act.wait_ge(*at("h_sum", item * 4))
            for n in range(4):
                act.wait_ge(*at("mm1", item * 7 + (n + 4)))
                fn(h_odd[0:BLK, 512 * n:512 * n + 512], B[n][64:64 + BLK, :], ACT.Copy).then_inc(sem("h_odd"), 1)
            act.wait_ge(*at("xg_ps", item + 2))
            fn(xg.rearrange("p k n -> p (k n)"), B[6][:, :], ACT.Copy).then_inc(sem("xg"), 1)
            act.wait_ge(*at("acc_done", item))
            for d in range(KD):
                if d == 2:
                    act.wait_ge(*at("glu", item + 1))
                    fn(sg, glu, ACT.Sigmoid, scale=ALPHA).then_inc(sem("sg"), 1)
                act.wait_ge(*at("scat_ps", item * 8 + (d + 1)))
                fn(part[:, d, :], B[6 + d % 2][:, 0:T], ACT.Copy).then_inc(sem("part_ready"), 1)
            act.wait_ge(*at("put_ps", item + 1))
            fn(put, B[7][:, 0:T], ACT.Copy).then_inc(sem("put"), 1)
            act.wait_ge(*at("mm2", item * 4 + 4))
            for n in range(2):
                fn(y_e[:, 512 * n:512 * n + 512], B[4 + n][:, :], ACT.Copy).then_inc(sem("y_evac"), 1)
        act.wait_ge(*at("acc_done", n_items))
        for d in range(KD):
            act.wait_ge(*at("scat_ps", n_items * 8 + (d + 1)))
            fn(part[:, d, :], B[6 + d % 2][:, 0:T], ACT.Copy).then_inc(sem("part_ready"), 1)
        for c, (a, n) in enumerate(TOK):
            act.wait_ge(*at("y_ps", 2 * c + 1))
            fn(y_out[0:n, c, 0:512], B[2 * c][0:n, :], ACT.Copy).then_inc(sem("y_half"), 1)

    @block.vector
    def _(dve):
        v = nc.vector

        def step(ins):
            link(dve, "dve_step", ins)

        def norm_scale(s, dst, gains):
            dve.wait_ge(*at("hn_inv", s + 1))
            for i in range(HN[s]):
                v.scalar_tensor_tensor(dst(i), dst(i), gains(i), rt[:, i, :], ALU.mult, ALU.mult).then_inc(sem("hn_done"), 1)

        def column(i):
            return colp[:, i:i + 1]

        v.memset(eps_col, EPS).then_inc(sem("eps"), 1)
        v.memset(ab_n, 0.0)
        v.memset(stat, 0.0)
        for r in range(4):
            v.memset(thr_col[32 * r:32 * r + 32, :], float(BLK * (r + 1)))
        for i in range(8):
            g = 2 * i + 1
            dve.wait_ge(*at("x_T", g + 1))
            dst = xT[:, g, :] if g < 8 else memT[:, g - 8, :]
            v.tensor_copy(dst, B[g % 4][:, 0:T if g < 8 else NP_TOK]).then_inc(sem("tr_evac_dve"), 1)
        dve.wait_ge(*at("prm_T", 1))
        v.tensor_copy(colp[:, 0:76], B[7][:, 0:76]).then_inc(sem("colp_ready"), 1)
        dve.wait_ge(*at("colp_ready", 1))
        step(v.tensor_scalar(column(C_QS), column(C_QS), HD_S ** -0.5, None, ALU.mult))
        dve.wait_ge(*at("const_ready", 3))
        step(v.scalar_tensor_tensor(e_col, thr_col, -0.5, e_col, ALU.mult, ALU.add))
        step(v.tensor_scalar(e_col, e_col, 32.0, None, ALU.add))
        dve.wait_ge(*at("x_T", 16))
        v.memset(cin[:, :, 0:3], 0.0)
        dve.wait_ge(*at("cst_T", 1))
        for c in range(12):
            dst = cin[:, c, 3 + NP_TOK:CONV_FLAT].rearrange("p (b j) -> p b j", j=4)[:, :, 0:3]
            ins = v.tensor_copy(dst, B[6][:, 24 * c:24 * c + 24].rearrange("p (b j) -> p b j", j=3))
        ins.then_inc(sem("cst_done"), 1)
        dve.wait_ge(*at("cst_done", 1))
        v.tensor_scalar(stat[:, 100:101], eps_col, 0.0, None, ALU.mult).then_inc(sem("cin_ready"), 1)
        dve.wait_ge(*at("ln_rt", 1))
        for k in range(KD):
            v.scalar_tensor_tensor(hT[:, k, :], xT[:, k, :], column(LN1 + k), rsx, ALU.mult, ALU.mult).then_inc(sem("hT_ready"), 1)
        dve.wait_ge(*at("ln_rt", 2))
        for k in range(KD):
            v.scalar_tensor_tensor(memTn[:, k, :], memT[:, k, :], column(LNM + k), rsm, ALU.mult, ALU.mult).then_inc(sem("memTn_ready"), 1)
        dve.wait_ge(*at("rowp_landed", 80))
        dve.wait_ge(*at("kn_sq", 1))
        v.reduce_sum(stat[:, 0:8], grid(G_flat[:, 0:1024], P), AX).then_inc(sem("kn_ss"), 1)
        dve.wait_ge(*at("kn_rt", 1))
        step(v.reciprocal(stat[:, 8:16], stat[:, 8:16]))
        kn8 = grid(Kn_flat, P)
        step(v.tensor_tensor(kn8, kn8, bc(stat[:, 8:16], P), ALU.mult))
        dve.wait_ge(*at("proj_evac", 8))
        v.tensor_tensor(kn8, kn8, mid(knorm_b, 8), ALU.mult).then_inc(sem("memkv_ready"), 1)
        norm_scale(0, lambda i: qm[:, i, :], lambda i: column(C_QM))
        for c in range(13):
            if c < 12:
                dve.wait_ge(*at("proj_evac", 19 + c))
                if c >= 2:
                    dve.wait_ge(*at("conv_done", c - 1))
                y = conv_y[:, c % 2, :]
                step(v.tensor_scalar(y, cin[:, c, 0:288], column(C_CONV + c), None, ALU.mult))
                for j in range(1, 4):
                    ins = v.scalar_tensor_tensor(y, cin[:, c, j:j + 288], column(C_CONV + 12 * j + c), y, ALU.mult, ALU.add)
                    if j < 3:
                        step(ins)
                    else:
                        ins.then_inc(sem("conv_y"), 1)
            if c:
                i = c - 1
                dve.wait_ge(*at("conv_sg", i + 1))
                y, s = conv_y[:, i % 2, :], conv_sg[:, i % 2, :]
                v.tensor_tensor(cv[:, i, 0:NP_TOK], y[:, 0:NP_TOK], s[:, 0:NP_TOK], ALU.mult)
                ys, s_s = (u[:, 256:288].rearrange("p (b j) -> p b j", j=4)[:, :, 3] for u in (y, s))
                v.tensor_tensor(cv[:, i, NP_TOK:T], ys, s_s, ALU.mult).then_inc(sem("conv_done"), 1)
        cs = grid(conv_save, 27)
        v.tensor_copy(cs[:, :, 0:3], cin[:, :, NP_TOK:NP_TOK + 3])
        for c in range(12):
            src = cin[:, c, 3 + NP_TOK:CONV_FLAT].rearrange("p (b j) -> p b j", j=4)[:, :, 1:4]
            ins = v.tensor_copy(cs[:, c, 3:27].rearrange("p (b j) -> p b j", j=3), src)
        ins.then_inc(sem("conv_saved"), 1)
        dve.wait_ge(*at("ab_nT", 1))
        for c, (a, n) in enumerate(TOK):
            ins = v.tensor_copy(ab_n[0:n, c, :], B[5][0:n, 8 * c:8 * c + 8])
        ins.then_inc(sem("ab_done"), 1)
        dve.wait_ge(*at("ab_done", 1))
        step(v.tensor_tensor(gt0, ab_n[:, :, 0:4], mid(dt_b, 3), ALU.add))
        step(v.tensor_scalar(gt1, gt0, -1.0, None, ALU.mult))
        v.tensor_tensor(gt1, gt0, gt1, ALU.min).then_inc(sem("dc"), 1)
        norm_scale(1, lambda i: qsk[:, i, :], lambda i: column(C_QS if i < 4 else C_KS))
        norm_scale(2, lambda i: cv[:, i, :], lambda i: HD_G ** -0.5 if i < 4 else 1.0)
        dve.wait_ge(*at("z_sg", 1))
        step(v.tensor_tensor(zT_flat, zT_flat, G_flat[:, 0:4 * T], ALU.mult))
        dve.wait_ge(*at("dc_act", 1))
        step(v.scalar_tensor_tensor(gt0, gt0, 0.0, gt1, ALU.max, ALU.add))
        step(v.tensor_tensor(gt0, gt0, mid(alog_b, 3), ALU.mult))
        step(v.tensor_scalar(g_n, gt0, -1.0, None, ALU.mult))
        step(v.tensor_scalar(beta_n, beta_n, 1.0, None, ALU.add))
        v.reciprocal(beta_n, beta_n).then_inc(sem("decay_ready"), 1)

        dve.wait_ge(*at("hn_done", HN_BASE[3]))
        for i in range(8):
            dve.wait_ge(*at("mm_s", i + 1))
            v.tensor_copy(mm_s[:, i, :], B[i % 2][:, 0:256]).then_inc(sem("mm_s_evac"), 1)
        dve.wait_ge(*at("mm_s_evac", 8))
        step(v.tensor_reduce(stat[:, 0:8], mm_s, AX, ALU.max))
        v.tensor_scalar(stat[:, 8:16], stat[:, 0:8], -(HD_M ** -0.5), None, ALU.mult).then_inc(sem("mm_m"), 1)
        dve.wait_ge(*at("mm_e", 1))
        step(v.reciprocal(stat[:, 16:24], stat[:, 16:24]))
        v.tensor_tensor(mm_s, mm_s, bc(stat[:, 16:24], NP_TOK), ALU.mult).then_inc(sem("mm_p"), 1)
        dve.wait_ge(*at("conv_stored", 1))
        for h in range(H_M):
            dve.wait_ge(*at("mm_o_ps", 2 * h + 2))
            v.tensor_copy(oT[:, 8 + h, 0:NP_TOK], B[4 + h % 2][:, 0:256]).then_inc(sem("mm_o"), 1)
        dve.wait_ge(*at("mm_o_ps", 8))
        for kv in range(2):
            for half in range(2):
                ins = v.tensor_copy(k_dup[64 * half:64 * half + 64, kv, :], qsk[64 * kv:64 * kv + 64, 4, :])
        ins.then_inc(sem("k_dup"), 1)
        dve.wait_ge(*at("swa_nat", 1))
        v.tensor_copy(kv_nat, B[6][:, 0:3 * P]).then_inc(sem("swa_rows_ready"), 1)
        dve.wait_ge(*at("swa_nat", 2))
        v.tensor_copy(kv_s[0:NB, :], B[7][0:NB, 0:2 * P]).then_inc(sem("swa_rows_ready"), 1)
        for h in range(H_S):
            dve.wait_ge(*at("sw_s", h + 1))
            v.scalar_tensor_tensor(sw_s3[:, h, :], neg_dist, 2.0 ** -(h + 1), B[h % 2][:, 0:3 * P], ALU.mult,
                                   ALU.add).then_inc(sem("sw_s_evac"), 1)
        dve.wait_ge(*at("sw_s_evac", 8))
        v.tensor_reduce(stat[:, 0:8], sw_s3[:, :, 0:P], AX, ALU.max)
        step(v.tensor_reduce(stat[:, 8:16], sw_s3[:, :, P:3 * P], AX, ALU.max))
        two = stat[:, 0:16].rearrange("p (c h) -> p c h", h=8)
        step(v.tensor_tensor(two, two, mid(sink_b, 2), ALU.max))
        v.tensor_scalar(stat[:, 16:32], stat[:, 0:16], -1.0, None, ALU.mult)
        v.tensor_tensor(stat[:, 48:64].rearrange("p (c h) -> p c h", h=8), mid(sink_b, 2), two,
                        ALU.subtract).then_inc(sem("sw_m"), 1)
        dve.wait_ge(*at("sw_e", 1))
        step(v.tensor_tensor(stat[:, 32:48], stat[:, 32:48], stat[:, 48:64], ALU.add))
        step(v.reciprocal(stat[:, 32:48], stat[:, 32:48]))
        v.tensor_tensor(sw_s3[:, :, 0:P], sw_s3[:, :, 0:P], bc(stat[:, 32:40], P), ALU.mult)
        v.tensor_tensor(sw_s3[:, :, P:3 * P], sw_s3[:, :, P:3 * P], bc(stat[:, 40:48], 2 * P),
                        ALU.mult).then_inc(sem("sw_p"), 1)
        for i in range(4):
            dve.wait_ge(*at("sw_o_ps", 2 * i + 2))
            v.tensor_copy(oT[:, i, 0:NP_TOK], B[4 + i % 2][:, 0:256]).then_inc(sem("sw_o"), 1)

        dve.wait_ge(*at("sw_o", 4))
        step(v.memset(q_bd, 0.0))
        for h in range(H_S):
            a, b = 64 * (h // 4), 64 * (h % 2)
            ins = v.tensor_copy(q_bd3[a:a + 64, :, h], qsk[b:b + 64, h // 2, NP_TOK:T])
            v.memset(rows64[0:1, h:64:8], 2.0 ** -(h + 1))
        step(v.tensor_copy(rows64[0:1, 64:128].rearrange("p (b h) -> p b h", h=8), mid(sink_b[0:1, :], 8)))
        v.tensor_tensor(ss_prod3, q_bd3, bc(qsk[:, 4, NP_TOK:T], 8), ALU.mult).then_inc(sem("ss_q"), 1)
        dve.wait_ge(*at("ss_new", 1))
        step(v.tensor_copy(stat[0:64, 4:7], B[3][0:64, 0:3]))
        step(v.tensor_copy(stat[0:64, 7:8], stat[0:64, 5:6]))
        step(v.tensor_copy(stat[0:64, 5:6], stat[0:64, 6:7]))
        dve.wait_ge(*at("ss_s", 1))
        v.tensor_copy(ss_T, B[2][:, 0:64]).then_inc(sem("ss_sT"), 1)
        dve.wait_ge(*at("ss_rows", 1))
        v.tensor_copy(ss[0:64, P:P + 1], stat[0:64, 4:5])
        step(v.scalar_tensor_tensor(ss[0:64, 0:P], neg_dist_s[0:64, :], stat[0:64, 7:8], B[4][0:64, 0:P], ALU.mult, ALU.add))
        step(v.tensor_reduce(stat[0:64, 0:1], ss[0:64, :], AX, ALU.max))
        step(v.tensor_tensor(stat[0:64, 0:1], stat[0:64, 0:1], stat[0:64, 5:6], ALU.max))
        v.tensor_scalar(stat[0:64, 1:2], stat[0:64, 0:1], -1.0, None, ALU.mult).then_inc(sem("ss_m"), 1)
        dve.wait_ge(*at("ss_e", 1))
        step(v.tensor_tensor(stat[0:64, 2:3], stat[0:64, 2:3], stat[0:64, 3:4], ALU.add))
        step(v.reciprocal(stat[0:64, 2:3], stat[0:64, 2:3]))
        step(v.tensor_scalar(ss[0:64, :], ss[0:64, :], stat[0:64, 2:3], None, ALU.mult))
        v.tensor_copy(ss_pb[0:64, :], ss[0:64, P:P + 1].broadcast_to([64, P])).then_inc(sem("ss_p"), 1)
        dve.wait_ge(*at("ss_pT_ps", 1))
        v.tensor_copy(ss_pT, B[5][:, 0:64]).then_inc(sem("ss_pT"), 1)
        step(v.tensor_tensor(ss_o3, grid(B[3][:, 0:64], 8), bc(vsT[:, NP_TOK:T], 8), ALU.mult))
        dve.wait_ge(*at("ss_o_ps", 1))
        step(v.tensor_tensor(ss_o, ss_o, B[2][:, 0:64], ALU.add))
        for h in range(H_S):
            a, b = 64 * (h // 4), 64 * (h % 2)
            ins = v.tensor_copy(oT[b:b + 64, h // 2, NP_TOK:T], ss_o3[a:a + 64, :, h])
        ins.then_inc(sem("ss_done"), 1)

        dve.wait_ge(*at("ss_done", 1))
        dve.wait_ge(*at("gd_cum", 1))
        step(v.tensor_copy(g_sm[:, 0:16], B[0][:, 0:16]))
        v.tensor_copy(g_sm[:, 16:32], g_sm[:, 0:16]).then_inc(sem("gd_cum_evac"), 1)
        v.tensor_tensor(g_sm[:, 32:40], g_sm[:, 8:16], g_sm[:, 0:8], ALU.subtract).then_inc(sem("gd_small"), 1)
        dve.wait_ge(*at("gd_row", 2))
        for m in range(8):
            h = m % 4
            ins = v.tensor_scalar(dec[:, m, :], B[1 + m // 4][:, P * h:P * h + P], g_sm[:, m:m + 1], 0.0, ALU.subtract, ALU.min)
        ins.then_inc(sem("gd_min"), 1)
        dve.wait_ge(*at("gd_erow", 1))
        step(v.tensor_tensor(q_dec, cv[:, 0:4, P:2 * P], e_row, ALU.mult))
        dve.wait_ge(*at("gd_exp", 1))
        step(v.tensor_tensor(g_sm[:, 40:48].rearrange("p (c h) -> p c h", h=4), g_sm[:, 16:24].rearrange("p (c h) -> p c h", h=4),
                             beta_n[:, 0:2, :], ALU.mult))
        step(v.tensor_scalar(g_sm[:, 40:48], g_sm[:, 40:48], -1.0, None, ALU.mult))
        dve.wait_ge(*at("gd_dec_e", 1))
        dve.wait_ge(*at("swa_stored", 1))
        v.tensor_tensor(inv[5], dec, mid(tri_strict, 8), ALU.mult).then_inc(sem("gd_dec"), 1)
        v.tensor_tensor(dec, dec, mid(tri_incl, 8), ALU.mult).then_inc(sem("gd_dec"), 1)
        dve.wait_ge(*at("gd_dec", 2))
        for c in range(2):
            dve.wait_ge(*at("gd_kk", c + 1))
            part_a = inv_flat[0][:, 512 * c:512 * c + 512]
            step(v.tensor_tensor(part_a, B[5 + c][:, :], inv_flat[5][:, 512 * c:512 * c + 512], ALU.mult))
            dve.wait_ge(*at("gd_brow", c + 1))
            v.tensor_tensor(part_a, part_a, B[3 + c][:, :], ALU.mult).then_inc(sem("gd_at"), 1)
        for c in range(2):
            dve.wait_ge(*at("gd_qk", c + 1))
            v.tensor_tensor(intra_flat[:, 512 * c:512 * c + 512], B[7 if c == 0 else 0][:, :],
                            dec_flat[:, 512 * c:512 * c + 512], ALU.mult).then_inc(sem("gd_qk_done"), 1)
        for s, (kind, a, b, what) in enumerate(INVERSE):
            for c in range(2):
                dve.wait_ge(*at("inv_ps", 2 * s + c + 1))
                bank = B[(5, 6, 7, 0)[2 * (s % 2) + c]]
                own = slice(512 * c, 512 * c + 512)
                ps = bank[:, :]
                if what[0] == "parts":
                    g4 = slice(4 * c, 4 * c + 4)
                    step(v.tensor_tensor(inv[1][:, g4, :], grid(ps, P), mid(diag16, 4), ALU.mult))
                    step(v.tensor_tensor(inv_flat[2][:, own], ps, inv_flat[1][:, own], ALU.subtract))
                    step(v.tensor_tensor(inv[3][:, g4, :], mid(ident, 4), inv[1][:, g4, :], ALU.subtract))
                    ins = v.tensor_tensor(inv[0][:, g4, :], inv[0][:, g4, :], mid(diag16, 4), ALU.mult)
                elif what[0] == "copy":
                    ins = v.tensor_copy(inv_flat[what[1]][:, own], ps)
                elif what[0] == "add":
                    ins = v.tensor_tensor(inv_flat[what[1]][:, own], inv_flat[what[1]][:, own], ps, ALU.add)
                else:
                    ins = v.tensor_tensor(inv_flat[what[1]][:, own], inv_flat[what[1]][:, own], ps, ALU.subtract)
                ins.then_inc(sem("inv"), 1)
        dve.wait_ge(*at("gd_s1", 1))
        v.tensor_copy(s_one.rearrange("p k n -> p (k n)"), B[2][:, :]).then_inc(sem("gd_s1_evac"), 1)
        dve.wait_ge(*at("gd_o0", 1))
        v.tensor_copy(oT[:, 4:8, 0:P], grid(B[3][:, :], P))
        dve.wait_ge(*at("gd_ks", 1))
        dve.wait_ge(*at("gd_vbeta", 2))
        for h in range(H_G):
            ins = v.scalar_tensor_tensor(r_new[:, h, :], B[4][:, P * h:P * h + P], g_sm[:, 44 + h:45 + h], v_beta[:, 4 + h, :],
                                         ALU.mult, ALU.add)
        ins.then_inc(sem("gd_r"), 1)
        dve.wait_ge(*at("gd_o1", 1))
        step(v.tensor_copy(oT[:, 4:8, P:2 * P], grid(B[5][:, :], P)))
        dve.wait_ge(*at("gd_s2", 1))
        for h in range(H_G):
            ins = v.scalar_tensor_tensor(s_one[:, h, :], s_one[:, h, :], g_sm[:, 28 + h:29 + h], B[2][:, P * h:P * h + P],
                                         ALU.mult, ALU.add)
        ins.then_inc(sem("gdn_state_ready"), 1)

        def by_bh(u):
            return u.rearrange("p h b -> p b h")

        kq4 = gs_kq.rearrange("p (b h) c -> p b h c", h=4)
        ks_, qs_ = cv[:, 4:8, NP_TOK:T], cv[:, 0:4, NP_TOK:T]
        bh = lambda u: u.rearrange("p (b h) -> p b h", h=4)
        dve.wait_ge(*at("gdn_state_ready", 1))
        v.tensor_copy(kq4[:, :, :, 0], by_bh(ks_))
        v.tensor_copy(kq4[:, :, :, 1], by_bh(qs_))
        v.tensor_tensor(bh(gs_qk), by_bh(ks_), by_bh(qs_), ALU.mult)
        dve.wait_ge(*at("gd_v1", 1))
        dg = gs_dg[0:8, :].rearrange("p (s b h) -> p s b h", s=2, h=4)
        v.tensor_tensor(dg[:, 0], bc(ident[0:8, 0:8], 4), mid(beta_n[0:8, 2, :], 8), ALU.mult)
        dve.wait_ge(*at("gs_eg", 1))
        v.tensor_tensor(dg[:, 1], bc(ident[0:8, 0:8], 4), mid(gt1[0:8, 2, :], 8), ALU.mult).then_inc(sem("gs_kq"), 1)
        dve.wait_ge(*at("gs_ps", 1))
        step(v.tensor_copy(gs_bc, B[1][:, 0:96]))
        sq = B[0][:, 0:64].rearrange("p (n c) -> p n c", c=2)
        step(v.tensor_tensor(gs_t, sq[:, :, 0], gs_bc[:, 64:96], ALU.mult))
        step(v.tensor_tensor(bh(gs_t), by_bh(cv[:, 8:12, NP_TOK:T]), bh(gs_t), ALU.subtract))
        step(v.tensor_tensor(gs_vn, gs_t, gs_bc[:, 32:64], ALU.mult))
        step(v.tensor_tensor(gs_bc[:, 0:32], gs_bc[:, 0:32], gs_vn, ALU.mult))
        step(v.tensor_tensor(gs_qk, sq[:, :, 1], gs_bc[:, 64:96], ALU.mult))
        v.tensor_tensor(by_bh(oT[:, 4:8, NP_TOK:T]), bh(gs_qk), bh(gs_bc[:, 0:32]), ALU.add)
        v.tensor_copy(gs_t, gs_kq[:, :, 0]).then_inc(sem("gs_v"), 1)
        for j in range(2):
            i = PC_STATE + j
            has_landed(dve, i)
            v.tensor_tensor(s_out3[:, 16 * j:16 * j + 16, :], grid(slot(i), P), bc(gs_bc[:, 64 + 16 * j:80 + 16 * j], P),
                            ALU.mult).then_inc(sem("state_used"), 1)
        dve.wait_ge(*at("gs_rows", 1))
        step(v.tensor_copy(gs_nat[0:32, :], B[2][0:32, 0:2 * P]))
        for j in range(8):
            if j % 2 == 0:
                if j >= 4:
                    dve.wait_ge(*at("gs_outer", j - 2))
                q = j // 2
                v.tensor_tensor(vn_mask[q % 2][0:32, :, :], mid(gs_nat[0:32, 0:P], 8), bc(ident[0:32, 8 * q:8 * q + 8], P),
                                ALU.mult).then_inc(sem("gs_mask"), 1)
            dve.wait_ge(*at("gs_outer", j + 1))
            dst = s_out[:, 512 * j:512 * j + 512]
            v.tensor_tensor(dst, dst, B[4 + j % 4][:, :], ALU.add).then_inc(sem("gs_state_ready"), 1)

        dve.wait_ge(*at("gdn_stored", 1))
        v.tensor_copy(pick8[0:8, :, :], bc(ident[0:8, 0:8], P))
        dve.wait_ge(*at("ms_q_ps", 1))
        v.tensor_copy(q_nat8[0:8, :], B[0][0:8, :]).then_inc(sem("ms_q"), 1)
        ms_T4 = ms_T.rearrange("p (c b h) -> p c b h", c=2, h=4)
        for b in range(NB):
            i = PC_MK + b // 2
            has_landed(dve, i)
            dve.wait_ge(*at("ms_qb", b + 1))
            kb = grid(slot(i)[:, 1024 * (b % 2):1024 * (b % 2) + 1024], 512)
            v.tensor_tensor(mk_prod.rearrange("p (c h) d -> p c (h d)", c=2), kb, mid(B[1 + b % 2][:, :], 2),
                            ALU.mult).then_inc(sem("ms_mul"), 1)
            dve.wait_ge(*at("ms_mul", b + 1))
            v.reduce_sum(ms_T4[:, :, b, :], mk_prod.rearrange("p (c h) d -> p c h d", c=2), AX).then_inc(sem("ms_s"), 1)
            dve.wait_ge(*at("ms_s", b + 1))
        dve.wait_ge(*at("ms_rows", 1))
        step(v.tensor_copy(ms[0:32, :], B[3][0:32, 0:256]))
        step(v.tensor_reduce(stat[0:32, 0:1], ms[0:32, :], AX, ALU.max))
        v.tensor_scalar(stat[0:32, 1:2], stat[0:32, 0:1], -(HD_M ** -0.5), None, ALU.mult).then_inc(sem("ms_m"), 1)
        dve.wait_ge(*at("ms_e", 1))
        step(v.reciprocal(stat[0:32, 2:3], stat[0:32, 2:3]))
        v.tensor_scalar(ms[0:32, :], ms[0:32, :], stat[0:32, 2:3], None, ALU.mult).then_inc(sem("ms_p"), 1)
        dve.wait_ge(*at("ms_pT_ps", 1))
        v.tensor_copy(ms_pT, B[4][:, 0:64]).then_inc(sem("ms_pT"), 1)
        for j in range(2):
            dve.wait_ge(*at("ms_oT", j + 1))
            for h in range(H_M):
                a = P * h + 16 * j + h
                ins = v.tensor_copy(oT[:, 8 + h, NP_TOK + 4 * j:NP_TOK + 4 * j + 4], B[(0, 7)[j]][:, a:a + 109:36])
        ins.then_inc(sem("ms_done"), 1)
        norm_scale(3, lambda i: oT[:, 4 + i, :], lambda i: column(C_GDN))
        dve.wait_ge(*at("hn_done", 21))
        v.tensor_tensor(oT_flat[:, 4 * T:8 * T], oT_flat[:, 4 * T:8 * T], zT_flat, ALU.mult).then_inc(sem("o_ready"), 1)

        for n in range(3):
            for d in range(8):
                j = 8 * n + d
                dve.wait_ge(*at("branch", j + 1))
                dve.wait_ge(*at("proj_evac", 34 + j + 1))
                ps = B[4 + j % 4][:, 0:T]
                if n == 0:
                    v.tensor_tensor(mT[:, d, :], ps, G[:, d, :], ALU.mult).then_inc(sem("merged"), 1)
                else:
                    step(v.tensor_tensor(mtmp[:, d % 2, :], ps, G[:, d, :], ALU.mult))
                    v.tensor_tensor(mT[:, d, :], mT[:, d, :], mtmp[:, d % 2, :], ALU.add).then_inc(sem("merged"), 1)
        for d in range(8):
            dve.wait_ge(*at("out_ps", d + 1))
            v.tensor_tensor(xT[:, d, :], xT[:, d, :], B[d % 4][:, 0:T], ALU.add).then_inc(sem("x1"), 1)
        dve.wait_ge(*at("ln_rt", 3))
        for k in range(KD):
            v.scalar_tensor_tensor(hT[:, k, :], xT[:, k, :], column(LN2 + k), rr[:, 0:T], ALU.mult, ALU.mult).then_inc(sem("h2_ready"), 1)
        dve.wait_ge(*at("lg_nat", 1))
        for c, (a, n) in enumerate(TOK):
            step(v.tensor_tensor(lg_n[0:n, c, :], B[4][0:n, 32 * c:32 * c + 32], brow_b[0:n, :], ALU.add))
            step(v.max(top_v[0:n, c, :], lg_n[0:n, c, :]))
            step(v.max_index(top_i[0:n, c, :], top_v[0:n, c, :], lg_n[0:n, c, :]))
            step(v.tensor_copy(top_f[0:n, c, :], top_i[0:n, c, :]))
            ins = v.tensor_scalar(top_s[0:n, c:c + 1], top_v[0:n, c, 0:1], -1.0, None, ALU.mult)
        ins.then_inc(sem("top"), 1)
        dve.wait_ge(*at("top_e", 1))
        for c, (a, n) in enumerate(TOK):
            step(v.reciprocal(top_s[0:n, 4 + c:5 + c], top_s[0:n, 4 + c:5 + c]))
            step(v.tensor_scalar(top_p[0:n, c, :], top_p[0:n, c, :], top_s[0:n, 4 + c:5 + c], None, ALU.mult))
            for k in range(TOP_K):
                dst = gate_n[0:n, c, :] if k == 0 else rtmp[0:n, :]
                step(v.tensor_scalar(dst, iota32[0:n, :], top_f[0:n, c, k:k + 1], top_p[0:n, c, k:k + 1], ALU.is_equal, ALU.mult))
                if k:
                    step(v.tensor_tensor(gate_n[0:n, c, :], gate_n[0:n, c, :], rtmp[0:n, :], ALU.add))
            step(v.tensor_scalar(sel_n[0:n, c, :], gate_n[0:n, c, :], 0.0, None, ALU.is_gt))
            step(v.tensor_copy(sel4[0:n, c, :, :], mid(sel_n[0:n, c, :], 4)))
        dve.nop().then_inc(sem("sel"), 1)
        dve.wait_ge(*at("rank", 1))
        for c, (a, n) in enumerate(TOK):
            step(v.scalar_tensor_tensor(pos_n[0:n, c, :], B[5][0:n, 32 * c:32 * c + 32], 1.0, sel_n[0:n, c, :], ALU.add, ALU.mult))
            ins = v.tensor_scalar(pos_n[0:n, c, :], pos_n[0:n, c, :], -1.0, None, ALU.add)
        ins.then_inc(sem("pos_ready"), 1)
        v.tensor_tensor(more_f, B[7][:, 0:1], thr_col, ALU.is_gt).then_inc(sem("more"), 1)
        dve.wait_ge(*at("more_ps", 1))
        step(v.tensor_copy(more_pos, B[7][:, 8:9]))
        for r in range(4):
            v.tensor_copy(e_mod[32 * r:32 * r + 32, :], ident[32 * r:32 * r + 32, 32 * r:32 * r + 32])
        v.tensor_copy(thr_b, thr_col.broadcast_to([P, P]))
        step(v.tensor_scalar(item_f[0:1, 0:1], B[7][0:1, 12:13], float(N_EXP), None, ALU.add))
        v.tensor_scalar(item_hot, iota32[:, 0:16], more_pos, more_f, ALU.is_equal, ALU.mult).then_inc(sem("hot"), 1)
        v.tensor_copy(item_oh[0:32, 0:32], ident[0:32, 0:32])
        v.memset(item_oh[0:32, 32:N_ITEM], 0.0)
        dve.wait_ge(*at("hot_ps", 1))
        dve.wait_ge(*at("gdn_stored", 1))
        step(v.tensor_copy(item_int[0:1, 0:1], item_f[0:1, 0:1]))
        step(v.tensor_copy(item_int[0:1, 2:18], B[7][0:1, 48:64]))
        v.tensor_copy(item_off, B[7][:, 32:48])
        v.tensor_copy(item_oh[0:32, 32:48], B[7][0:32, 16:32]).then_inc(sem("items_ready"), 1)
        dve.wait_ge(*at("gateT_ps", 1))
        v.tensor_copy(gateT[0:32, :], B[4][0:32, 0:T])
        dve.wait_ge(*at("posT_ps", 1))
        step(v.tensor_copy(posT[0:32, :], B[5][0:32, 0:T]))
        dve.nop().then_inc(sem("gateT"), 1)
        for c, (a, n) in enumerate(TOK):
            dve.wait_ge(*at("h2_hi", c + 1))
            t0 = h2_nat[0:n, c, :]
            step(v.tensor_tensor(t0, t0, h2_parts[0:n, 0, c, :], ALU.subtract))
            step(v.tensor_copy(h2_parts[0:n, 1, c, :], t0))
            step(v.tensor_tensor(t0, t0, h2_parts[0:n, 1, c, :], ALU.subtract))
            v.tensor_copy(h2_parts[0:n, 2, c, :], t0).then_inc(sem("h2_split"), 1)
        dve.wait_ge(*at("tables", 1))
        for c, (a, n) in enumerate(TOK):
            v.tensor_copy(item_gate[0:n, c, :], B[6][0:n, 256 + N_ITEM * c:256 + N_ITEM * c + N_ITEM])
            step(v.tensor_copy(item_pos[0:n, c, :], B[6][0:n, N_ITEM * c:N_ITEM * c + N_ITEM]))
            step(v.tensor_tensor(item_pos[0:n, c, 32:48], item_pos[0:n, c, 32:48], item_off[0:n, :], ALU.subtract))
        v.memset(gpick, 0.0)
        v.memset(put, 0.0)
        step(v.memset(y_e, 0.0))
        dve.nop().then_inc(sem("tables_done"), 1)

        def build_pick(i):
            for c, (a, n) in enumerate(TOK):
                ins = v.tensor_scalar(pick[0:n, c, :], slot_iota[0:n, 0:BLK], item_pos[0:n, c, bass.ds(i, 1)], None, ALU.is_equal)
            ins.then_inc(sem("picks"), 1)

        build_pick(0)
        for j in range(2):
            dve.wait_ge(*at("b1_ps", j + 1))
            v.tensor_copy(item_b1[:, :, 8 * j:8 * j + 8].rearrange("p i f -> p f i"),
                          grid(B[j][:, 0:8 * N_ITEM], N_ITEM)).then_inc(sem("b1_done"), 1)
        for d in range(8):
            dve.wait_ge(*at("b2_ps", d + 1))
            v.tensor_tensor(xT[:, d, :], xT[:, d, :], B[2 + d % 2][:, 0:T], ALU.add).then_inc(sem("acc_ready"), 1)

        dve.wait_ge(*at("b1_done", 2))
        dve.wait_ge(*at("items_ready", 1))
        n_items = dve.value_load(item_count[0:1, 0:1], min_val=N_EXP, max_val=N_EXP + EXTRA)
        dve.nop().then_inc(sem("h_sum"), 1)
        with dve.Fori(0, n_items) as item:
            dve.wait_ge(*at("xg_ps", item + 1))
            build_pick(item + 1)
            dve.wait_ge(*at("put_ps", item))
            for c, (a, n) in enumerate(TOK):
                ins = v.tensor_scalar(gpick[0:n, c, :], slot_iota[0:n, :], item_pos[0:n, c, bass.ds(item, 1)],
                                      item_gate[0:n, c, bass.ds(item, 1)], ALU.is_equal, ALU.mult)
            ins.then_inc(sem("gpicks"), 1)
            for n in range(4):
                dve.wait_ge(*at("h_odd", item * 4 + (n + 1)))
                own = slice(512 * n, 512 * n + 512)
                v.tensor_tensor(h_sum[0:BLK, own], B[n][0:BLK, :], h_odd[0:BLK, own], ALU.add).then_inc(sem("h_sum"), 1)
            b1 = item_b1[:, bass.ds(item, 1), :].rearrange("p i f -> p (i f)")
            dve.wait_ge(*at("hT_ps", item * 2 + 1))
            v.tensor_tensor(grid(glu, BLK), grid(B[0][:, :], BLK), bc(b1[:, 0:8], BLK), ALU.add).then_inc(sem("e_step"), 1)
            dve.wait_ge(*at("e_step", item * 4 + 1))
            v.tensor_scalar(glu, glu, LIMIT, None, ALU.min).then_inc(sem("glu"), 1)
            dve.wait_ge(*at("hT_ps", item * 2 + 2))
            v.tensor_tensor(grid(lin, BLK), grid(B[1][:, :], BLK), bc(b1[:, 8:16], BLK), ALU.add).then_inc(sem("e_step"), 1)
            dve.wait_ge(*at("e_step", item * 4 + 2))
            v.tensor_scalar(lin, lin, LIMIT, -LIMIT, ALU.min, ALU.max).then_inc(sem("e_step"), 1)
            dve.wait_ge(*at("e_step", item * 4 + 3))
            dve.wait_ge(*at("glu", item + 1))
            v.scalar_tensor_tensor(lin, lin, 1.0, glu, ALU.add, ALU.mult).then_inc(sem("e_step"), 1)
            dve.wait_ge(*at("e_step", item * 4 + 4))
            dve.wait_ge(*at("sg", item + 1))
            v.tensor_tensor(act_e, lin, sg, ALU.mult).then_inc(sem("act"), 1)
        for c, (a, n) in enumerate(TOK):
            dve.wait_ge(*at("y_ps", 2 * c + 2))
            dve.wait_ge(*at("y_half", c + 1))
            v.tensor_copy(y_out[0:n, c, 512:1024], B[2 * c + 1][0:n, :]).then_inc(sem("y_ready"), 1)


_INS = ['x_prompt', 'x_sample', 'cache_swa_k', 'cache_swa_v', 'state_gdn', 'state_conv', 'cache_mem_k', 'cache_mem_v',
        'mem_prompt', 'ln1_gain', 'w_in', 'q_norm_swa', 'k_norm_swa', 'swa_sinks', 'conv_w', 'a_log', 'dt_bias',
        'gdn_norm', 'q_norm_mem', 'k_norm_mem', 'mem_norm', 'w_mem_kv', 'w_branch', 'w_out', 'ln2_gain', 'w_router',
        'b_router', 'w_mlp1', 'b_mlp1', 'w_mlp2', 'b_mlp2']
_OUTS = [('y_p', (1, 256, 1024)), ('y_s', (8, 1, 1024)), ('swa_kp', (1, 1, 128, 2, 64)), ('swa_vp', (1, 1, 128, 2, 64)),
         ('swa_ks', (1, 8, 128, 2, 64)), ('swa_vs', (1, 8, 128, 2, 64)), ('gdn_p', (1, 1, 4, 128, 128)),
         ('gdn_s', (1, 8, 4, 128, 128)), ('conv_p', (1, 1, 3, 1536)), ('conv_s', (1, 8, 3, 1536)),
         ('mem_k', (1, 1, 256, 4, 128)), ('mem_v', (1, 1, 256, 4, 128))]


def kernel(**inputs):
    import numpy as _np
    import concourse.bacc as _bacc
    from concourse import mybir as _mybir
    from concourse.bass_utils import run_bass_kernel_spmd as _run

    nc = _bacc.Bacc("TRN2", target_bir_lowering=False, num_devices=1)
    arrays, A, O = {}, {}, {}
    for name in _INS:
        a = _np.ascontiguousarray(inputs[name])
        arrays[f"in_{name}"] = a
        A[name] = nc.dram_tensor(f"in_{name}", a.shape, _mybir.dt.from_np(a.dtype), kind="ExternalInput").ap()
    for name, shape in _OUTS:
        O[name] = nc.dram_tensor(f"out_{name}", shape, _mybir.dt.float32, kind="ExternalOutput").ap()
    build_layer(nc, A, O)
    r = _run(nc, [arrays], core_ids=[0])
    return tuple(r.results[0][f"out_{name}"] for name, _ in _OUTS)
```

```python
from contextlib import ExitStack

import concourse.bass as bass
from concourse import mybir

F32 = mybir.dt.float32
BF16 = mybir.dt.bfloat16
I32 = mybir.dt.int32
U32 = mybir.dt.uint32
ALU = mybir.AluOpType
ACT = mybir.ActivationFunctionType
AX = mybir.AxisListType.X
PE_ENGINE = mybir.EngineType.PE

P = 128
D = 1024
KD = D // P
NP_TOK = 256
NB = 8
T = NP_TOK + NB
EPS = 1e-6
NEG = -1e30
HD_S, H_S, KV_S, WIN = 64, 8, 2, 128
HD_G, H_G = 128, 4
HD_M, H_M, MEM = 128, 4, 256
N_EXP, TOP_K = 32, 4
LIMIT, ALPHA = 7.0, 1.702
SLOTS, SLOT = 12, 2048
PRE_SLOTS = 8
BLK = 64
EXTRA = 16
N_ITEM = N_EXP + EXTRA + 1
N_BLK = -(-T // BLK)
CONV_FLAT = 3 + NP_TOK + 4 * NB
OFF_QS, OFF_QG, OFF_AB, OFF_QM, OFF_GATE = 0, 768, 2816, 2824, 3336
BRANCHES = (0, 2, 1)
TOK = [(0, P), (P, P), (2 * P, NB)]


INVERSE = [
    ("turn", 0, None, ("parts",)),
    ("mult", 0, 1, ("copy", 4)),
    ("turn", 4, None, ("copy", 5)),
    ("mult", 5, 4, ("copy", 0)),
    ("turn", 0, None, ("copy", 1)),
    ("mult", 1, 0, ("copy", 4)),
    ("turn", 4, None, ("copy", 4)),
    ("mult", 5, 3, ("add", 3)),
    ("mult", 1, 3, ("add", 3)),
    ("mult", 4, 3, ("add", 3)),
    ("turn", 3, None, ("copy", 4)),
    ("mult", 4, 2, ("copy", 0)),
    ("turn", 0, None, ("copy", 1)),
    ("mult", 1, 0, ("copy", 2)),
    ("turn", 2, None, ("copy", 4)),
    ("mult", 4, 2, ("copy", 5)),
    ("turn", 5, None, ("copy", 5)),
    ("mult", 5, 3, ("add", 3)),
    ("mult", 4, 3, ("add", 3)),
    ("mult", 1, 3, ("subtract", 3)),
    ("turn", 3, None, ("copy", 3)),
]


INV_COPIES = sum(step[3][0] == "copy" for step in INVERSE)


def inverse_out(s, c):
    copies = sum(step[3][0] == "copy" for step in INVERSE[:s])
    if INVERSE[s][3][0] == "copy":
        return ("inv_act", copies + 1) if c else ("inv", 2 * s - copies + 1)
    return "inv", 2 * s - copies + 1 + c


CHAINS = {
    "pe_load": [("x_T", 16), ("prm_T", 1), ("cst_T", 1)],
    "pe_small": [("ab_ps", 1), ("ab_nT", 1), ("kmT_ps", 2), ("conv_rows_ps", 3)],
    "pe_scores": [("mm_s", 8), ("swa_nat", 2), ("sw_s", 8)],
    "pe_turned": [("mm_pT_ps", 8), ("sw_pT_ps", 8)],
    "pe_outputs": [("mm_o_ps", 8), ("sw_o_ps", 8)],
    "pe_window": [("ss_kT_ps", 2), ("ss_new", 1), ("ss_s", 1), ("ss_rows", 1), ("ss_pT_ps", 1), ("ss_o_ps", 1)],
    "pe_delta": [("gd_cum", 1), ("gd_row", 2), ("gd_brow", 2), ("gd_kk", 2), ("gd_qk", 2), ("gd_kn", 2), ("gd_vn", 2),
                 ("inv_ps", 2 * len(INVERSE)), ("gd_v0", 1), ("gd_s1", 1), ("gd_o0", 1), ("gd_ks", 1), ("gd_v1", 1),
                 ("gd_o1", 1), ("gd_s2", 1), ("gs_ps", 1), ("gs_rows", 1), ("gs_outer", 8)],
    "pe_memory": [("ms_q_ps", 1), ("ms_qb", 8), ("ms_rows", 1), ("ms_pT_ps", 1), ("ms_o_ps", 8), ("ms_oT", 2)],
    "pe_router": [("out_ps", 8), ("lg_ps", 1), ("h2_nat_ps", 6), ("b1_ps", 1), ("rank", 1), ("counts", 1),
                  ("gateT_ps", 1), ("more_ps", 1), ("hot_ps", 1), ("b2_ps", 8)],
    "act_small": [("tr_evac_act", 8), ("kn_sq", 1), ("kn_rt", 1), ("ab_T", 1), ("z_sg", 1), ("dc_act", 1),
                  ("KmT_ready", 2), ("conv_rows_ready", 3)],
    "act_attend": [("mm_e", 1), ("mm_pT", 8), ("sw_e", 1), ("sw_pT", 8), ("ss_kT", 2), ("ss_e", 1)],
    "act_delta": [("gd_exp", 1), ("gs_eg", 1), ("gd_erow", 1), ("gd_dec_e", 1), ("gd_kdec", 2), ("gd_vbeta", 2),
                  ("inv_act", INV_COPIES), ("gd_v0_evac", 1), ("gd_v1_evac", 1)],
    "act_late": [("ms_e", 1), ("ms_o_evac", 2), ("lgT", 1), ("top_e", 1), ("b1_done", 1), ("gateT", 1)],
    "dve_load": [("eps", 1), ("tr_evac_dve", 8), ("colp_ready", 1), ("cst_done", 1), ("cin_ready", 1),
                 ("hT_ready", 8), ("memTn_ready", 8), ("kn_ss", 1), ("memkv_ready", 1)],
    "dve_small": [("conv_saved", 1), ("ab_done", 1), ("dc", 1), ("decay_ready", 1)],
    "dve_attend": [("mm_s_evac", 8), ("mm_m", 1), ("mm_p", 1), ("mm_o", 4), ("k_dup", 1), ("swa_rows_ready", 2),
                   ("sw_s_evac", 8), ("sw_m", 1), ("sw_p", 1), ("sw_o", 4)],
    "dve_window": [("ss_q", 1), ("ss_sT", 1), ("ss_m", 1), ("ss_p", 1), ("ss_pT", 1), ("ss_done", 1)],
    "dve_delta": [("gd_cum_evac", 1), ("gd_small", 1), ("gd_min", 1), ("gd_dec", 2), ("gd_at", 2), ("gd_qk_done", 2),
                  ("inv", 2 * len(INVERSE) - INV_COPIES), ("gd_s1_evac", 1), ("gd_r", 1), ("gdn_state_ready", 1), ("gs_kq", 1),
                  ("gs_v", 1)],
    "dve_memory": [("ms_q", 1), ("ms_m", 1), ("ms_p", 1), ("ms_pT", 1), ("ms_done", 1), ("o_ready", 1)],
    "dve_router": [("x1", 8), ("h2_ready", 8), ("top", 1), ("sel", 1), ("gate_ready", 1), ("pick_0", 1), ("more", 1), ("hot", 1),
                   ("items_ready", 1)],
}


PRIMED = ("put_ps", "part_ready", "put", "y_evac", "h_sum", "acc_done")


def build_layer(nc, A, O):
    with ExitStack() as ctx:
        build_program(nc, ctx, A, O)


def build_program(nc, ctx, A, O):
    sems, signalled = {}, {}
    where = {name: (chain, i) for chain, steps in CHAINS.items() for i, (name, _) in enumerate(steps)}

    def handle(name):
        if name not in sems:
            sems[name] = ctx.enter_context(nc.semaphore(name))
        return sems[name]

    def sem(name):
        if name not in where:
            return handle(name)
        chain, i = where[name]
        signalled[name] = signalled.get(name, 0) + 1
        for before_it, count in CHAINS[chain][:i]:
            assert signalled.get(before_it, 0) == count, (name, before_it)
        assert signalled[name] <= CHAINS[chain][i][1], name
        return handle(chain)

    def at(name, n):
        if name not in where:
            return handle(name), n + (name in PRIMED)
        chain, i = where[name]
        return handle(chain), sum(count for _, count in CHAINS[chain][:i]) + n

    made = {}

    def link(eng, name, ins):
        made[name] = made.get(name, 0) + 1
        ins.then_inc(sem(name), 1)
        eng.wait_ge(*at(name, made[name]))

    ring = ctx.enter_context(nc.sbuf_tensor("ring", [P, SLOTS, SLOT], F32))
    ARENA = 28600
    arena = ctx.enter_context(nc.sbuf_tensor("arena", [P, ARENA], F32))
    top = [0]

    def take(n):
        top[0] += n
        assert top[0] <= ARENA, top[0]
        return arena[:, top[0] - n:top[0]]

    def cols(region, a, n):
        return region[:, a:a + n]

    def grid(v, n):
        return v.rearrange("p (k n) -> p k n", n=n)

    ident, ones, blk64 = take(P), take(P), take(P)
    tri_incl, tri_strict, diag16 = take(P), take(P), take(P)
    neg_dist = take(3 * P)
    neg_dist_s = take(P)
    slot_iota = take(P)
    iota32 = take(32)
    colp = take(80)
    sink_b, alog_b, dt_b, brow_b = take(8), take(4), take(4), take(32)
    eps_col, thr_col, e_col = take(1), take(1), take(1)
    w_ab = grid(take(64), 8)
    w_rt = grid(take(256), 32)
    ab_T = take(T)
    ab_n = grid(take(24), 8)
    g_n, beta_n, gt0, gt1 = (grid(take(12), 4) for _ in range(4))
    conv_save = take(12 * 27)
    stat = take(160)
    xT_flat, hT_flat = take(KD * T), take(KD * T)
    xT, hT = grid(xT_flat, T), grid(hT_flat, T)
    at_qsk = top[0]
    qsk_flat = take(5 * T)
    vsT = take(T)
    qsk = grid(qsk_flat, T)
    region_q = arena[:, at_qsk:at_qsk + 6 * T]
    at_cv = top[0]
    cv_flat, zT_flat, qm_flat = take(12 * T), take(4 * T), take(4 * T)
    cv, zT, qm = grid(cv_flat, T), grid(zT_flat, T), grid(qm_flat, T)
    int_tmp, prm = cols(zT_flat, 0, 3 * P).bitcast(I32), cols(zT_flat, 3 * P, P)
    region_cv = arena[:, at_cv:at_cv + 20 * T]
    G_flat = take(KD * T)
    G = grid(G_flat, T)
    oT_flat = take(12 * T)
    oT = grid(oT_flat, T)
    at_mem = top[0]
    Kn_flat, Vm_flat, KmT_flat = take(1024), take(1024), take(1024)
    knorm_b = cols(KmT_flat, 0, P)
    region_mem = arena[:, at_mem:at_mem + 3072]
    scr = take(6400)

    x_nat = grid(cols(scr, 0, 2048), D)
    xs_nat = cols(scr, 2048, 1024)
    mem_nat = grid(cols(scr, 3072, 2048), D)
    memT = grid(cols(oT_flat, 0, 2048), NP_TOK)
    memTn = grid(cols(cv_flat, 0, 2048), NP_TOK)
    rsx, rsm = cols(Kn_flat, 0, T), cols(Kn_flat, 512, NP_TOK)
    cst_nat = cols(region_q, 0, 1536)
    cin = grid(cols(scr, 0, 12 * CONV_FLAT), CONV_FLAT)
    conv_y = grid(cols(scr, 3492, 576), 288)
    conv_sg = grid(cols(oT_flat, 2112, 576), 288)
    rt = grid(cols(scr, 4288, KD * T), T)
    cso = cols(oT_flat, 0, 1536)
    Kn, Vm = grid(Kn_flat, 512), grid(Vm_flat, 512)
    KmT = grid(KmT_flat, NP_TOK)

    gates_flat = cols(ring[:, PRE_SLOTS:SLOTS, :].rearrange("p s n -> p (s n)"), 0, 24 * T)
    gates = grid(gates_flat, T)

    B = [ctx.enter_context(nc.psum_tensor(f"bank{i}", [P, 512], F32)) for i in range(8)]

    LN1, LN2, LNM, C_GDN, C_QM, C_QS, C_KS, C_CONV = 0, 8, 16, 24, 25, 26, 27, 28

    w_in, w_mkv, w_br, w_out = A["w_in"][0], A["w_mem_kv"][0], A["w_branch"][0], A["w_out"][0]

    def columns(w, a):
        return [(0, SLOT, 256, w[:, a:a + 256].rearrange("(k p) n -> p k n", p=P))]

    pieces = [columns(w_mkv, 256 * i) for i in range(4)]
    PC_QM = len(pieces)
    pieces += [columns(w_in, OFF_QM + 256 * i) for i in range(2)]
    PC_IN = len(pieces)
    pieces += [columns(w_in, 256 * i) for i in range(OFF_AB // 256)]
    N_PROJ = len(pieces)
    PC_GATE = {}

    def gate_pieces(first, end):
        for i in range(first, end):
            PC_GATE[i] = len(pieces)
            pieces.append(columns(w_in, OFF_GATE + 256 * i)[0:1])

    gate_pieces(0, 7)
    PC_SWA = len(pieces)
    pieces.append([(0, 1024, P, A["cache_swa_k"][0].rearrange("b w k d -> w b (k d)")),
                   (1024, 1024, P, A["cache_swa_v"][0].rearrange("b w k d -> w b (k d)"))])
    gate_pieces(7, 11)
    PC_STATE = len(pieces)
    state = A["state_gdn"][0].rearrange("b h k v -> k (b h) v")
    pieces += [[(0, SLOT, HD_G, state[:, 16 * i:16 * i + 16, :])] for i in range(2)]
    gate_pieces(11, 12)
    PC_BR = {}

    def branch_pieces(n):
        PC_BR[n] = len(pieces)
        v = w_br[n].rearrange("(c p) d -> p c d", p=P)
        return [[(0, SLOT, 512, v[:, :, 512 * i:512 * i + 512])] for i in range(2)]

    pieces += branch_pieces(BRANCHES[0])
    PC_MK = len(pieces)
    for name in ("cache_mem_k", "cache_mem_v"):
        v = A[name][0].rearrange("b (c m) h d -> m (b c) (h d)", m=P)
        pieces += [[(0, SLOT, 512, v[:, 4 * i:4 * i + 4, :])] for i in range(4)]
    PC_MV = PC_MK + 4
    pieces += branch_pieces(BRANCHES[1])
    pieces += branch_pieces(BRANCHES[2])
    PC_OUT = len(pieces)
    pieces += [columns(w_out, 256 * i) for i in range(4)]
    N_PRE = len(pieces)
    landed_at, landed_pre = [], [0] * SLOTS
    for i, dmas in enumerate(pieces):
        landed_pre[i % PRE_SLOTS] += 16 * len(dmas)
        landed_at.append(landed_pre[i % PRE_SLOTS])
    landed = [sem(f"landed{s}") for s in range(SLOTS)]
    release = {i: ("proj", 2 * i + 2) for i in range(N_PROJ)}
    release.update({PC_GATE[i]: ("gate_ps", 2 * i + 2) for i in range(12)})
    release.update({PC_SWA: ("ss_o_ps", 1), PC_STATE: ("state_used", 1), PC_STATE + 1: ("state_used", 2)})
    for i in range(4):
        release[PC_MK + i], release[PC_MV + i] = ("ms_mul", 2 * i + 2), ("ms_o_ps", 2 * i + 2)
        release[PC_OUT + i] = ("out_ps", 2 * i + 2)
    for j, n in enumerate(BRANCHES):
        for i in range(2):
            release[PC_BR[n] + i] = ("branch", 8 * j + 4 * i + 4)

    def slot(i):
        return ring[:, i % PRE_SLOTS, :]

    def has_landed(eng, i):
        eng.wait_ge(landed[i % PRE_SLOTS], landed_at[i])

    def expert_slot(p):
        return (N_PRE + p) % PRE_SLOTS if p < PRE_SLOTS else p

    GATE_BANKS = [2, 3, 0, 1, 3, 4, 5, 7, 6, 7, 6, 7, 6, 7, 6] + [1 + n % 2 for n in range(15, 20)] + [7, 3, 3, 3]

    n_store = [0]

    HN = [4, 5, 8, 4]
    HN_BASE = [0, 4, 9, 17]

    block = ctx.enter_context(nc.Block())

    sw_s = cols(scr, 0, H_S * 3 * P)
    sw_s3 = grid(sw_s, 3 * P)
    sw_pT = grid(cols(scr, 3072, 2 * 3 * P), 3 * P)
    k_dup = grid(cols(scr, 3840, 2 * T), T)
    kv_nat = cols(scr, 4368, 3 * P)
    kv_s = cols(scr, 4752, 2 * P)
    mm_s = grid(cols(scr, 0, 8 * NP_TOK), NP_TOK)
    mm_pT = grid(cols(scr, 2048, 2 * NP_TOK), NP_TOK)
    sw_kT = grid(cols(scr, 0, 1024), P)
    q_bd = cols(scr, 1024, 64)
    q_bd3 = q_bd.rearrange("p (b h) -> p b h", h=H_S)
    ss_prod = cols(scr, 1088, 64)
    ss_prod3 = ss_prod.rearrange("p (b h) -> p b h", h=H_S)
    rows64 = cols(scr, 1664, 128)
    ss_T = cols(scr, 1152, 64)
    ss = cols(scr, 1216, P + 1)
    ss_pT = cols(scr, 1408, 64)
    ss_pb = cols(scr, 1472, P)
    ss_o = cols(scr, 1600, 64)
    ss_o3 = ss_o.rearrange("p (b h) -> p b h", h=H_S)
    inv = [grid(cols(scr, 1024 * i, 1024), P) for i in range(6)]
    inv_flat = [cols(scr, 1024 * i, 1024) for i in range(6)]
    dec_flat, intra_flat = cols(G_flat, 0, 1024), cols(G_flat, 1024, 1024)
    dec, intra = grid(dec_flat, P), grid(intra_flat, P)
    k_dec, v_beta = grid(Kn_flat, P), grid(Vm_flat, P)
    v_new = grid(cols(KmT_flat, 0, 512), P)
    s_one = grid(cols(KmT_flat, 512, 512), P)
    q_dec, r_new, e_row = (grid(cols(region_q, 512 * i, 512), P) for i in range(3))
    g_sm = cols(scr, 6144, 64)
    s_out = cols(scr, 0, 4096)
    s_out3 = grid(s_out, P)
    vn_mask = [grid(cols(scr, 4096 + 1024 * i, 1024), P) for i in range(2)]
    gs = cols(scr, 6144, 256)
    gs_kq = gs[:, 0:64].rearrange("p (n c) -> p n c", c=2)
    gs_qk, gs_bc = gs[:, 64:96], gs[:, 96:192]
    gs_vn, gs_t = gs[:, 192:224], gs[:, 224:256]
    gs_nat = cols(region_q, 0, 2 * P)
    gs_dg = cols(region_q, 256, 64)
    pick8 = grid(Kn_flat, P)
    q_nat8 = cols(Vm_flat, 0, 512)
    ms_T = cols(Vm_flat, 512, 64)
    ms = cols(Vm_flat, 576, NP_TOK)
    ms_pT = cols(Vm_flat, 832, 64)
    mk_prod = grid(cols(G_flat, 0, 1024), P)
    ms_pv = grid(cols(G_flat, 1024, 1024), 512)
    mT = grid(cols(cv_flat, 0, KD * T), T)
    mtmp = grid(cols(scr, 0, 2 * T), T)
    h2_nat = grid(cols(oT_flat, 0, 3 * D), D)
    h2_parts = cols(region_cv, 0, 4608).bitcast(BF16).rearrange("p (s c d) -> p s c d", s=3, d=D)
    b1_nat, b2_nat = cols(scr, 0, 2048), cols(scr, 2048, 1024)
    rr, lgT, gateT = (cols(scr, 3072 + T * i, T) for i in range(3))
    used_scr = [4096]

    def tmp(n):
        used_scr[0] += n
        return cols(scr, used_scr[0] - n, n)

    lg_n, sel_n = grid(tmp(96), 32), grid(tmp(96), 32)
    top_flat = tmp(3 * (8 + 8 + 4 + 1))
    top_v, top_f, top_p = (grid(cols(top_flat, a, n), n // 3) for a, n in ((0, 24), (24, 24), (48, 12)))
    top_s = cols(top_flat, 60, 3)
    top_i = tmp(24).bitcast(U32).rearrange("p (c n) -> p c n", n=8)
    hot4, sel4 = (tmp(384).rearrange("p (c r e) -> p c r e", c=3, r=4) for _ in range(2))
    pick_0 = grid(tmp(3 * BLK), BLK)
    more_f, more_pos, item_hot, item_f = tmp(1), tmp(1), tmp(16), tmp(1)
    used_cols = [0]

    def moe(n):
        used_cols[0] += n
        assert used_cols[0] <= 3072
        return cols(region_mem, used_cols[0] - n, n)

    pos_n, gate_n = grid(moe(96), 32), grid(moe(96), 32)
    b1_e = grid(moe(16 * N_EXP), 16)
    item_list = moe(2 + 2 * N_ITEM)
    item_int = item_list.bitcast(I32)
    item_count, item_expert, item_first = item_int[:, 0:1], item_int[:, 1:1 + N_ITEM], item_int[:, 1 + N_ITEM:1 + 2 * N_ITEM]
    places = moe(P * N_BLK)
    pick = moe(96).bitcast(BF16).rearrange("p (c n) -> p c n", n=BLK)
    gpick = grid(moe(3 * P), P)
    xg = grid(moe(512), BLK)
    put = moe(T)
    h_odd, h_sum = cols(scr, 0, 2048), cols(scr, 2048, 2048)
    glu, lin, sg, act_e = (cols(scr, 4096 + 512 * i, 512) for i in range(4))
    y_e = cols(region_q, 0, 1024)
    part_flat = hT_flat
    part = hT
    y_out = h2_nat

    def bc(v, n):
        return v.unsqueeze(len(v.shape)).broadcast_to([*v.shape, n])

    def mid(v, n):
        return v.unsqueeze(1).broadcast_to([v.shape[0], n, v.shape[1]])

    @block.sync
    def _(sp):
        sp.dma_start(x_nat, A["x_prompt"][0].rearrange("(c p) d -> p c d", p=P)).then_inc(sem("x_landed"), 16)
        sp.dma_start(mem_nat, A["mem_prompt"][0].rearrange("(c p) d -> p c d", p=P)).then_inc(sem("mem_landed"), 16)
        sp.wait_ge(*at("prm_landed", 160))
        sp.wait_ge(*at("cst_landed", 16))
        for i, dmas in enumerate(pieces):
            if i >= PRE_SLOTS:
                sp.wait_ge(*at(*release[i - PRE_SLOTS]))
            for a, n, w, src in dmas:
                sp.dma_start(grid(slot(i)[:, a:a + n], w), src).then_inc(landed[i % PRE_SLOTS], 16)

        w1 = A["w_mlp1"][0].rearrange("e (k p) n -> e k p n", p=P)
        w2 = A["w_mlp2"][0].rearrange("e (j k p) n -> e j p k n", p=P, k=2)

        def load_expert(e, item):
            for p in range(SLOTS):
                s = expert_slot(p)
                if item is None:
                    sp.wait_ge(*at(*(release[N_PRE - PRE_SLOTS + p] if p < PRE_SLOTS else ("merged", 24))))
                elif p < 8:
                    sp.wait_ge(*at("mm1", item * 7 - 7 + (p // 2 + 1 if p < 6 else 7)))
                else:
                    sp.wait_ge(*at("mm2", item * 4 - 4 + (p - 7)))
                if p < 8:
                    src = w1[bass.ds(e, 1), p, :, :].rearrange("e p n -> p (e n)")
                    dst = ring[:, s, :]
                else:
                    src = w2[bass.ds(e, 1), p - 8, :, :, :].rearrange("e p k n -> p (e k) n")
                    dst = grid(ring[:, s, :], D)
                sp.dma_start(dst, src).then_inc(landed[s], 16)

        load_expert(0, None)
        with sp.Fori(1, N_EXP) as e:
            load_expert(e, e)
        sp.wait_ge(*at("items_ready", 1))
        n_items = sp.value_load(item_count[0:1, 0:1], min_val=N_EXP, max_val=N_EXP + EXTRA)
        with sp.If(n_items > N_EXP):
            with sp.Fori(N_EXP, n_items) as item:
                e = sp.value_load(item_expert[0:1, bass.ds(item, 1)], min_val=0, max_val=N_EXP - 1)
                load_expert(e, item)
        sp.wait_ge(*at("y_ready", 3))
        sp.dma_start(O["y_p"][0].rearrange("(c p) d -> p c d", p=P), y_out[:, 0:2, :]).then_inc(sem("y_stored"), 16)
        sp.dma_start(O["y_s"].rearrange("b l d -> (b l) d"), y_out[0:NB, 2, :]).then_inc(sem("y_stored"), 16)
        sp.wait_ge(*at("y_stored", 32))

    @block.gpsimd
    def _(pool):
        def step(ins):
            link(pool, "pool_step", ins)

        step(pool.memset(arena[:, 0:6 * P], 1.0))
        step(pool.affine_select(out=ident, in_=ident, compare_op=ALU.is_equal, fill=0.0, base=0,
                                pattern=[[-1, P]], channel_multiplier=1))
        pool.nop().then_inc(sem("const_ready"), 1)
        step(pool.affine_select(out=tri_incl, in_=tri_incl, compare_op=ALU.is_ge, fill=0.0, base=0,
                                pattern=[[1, P]], channel_multiplier=-1))
        step(pool.affine_select(out=tri_strict, in_=tri_strict, compare_op=ALU.is_gt, fill=0.0, base=0,
                                pattern=[[1, P]], channel_multiplier=-1))
        d16 = diag16.rearrange("p (a b) -> p a b", b=16)
        step(pool.affine_select(out=d16, in_=d16, compare_op=ALU.is_ge, fill=0.0, base=0,
                                pattern=[[-16, 8], [0, 16]], channel_multiplier=1))
        step(pool.affine_select(out=d16, in_=d16, compare_op=ALU.is_ge, fill=0.0, base=15,
                                pattern=[[16, 8], [0, 16]], channel_multiplier=-1))
        b64 = blk64.rearrange("p (a b) -> p a b", b=64)
        step(pool.affine_select(out=b64, in_=b64, compare_op=ALU.is_ge, fill=0.0, base=0,
                                pattern=[[-64, 2], [0, 64]], channel_multiplier=1))
        pool.affine_select(out=b64, in_=b64, compare_op=ALU.is_ge, fill=0.0, base=63,
                           pattern=[[64, 2], [0, 64]], channel_multiplier=-1).then_inc(sem("const_ready"), 1)

        step(pool.iota(int_tmp[:, 0:P], pattern=[[1, P]], base=0, channel_multiplier=-1))
        step(pool.iota(int_tmp[:, P:3 * P], pattern=[[1, 2 * P]], base=-P, channel_multiplier=-1))
        step(pool.tensor_copy(neg_dist, int_tmp))
        step(pool.affine_select(out=neg_dist[:, 0:P], in_=neg_dist[:, 0:P], compare_op=ALU.is_ge, fill=NEG, base=0,
                                pattern=[[-1, P]], channel_multiplier=1))
        step(pool.affine_select(out=neg_dist[:, P:3 * P], in_=neg_dist[:, P:3 * P], compare_op=ALU.is_ge, fill=NEG,
                                base=P, pattern=[[-1, 2 * P]], channel_multiplier=1))
        step(pool.affine_select(out=neg_dist[:, P:3 * P], in_=neg_dist[:, P:3 * P], compare_op=ALU.is_ge, fill=NEG,
                                base=0, pattern=[[1, 2 * P]], channel_multiplier=-1))
        step(pool.iota(int_tmp[:, 0:P], pattern=[[1, P]], base=-P, channel_multiplier=0))
        step(pool.iota(int_tmp[:, P:2 * P], pattern=[[0, 2], [1, BLK]], base=0, channel_multiplier=0))
        step(pool.iota(int_tmp[:, 2 * P:2 * P + 32], pattern=[[1, 32]], base=0, channel_multiplier=0))
        step(pool.iota(int_tmp[:, 2 * P + 32:2 * P + 33], pattern=[[0, 1]], base=0, channel_multiplier=1))
        step(pool.tensor_copy(neg_dist_s, int_tmp[:, 0:P]))
        step(pool.tensor_copy(slot_iota, int_tmp[:, P:2 * P]))
        step(pool.tensor_copy(iota32, int_tmp[:, 2 * P:2 * P + 32]))
        pool.tensor_copy(e_col, int_tmp[:, 2 * P + 32:2 * P + 33]).then_inc(sem("const_ready"), 1)

        def spread(v, n):
            return v.broadcast_to([P, n])
        pool.dma_start(knorm_b, spread(A["k_norm_mem"], P)).then_inc(sem("rowp_landed"), 16)
        pool.dma_start(sink_b, spread(A["swa_sinks"], 8)).then_inc(sem("rowp_landed"), 16)
        pool.dma_start(alog_b, spread(A["a_log"], 4)).then_inc(sem("rowp_landed"), 16)
        pool.dma_start(dt_b, spread(A["dt_bias"], 4)).then_inc(sem("rowp_landed"), 16)
        pool.dma_start(brow_b, spread(A["b_router"], 32)).then_inc(sem("rowp_landed"), 16)
        pool.dma_start(w_ab, w_in[:, OFF_AB:OFF_AB + 8].rearrange("(k p) n -> p k n", p=P)).then_inc(sem("wab_landed"), 16)
        pool.dma_start(w_rt, A["w_router"][0].rearrange("(k p) n -> p k n", p=P)).then_inc(sem("wrt_landed"), 16)

        def store(dst, src):
            pool.dma_start(dst, src).then_inc(sem("stored"), 16)
            n_store[0] += 1

        store(O["swa_ks"][0, :, 0:WIN - 1].rearrange("b w k d -> b w (k d)"),
              A["cache_swa_k"][0, :, 1:WIN].rearrange("b w k d -> b w (k d)"))
        store(O["swa_vs"][0, :, 0:WIN - 1].rearrange("b w k d -> b w (k d)"),
              A["cache_swa_v"][0, :, 1:WIN].rearrange("b w k d -> b w (k d)"))
        pool.wait_ge(*at("memkv_ready", 1))
        store(O["mem_k"][0, 0].rearrange("(c m) h d -> m c (h d)", m=P), Kn)
        store(O["mem_v"][0, 0].rearrange("(c m) h d -> m c (h d)", m=P), Vm)
        pool.wait_ge(*at("stored", 16 * n_store[0]))
        pool.nop().then_inc(sem("memkv_stored"), 1)
        pool.wait_ge(*at("conv_rows_ready", 3))
        store(O["conv_p"][0, 0], cso[0:3, :])
        store(O["conv_s"][0].rearrange("b j n -> (b j) n"), cso[3:27, :])
        pool.wait_ge(*at("stored", 16 * n_store[0]))
        pool.nop().then_inc(sem("conv_stored"), 1)
        pool.wait_ge(*at("swa_rows_ready", 2))
        store(O["swa_kp"][0, 0].rearrange("w k d -> w (k d)"), kv_nat[:, 2 * P:3 * P])
        store(O["swa_vp"][0, 0].rearrange("w k d -> w (k d)"), kv_nat[:, P:2 * P])
        store(O["swa_ks"][0, :, WIN - 1].rearrange("b k d -> b (k d)"), kv_s[0:NB, 0:P])
        store(O["swa_vs"][0, :, WIN - 1].rearrange("b k d -> b (k d)"), kv_s[0:NB, P:2 * P])
        pool.wait_ge(*at("stored", 16 * n_store[0]))
        pool.nop().then_inc(sem("swa_stored"), 1)
        pool.wait_ge(*at("gdn_state_ready", 1))
        store(O["gdn_p"][0, 0].rearrange("h k v -> k h v"), s_one)
        pool.wait_ge(*at("gs_state_ready", 8))
        for j in range(2):
            store(O["gdn_s"][0].rearrange("b h k v -> k (b h) v")[:, 16 * j:16 * j + 16, :], s_out3[:, 16 * j:16 * j + 16, :])
        pool.wait_ge(*at("stored", 16 * n_store[0]))
        pool.nop().then_inc(sem("gdn_stored"), 1)
        pool.wait_ge(*at("ms_done", 1))
        for r in range(N_BLK):
            pool.tensor_scalar(places[:, P * r:P * r + P], slot_iota, float(BLK * r), None, ALU.add)
        pool.memset(put, 0.0)
        pool.memset(item_list, 0.0)
        pool.memset(y_e, 0.0).then_inc(sem("moe_ready"), 1)
        pool.wait_ge(*at("merged", 24))
        pool.dma_start(b1_nat[0:N_EXP, :], A["b_mlp1"][0]).then_inc(sem("b_landed"), 16)
        pool.dma_start(b2_nat[0:N_EXP, :], A["b_mlp2"][0]).then_inc(sem("b_landed"), 16)

        pool.wait_ge(*at("items_ready", 1))
        pool.wait_ge(*at("acc_ready", 8))
        n_items = pool.value_load(item_count[0:1, 0:1], min_val=N_EXP, max_val=N_EXP + EXTRA)
        pool.nop().then_inc(sem("acc_done"), 1)
        with pool.Fori(0, n_items) as item:
            pool.wait_ge(*at("part_ready", (item + 1) * 8))
            pool.tensor_tensor(xT_flat, xT_flat, part_flat, ALU.add).then_inc(sem("acc_done"), 1)
            pool.wait_ge(*at("acc_done", item + 1))
        pool.wait_ge(*at("part_ready", (n_items + 1) * 8))
        pool.tensor_tensor(xT_flat, xT_flat, part_flat, ALU.add).then_inc(sem("acc_last"), 1)

    @block.tensor
    def _(pe):
        def mm(out, lhsT, rhs, start=True, stop=True):
            return nc.tensor.matmul(out, lhsT, rhs, start=start, stop=stop, skip_group_check=True)

        def tr(out, in_):
            n = in_.shape[0]
            return nc.tensor.transpose(out, in_, ident[0:n, 0:n])

        pe.wait_ge(*at("const_ready", 1))
        pe.wait_ge(*at("x_landed", 16))
        pe.wait_ge(*at("xs_landed", 16))
        for g in range(16):
            k = g % 8
            if g == 8:
                pe.wait_ge(*at("mem_landed", 16))
            if g >= 4:
                pe.wait_ge(*at("tr_evac_dve" if g % 2 else "tr_evac_act", (g - 4) // 2 + 1))
            src = x_nat if g < 8 else mem_nat
            for c in range(2):
                ins = tr(B[g % 4][:, P * c:P * c + P], src[:, c, P * k:P * k + P])
            if g < 8:
                ins = tr(B[g % 4][:, 2 * P:T], xs_nat[0:NB, P * k:P * k + P])
            ins.then_inc(sem("x_T"), 1)
        pe.wait_ge(*at("prm_landed", 160))
        tr(B[7][:, 0:76], prm[0:76, :]).then_inc(sem("prm_T"), 1)
        pe.wait_ge(*at("cst_landed", 16))
        for c in range(12):
            ins = tr(B[6][:, 24 * c:24 * c + 24], cst_nat[0:24, P * c:P * c + P])
        ins.then_inc(sem("cst_T"), 1)
        for i, n in ((0, T), (1, NP_TOK)):
            pe.wait_ge(*at("ln_sq", i + 1))
            for k in range(KD):
                ins = mm(B[4 + i][:, 0:n], ones, G_flat[:, n * k:n * k + n], start=(k == 0), stop=(k == KD - 1))
            ins.then_inc(sem("ln_ss"), 1)

        pe.wait_ge(*at("memTn_ready", 8))
        for n in range(8):
            i, c = n // 2, n % 2
            if n % 2 == 0:
                has_landed(pe, i)
            if n >= 4:
                pe.wait_ge(*at("proj_evac", n - 3))
            w = grid(slot(i), 256)
            for k in range(KD):
                ins = mm(B[n % 4][:, 0:256], memTn[:, k, P * c:P * c + P], w[:, k, :], start=(k == 0), stop=(k == KD - 1))
            ins.then_inc(sem("proj"), 1)

        def project(i, half, n, rhs):
            if half == 0:
                has_landed(pe, i)
            pe.wait_ge(*at("proj_evac", n - 3))
            w = grid(slot(i), 256)
            for k in range(KD):
                ins = mm(B[n % 4][:, 0:T], w[:, k, P * half:P * half + P], rhs[:, k, :], start=(k == 0), stop=(k == KD - 1))
            ins.then_inc(sem("proj"), 1)

        def gate(n, after=None, blocks=range(KD)):
            if blocks[0] == 0:
                has_landed(pe, PC_GATE[n // 2])
                if after is not None:
                    pe.wait_ge(*at("gate_evac", after + 1))
            w = grid(slot(PC_GATE[n // 2]), 256)
            a = P * (n % 2)
            for k in blocks:
                ins = mm(B[GATE_BANKS[n]][:, 0:T], w[:, k, a:a + P], hT[:, k, :], start=(k == 0), stop=(k == KD - 1))
            if blocks[-1] == KD - 1:
                ins.then_inc(sem("gate_ps"), 1)

        def branch(j, chunks=range(8)):
            for d in chunks:
                i = PC_BR[BRANCHES[j]] + d // 4
                has_landed(pe, i)
                w = grid(slot(i), 512)
                m = 8 * j + d
                if m % 8 >= 4 or j == 2:
                    pe.wait_ge(*at("merged", m - 3))
                for c in range(4):
                    ins = mm(B[4 + m % 4][:, 0:T], w[:, c, P * (d % 4):P * (d % 4) + P], oT[:, 4 * BRANCHES[j] + c, :],
                             start=(c == 0), stop=(c == 3))
                ins.then_inc(sem("branch"), 1)

        def norm_sums(s, lhsT):
            pe.wait_ge(*at("hn_sq", s + 1))
            for i in range(HN[s]):
                if i >= 4 or s:
                    pe.wait_ge(*at("hn_rt", max(HN_BASE[s], HN_BASE[s] + i - 3) if i >= 4 else HN_BASE[s]))
                mm(B[4 + i % 4][:, 0:T], lhsT, G_flat[:, T * i:T * i + T]).then_inc(sem("hn_ss"), 1)

        pe.wait_ge(*at("const_ready", 3))
        pe.wait_ge(*at("hT_ready", 8))
        for n in range(8, 12):
            project(PC_QM + (n - 8) // 2, n % 2, n, hT)
        pe.wait_ge(*at("cst_done", 1))
        pe.wait_ge(*at("colp_ready", 1))
        norm_sums(0, ones)
        for n in range(12, 34):
            project(PC_IN + (n - 12) // 2, n % 2, n, hT)
        pe.wait_ge(*at("wab_landed", 16))
        pe.wait_ge(*at("hn_rt", 4))
        for k in range(KD):
            ins = mm(B[4][0:8, 0:T], w_ab[:, k, :], hT[:, k, :], start=(k == 0), stop=(k == KD - 1))
        ins.then_inc(sem("ab_ps"), 1)
        pe.wait_ge(*at("proj_evac", 32))
        gate(0)
        gate(1)
        pe.wait_ge(*at("ab_T", 1))
        for c, (a, n) in enumerate(TOK):
            ins = tr(B[5][0:n, 8 * c:8 * c + 8], ab_T[0:8, a:a + n])
        ins.then_inc(sem("ab_nT"), 1)
        pe.wait_ge(*at("ab_done", 1))
        norm_sums(1, blk64)
        pe.wait_ge(*at("proj_evac", 34))
        gate(2)
        gate(3)
        norm_sums(2, ones)
        pe.wait_ge(*at("memkv_ready", 1))
        pe.wait_ge(*at("hn_rt", HN_BASE[3]))
        for c in range(2):
            for h in range(H_M):
                ins = tr(B[6 + c][:, P * h:P * h + P], Kn[:, c, P * h:P * h + P])
            ins.then_inc(sem("kmT_ps"), 1)
        pe.wait_ge(*at("conv_saved", 1))
        pe.wait_ge(*at("gate_evac", 4))
        cs = grid(conv_save, 27)
        for c in range(12):
            ins = tr(B[c // 4][0:27, P * (c % 4):P * (c % 4) + P], cs[:, c, :])
            if c % 4 == 3:
                ins.then_inc(sem("conv_rows_ps"), 1)

        gate(4)
        gate(5)
        gate(6)

        def attend(tag, n, between, scores, values, part_n):
            if tag == "mm":
                pe.wait_ge(*at("gate_evac", 7))
            for i in range(n):
                if i >= 2:
                    pe.wait_ge(*at(tag + "_s_evac", i - 1))
                scores(i, B[i % 2]).then_inc(sem(tag + "_s"), 1)
            for i in between:
                gate(i, after=i - 2 if i > between[1] else None)
            for i in range(n):
                pe.wait_ge(*at(tag + "_p", 1))
                if i >= 2:
                    pe.wait_ge(*at(tag + "_pT", i - 1))
                part_n(i, B[2 + i % 2]).then_inc(sem(tag + "_pT_ps"), 1)
                if i:
                    values(i - 1)
            values(n - 1)

        pe.wait_ge(*at("hn_done", HN_BASE[3]))
        pe.wait_ge(*at("KmT_ready", 2))
        pe.wait_ge(*at("conv_rows_ready", 3))

        def mm_scores(i, bank):
            h, q = i // 2, i % 2
            return mm(bank[:, 0:256], qm[:, h, P * q:P * q + P], KmT[:, h, :])

        def mm_turn(i, bank):
            tr(bank[:, 0:P], mm_s[:, i, 0:P])
            return tr(bank[:, P:2 * P], mm_s[:, i, P:2 * P])

        def mm_values(i):
            h, q = i // 2, i % 2
            pe.wait_ge(*at("mm_pT", i + 1))
            if q == 0 and h >= 2:
                pe.wait_ge(*at("mm_o", h - 1))
            for c in range(2):
                ins = mm(B[4 + h % 2][:, P * q:P * q + P], Vm[:, c, P * h:P * h + P], mm_pT[:, i % 2, P * c:P * c + P],
                         start=(c == 0), stop=(c == 1))
            ins.then_inc(sem("mm_o_ps"), 1)

        attend("mm", 8, (7, 8), mm_scores, mm_values, mm_turn)

        pe.wait_ge(*at("gate_evac", 9))
        pe.wait_ge(*at("mm_o", 4))
        for j in range(2):
            tr(B[6][:, P * j:P * j + P], vsT[:, P * j:P * j + P])
        tr(B[6][:, 2 * P:3 * P], qsk[:, 4, P:2 * P]).then_inc(sem("swa_nat"), 1)
        tr(B[7][0:NB, 0:P], qsk[:, 4, 2 * P:T])
        tr(B[7][0:NB, P:2 * P], vsT[:, 2 * P:T]).then_inc(sem("swa_nat"), 1)
        pe.wait_ge(*at("k_dup", 1))
        pe.wait_ge(*at("swa_rows_ready", 2))

        def sw_scores(i, bank):
            r = HD_S * (i % 2)
            q, k = qsk[r:r + HD_S, i // 2, :], k_dup[r:r + HD_S, i // 4, :]
            mm(bank[:, 0:P], q[:, 0:P], k[:, 0:P])
            return mm(bank[:, P:3 * P], q[:, P:2 * P], k[:, 0:2 * P])

        def sw_turn(i, bank):
            for c in range(3):
                ins = tr(bank[:, P * c:P * c + P], sw_s3[:, i, P * c:P * c + P])
            return ins

        def sw_values(i):
            r, v = HD_S * (i % 2), HD_S * (i // 4)
            pe.wait_ge(*at("sw_pT", i + 1))
            if i % 2 == 0 and i >= 4:
                pe.wait_ge(*at("sw_o", i // 2 - 1))
            out = B[4 + (i // 2) % 2][r:r + HD_S, :]
            mm(out[:, 0:P], kv_nat[:, v:v + HD_S], sw_pT[:, i % 2, 0:P])
            mm(out[:, P:2 * P], kv_nat[:, v:v + HD_S], sw_pT[:, i % 2, P:2 * P], stop=False)
            mm(out[:, P:2 * P], kv_nat[:, P + v:P + v + HD_S], sw_pT[:, i % 2, 2 * P:3 * P],
               start=False).then_inc(sem("sw_o_ps"), 1)

        attend("sw", 8, (9, 10, 11, 12), sw_scores, sw_values, sw_turn)

        pe.wait_ge(*at("sw_o", 4))
        has_landed(pe, PC_SWA)
        kc, vc = grid(slot(PC_SWA)[:, 0:1024], P), grid(slot(PC_SWA)[:, 1024:2048], P)
        for b in range(NB):
            ins = tr(B[b // 4][:, P * (b % 4):P * (b % 4) + P], kc[:, b, :])
            if b % 4 == 3:
                ins.then_inc(sem("ss_kT_ps"), 1)
        pe.wait_ge(*at("ss_q", 1))
        mm(B[3][0:64, 0:1], ss_prod, ones[:, 0:1])
        mm(B[3][0:64, 1:2], rows64[0:1, 0:64], ones[0:1, 0:1])
        mm(B[3][0:64, 2:3], rows64[0:1, 64:128], ones[0:1, 0:1]).then_inc(sem("ss_new"), 1)
        for b in range(NB):
            pe.wait_ge(*at("ss_kT", b // 4 + 1))
            ins = mm(B[2][:, 8 * b:8 * b + 8], sw_kT[:, b, :], q_bd[:, 8 * b:8 * b + 8])
        ins.then_inc(sem("ss_s"), 1)
        pe.wait_ge(*at("ss_sT", 1))
        tr(B[4][0:64, 0:P], ss_T).then_inc(sem("ss_rows"), 1)
        gate(13, after=11)
        pe.wait_ge(*at("ss_p", 1))
        mm(B[3][:, 0:64], ss_pb[0:64, :], ident[0:64, 0:64])
        tr(B[5][:, 0:64], ss[0:64, 0:P]).then_inc(sem("ss_pT_ps"), 1)
        pe.wait_ge(*at("ss_pT", 1))
        for b in range(NB):
            ins = mm(B[2][:, 8 * b:8 * b + 8], vc[:, b, :], ss_pT[:, 8 * b:8 * b + 8])
        ins.then_inc(sem("ss_o_ps"), 1)

        gate(14, after=12)
        pe.wait_ge(*at("ss_done", 1))
        pe.wait_ge(*at("decay_ready", 1))
        for c in range(2):
            mm(B[0][:, 4 * c:4 * c + 4], tri_incl, g_n[:, c, :])
            ins = mm(B[0][:, 8 + 4 * c:12 + 4 * c], ones, g_n[:, c, :])
        ins.then_inc(sem("gd_cum"), 1)
        for c in range(2):
            for h in range(H_G):
                ins = mm(B[1 + c][:, P * h:P * h + P], g_n[:, c, h:h + 1].broadcast_to([P, P]), tri_incl)
            ins.then_inc(sem("gd_row"), 1)
        for c in range(2):
            for h in range(H_G):
                ins = mm(B[3 + c][:, P * h:P * h + P], beta_n[:, c, h:h + 1].broadcast_to([P, P]), ident)
            ins.then_inc(sem("gd_brow"), 1)
        pe.wait_ge(*at("gate_evac", 15))
        for c in range(2):
            for h in range(H_G):
                k = cv[:, 4 + h, P * c:P * c + P]
                ins = mm(B[5 + c][:, P * h:P * h + P], k, k)
            ins.then_inc(sem("gd_kk"), 1)
        for c in range(2):
            if c:
                pe.wait_ge(*at("gd_cum_evac", 1))
            for h in range(H_G):
                ins = mm(B[7 if c == 0 else 0][:, P * h:P * h + P], cv[:, 4 + h, P * c:P * c + P], cv[:, h, P * c:P * c + P])
            ins.then_inc(sem("gd_qk"), 1)
        pe.wait_ge(*at("gd_dec", 2))
        for c in range(2):
            for h in range(H_G):
                ins = tr(B[1 + c][:, P * h:P * h + P], cv[:, 4 + h, P * c:P * c + P])
            ins.then_inc(sem("gd_kn"), 1)
        pe.wait_ge(*at("gd_at", 2))
        for c in range(2):
            for h in range(H_G):
                ins = tr(B[3 + c][:, P * h:P * h + P], cv[:, 8 + h, P * c:P * c + P])
            ins.then_inc(sem("gd_vn"), 1)

        pe.wait_ge(*at("gd_qk_done", 2))
        for s, (kind, a, b, _) in enumerate(INVERSE):
            for c in range(2):
                if s:
                    pe.wait_ge(*at(*inverse_out(s - 1, c)))
                bank = B[(5, 6, 7, 0)[2 * (s % 2) + c]]
                for h in range(H_G):
                    m = 4 * c + h
                    out = bank[:, P * h:P * h + P]
                    ins = tr(out, inv[a][:, m, :]) if kind == "turn" else mm(out, inv[a][:, m, :], inv[b][:, m, :])
                ins.then_inc(sem("inv_ps"), 1)
            if s == 0:
                pe.wait_ge(*at("gd_kdec", 2))
            if s < 20:
                n = 15 + s // 4
                gate(n, after=n - 2 if n > 16 else None, blocks=range(2 * (s % 4), 2 * (s % 4) + 2))
        for c in range(2):
            pe.wait_ge(*at(*inverse_out(len(INVERSE) - 1, c)))
        pe.wait_ge(*at("gd_vbeta", 2))

        def per_head(bank, left, right, name, **kw):
            for h in range(H_G):
                ins = mm(bank[:, P * h:P * h + P], left(h), right(h), **kw)
            if name:
                ins.then_inc(sem(name), 1)

        pe.wait_ge(*at("gate_evac", 20))
        T_inv = inv[3]
        per_head(B[1], lambda h: T_inv[:, h, :], lambda h: v_beta[:, h, :], "gd_v0")
        gate(20, blocks=range(0, 2))
        pe.wait_ge(*at("gd_v0_evac", 1))
        per_head(B[2], lambda h: k_dec[:, h, :], lambda h: v_new[:, h, :], "gd_s1")
        per_head(B[3], lambda h: v_new[:, h, :], lambda h: intra[:, h, :], "gd_o0")
        gate(20, blocks=range(2, 4))
        pe.wait_ge(*at("gd_s1_evac", 1))
        per_head(B[4], lambda h: cv[:, 4 + h, P:2 * P], lambda h: s_one[:, h, :], "gd_ks")
        gate(20, blocks=range(4, 6))
        pe.wait_ge(*at("gd_r", 1))
        per_head(B[1], lambda h: T_inv[:, 4 + h, :], lambda h: r_new[:, h, :], "gd_v1")
        gate(20, blocks=range(6, 8))
        pe.wait_ge(*at("gd_v1_evac", 1))
        for h in range(H_G):
            mm(B[5][:, P * h:P * h + P], s_one[:, h, :], q_dec[:, h, :], stop=False)
            ins = mm(B[5][:, P * h:P * h + P], v_new[:, h, :], intra[:, 4 + h, :], start=False)
        ins.then_inc(sem("gd_o1"), 1)
        per_head(B[2], lambda h: k_dec[:, 4 + h, :], lambda h: v_new[:, h, :], "gd_s2")

        pe.wait_ge(*at("gdn_state_ready", 1))
        pe.wait_ge(*at("gs_kq", 1))
        for i in range(32):
            if i % 16 == 0:
                has_landed(pe, PC_STATE + i // 16)
            ins = mm(B[0][:, 2 * i:2 * i + 2], slot(PC_STATE + i // 16)[:, P * (i % 16):P * (i % 16) + P], gs_kq[:, i, :])
        mm(B[1][:, 0:32], ones, gs_qk)
        mm(B[1][:, 32:96], ones[0:8, :], gs_dg[0:8, :]).then_inc(sem("gs_ps"), 1)
        gate(21)
        pe.wait_ge(*at("gs_v", 1))
        tr(B[2][0:32, 0:P], gs_vn)
        tr(B[2][0:32, P:2 * P], gs_t).then_inc(sem("gs_rows"), 1)
        gate(22, after=21)
        for j in range(8):
            if j == 2:
                gate(23, after=22)
            pe.wait_ge(*at("gs_mask", j // 2 + 1))
            if j >= 4:
                pe.wait_ge(*at("gs_state_ready", j - 3))
            elif j == 3:
                pe.wait_ge(*at("gate_evac", 21))
            mm(B[4 + j % 4][:, :], gs_nat[0:32, P:2 * P],
               vn_mask[(j // 2) % 2][0:32, 4 * (j % 2):4 * (j % 2) + 4, :].rearrange("p a b -> p (a b)")).then_inc(sem("gs_outer"), 1)

        pe.wait_ge(*at("gs_state_ready", 8))
        for h in range(H_M):
            ins = tr(B[0][0:NB, P * h:P * h + P], qm[:, h, 2 * P:T])
        ins.then_inc(sem("ms_q_ps"), 1)
        pe.wait_ge(*at("ms_q", 1))
        for b in range(NB):
            if b >= 2:
                pe.wait_ge(*at("ms_mul", b - 1))
            mm(B[1 + b % 2][:, :], pick8[0:8, b, :], q_nat8[0:8, :]).then_inc(sem("ms_qb"), 1)
            branch(0, [b])
        pe.wait_ge(*at("gate_evac", 24))
        pe.wait_ge(*at("ms_s", 8))
        for c in range(2):
            ins = tr(B[3][0:32, P * c:P * c + P], ms_T[:, 32 * c:32 * c + 32])
        ins.then_inc(sem("ms_rows"), 1)
        pe.wait_ge(*at("ms_p", 1))
        pe.wait_ge(*at("merged", 8))
        for c in range(2):
            ins = tr(B[4][:, 32 * c:32 * c + 32], ms[0:32, P * c:P * c + P])
        ins.then_inc(sem("ms_pT_ps"), 1)
        pe.wait_ge(*at("ms_pT", 1))
        for b in range(NB):
            i = PC_MV + b // 2
            has_landed(pe, i)
            v = grid(slot(i), 512)
            for c in range(2):
                ins = mm(B[5 + b // 4][32 * (b % 4):32 * (b % 4) + 32, :], ms_pT[:, 32 * c:32 * c + 32],
                         v[:, 2 * (b % 2) + c, :], start=(c == 0), stop=(c == 1))
            ins.then_inc(sem("ms_o_ps"), 1)
        for j in range(2):
            pe.wait_ge(*at("ms_o_evac", j + 1))
            for h in range(H_M):
                ins = tr(B[(0, 7)[j]][:, P * h:P * h + P], ms_pv[:, j, P * h:P * h + P])
            ins.then_inc(sem("ms_oT"), 1)
        pe.wait_ge(*at("ms_done", 1))
        norm_sums(3, ones)

        pe.wait_ge(*at("hn_rt", 21))
        branch(1)
        pe.wait_ge(*at("o_ready", 1))
        branch(2)
        pe.wait_ge(*at("merged", 24))
        for d in range(8):
            i = PC_OUT + d // 2
            has_landed(pe, i)
            w = grid(slot(i), 256)
            if d >= 4:
                pe.wait_ge(*at("x1", d - 3))
            for k in range(KD):
                ins = mm(B[d % 4][:, 0:T], w[:, k, P * (d % 2):P * (d % 2) + P], mT[:, k, :], start=(k == 0), stop=(k == KD - 1))
            ins.then_inc(sem("out_ps"), 1)
        for k in range(KD):
            pe.wait_ge(*at("ln_sq", 3 + k))
            ins = mm(B[4][:, 0:T], ones, G[:, k, :], start=(k == 0), stop=(k == KD - 1))
        ins.then_inc(sem("ln_ss"), 1)
        pe.wait_ge(*at("wrt_landed", 16))
        for k in range(KD):
            pe.wait_ge(*at("h2_ready", k + 1))
            ins = mm(B[5][0:32, 0:T], w_rt[:, k, :], hT[:, k, :], start=(k == 0), stop=(k == KD - 1))
        ins.then_inc(sem("lg_ps"), 1)
        for c, (a, n) in enumerate(TOK):
            for k in range(KD):
                bank = B[(0, 2, 6)[c] + k // 4]
                ins = tr(bank[0:n, P * (k % 4):P * (k % 4) + P], hT[:, k, a:a + n])
                if k % 4 == 3:
                    ins.then_inc(sem("h2_nat_ps"), 1)
            if c == 0:
                pe.wait_ge(*at("lgT", 1))
                for i, (b, m) in enumerate(TOK):
                    ins = tr(B[5][0:m, 32 * i:32 * i + 32], lgT[0:32, b:b + m])
                ins.then_inc(sem("lg_nat"), 1)
        pe.wait_ge(*at("b_landed", 32))
        for f in range(16):
            ins = tr(B[4][:, 32 * f:32 * f + 32], b1_nat[0:32, P * f:P * f + P])
        ins.then_inc(sem("b1_ps"), 1)
        pe.wait_ge(*at("sel", 1))
        for c, (a, n) in enumerate(TOK):
            for i in range(c):
                mm(B[5][0:n, 32 * c:32 * c + 32], ones[:, 0:n], sel_n[:, i, :], start=(i == 0), stop=False)
            ins = mm(B[5][0:n, 32 * c:32 * c + 32], tri_strict[0:n, 0:n], sel_n[0:n, c, :], start=(c == 0), stop=True)
        ins.then_inc(sem("rank"), 1)
        pe.wait_ge(*at("h2_nat", 6))
        for c, (a, n) in enumerate(TOK):
            ins = mm(B[7][:, 0:1], sel4[0:n, c, :, :].rearrange("p r e -> p (r e)"), ones[0:n, 0:1], start=(c == 0), stop=(c == 2))
        ins.then_inc(sem("counts"), 1)
        pe.wait_ge(*at("gate_ready", 1))
        for c, (a, n) in enumerate(TOK):
            ins = tr(B[0][0:32, a:a + n], gate_n[0:n, c, :])
        ins.then_inc(sem("gateT_ps"), 1)

        def gather():
            for k in range(KD):
                for s in range(3):
                    for c, (a, n) in enumerate(TOK):
                        ins = mm(B[6][:, BLK * k:BLK * k + BLK], h2_parts[0:n, s, c, P * k:P * k + P], pick[0:n, c, :],
                                 start=(s == 0 and c == 0), stop=(s == 2 and c == 2))
            ins.then_inc(sem("xg_ps"), 1)

        pe.wait_ge(*at("pick_0", 1))
        for k in range(KD):
            for c, (a, n) in enumerate(TOK):
                ins = mm(B[6][:, BLK * k:BLK * k + BLK], h2_nat[0:n, c, P * k:P * k + P], pick_0[0:n, c, :], start=(c == 0), stop=(c == 2))
        ins.then_inc(sem("xg_ps"), 1)
        pe.wait_ge(*at("more", 1))
        mm(B[7][:, 8:9], tri_strict, more_f)
        mm(B[7][0:1, 12:13], more_f, ones[:, 0:1]).then_inc(sem("more_ps"), 1)
        pe.wait_ge(*at("hot", 1))
        mm(B[7][0:1, 16:32], e_col, item_hot)
        mm(B[7][0:1, 32:48], thr_col, item_hot).then_inc(sem("hot_ps"), 1)
        pe.wait_ge(*at("gateT", 1))
        for d in range(8):
            if d >= 2:
                pe.wait_ge(*at("acc_ready", d - 1))
            mm(B[2 + d % 2][:, 0:T], b2_nat[0:32, P * d:P * d + P], gateT[0:32, :]).then_inc(sem("b2_ps"), 1)
        pe.wait_ge(*at("acc_ready", 8))
        pe.wait_ge(*at("b1_done", 1))
        pe.wait_ge(*at("items_ready", 1))
        n_items = pe.value_load(item_count[0:1, 0:1], min_val=N_EXP, max_val=N_EXP + EXTRA)
        pe.nop().then_inc(sem("put_ps"), 1)
        with pe.Fori(0, n_items) as item:
            pe.wait_ge(*at("xg", item + 1))
            for j in range(4):
                for r in range(2):
                    s = expert_slot(2 * j + r)
                    pe.wait_ge(landed[s], (item + 1) * 16 + landed_pre[s])
                for n in range(4):
                    for r in range(2):
                        k = 2 * j + r
                        ins = mm(B[n][64 * r:64 * r + 64, :], xg[:, k, :], ring[:, expert_slot(k), 512 * n:512 * n + 512],
                                 start=(j == 0), stop=(j == 3))
                    if j == 3 or n == 3:
                        ins.then_inc(sem("mm1"), 1)
            pe.wait_ge(*at("h2_split", 3))
            pe.wait_ge(*at("picks", item + 1))
            pe.wait_ge(*at("part_ready", item * 8))
            gather()
            for n in range(4):
                pe.wait_ge(*at("h_sum", item * 4 + (n + 1)))
                pe.nop().then_inc(sem("turning"), 1)
                for i in range(4):
                    f = 4 * n + i
                    ins = tr(B[f // 8][:, BLK * (f % 8):BLK * (f % 8) + BLK], h_sum[0:BLK, P * f:P * f + P])
                if n % 2:
                    ins.then_inc(sem("hT_ps"), 1)
            pe.wait_ge(*at("y_evac", item * 2))
            pe.wait_ge(*at("put", item))
            pe.wait_ge(*at("xg", item + 2))
            for d in range(KD):
                if d >= 2:
                    pe.wait_ge(*at("part_ready", item * 8 + (d - 1)))
                mm(B[6 + d % 2][:, 0:T], y_e[:, P * d:P * d + P], put).then_inc(sem("scat_ps"), 1)
            pe.wait_ge(*at("part_ready", item * 8 + 8))
            pe.wait_ge(*at("gpicks", item + 1))
            for c, (a, n) in enumerate(TOK):
                ins = tr(B[7][:, a:a + n], gpick[0:n, c, :])
            ins.then_inc(sem("put_ps"), 1)
            pe.wait_ge(*at("act", item + 1))
            for j in range(4):
                s = expert_slot(8 + j)
                pe.wait_ge(landed[s], (item + 1) * 16 + landed_pre[s])
                for n in range(2):
                    for r in range(2):
                        k = 2 * j + r
                        ins = mm(B[4 + n][64 * r:64 * r + 64, :], act_e[:, BLK * k:BLK * k + BLK],
                                 ring[:, s, D * r + 512 * n:D * r + 512 * n + 512], start=(j == 0), stop=(j == 3))
                ins.then_inc(sem("mm2"), 1)
        pe.wait_ge(*at("y_evac", n_items * 2))
        pe.wait_ge(*at("put", n_items))
        for d in range(KD):
            if d >= 2:
                pe.wait_ge(*at("part_ready", n_items * 8 + (d - 1)))
            mm(B[6 + d % 2][:, 0:T], y_e[:, P * d:P * d + P], put).then_inc(sem("scat_ps"), 1)
        pe.wait_ge(*at("acc_last", 1))
        for c, (a, n) in enumerate(TOK):
            for k in range(KD):
                bank = B[2 * c + k // 4]
                ins = tr(bank[0:n, P * (k % 4):P * (k % 4) + P], xT[:, k, a:a + n])
                if k % 4 == 3:
                    ins.then_inc(sem("y_ps"), 1)

    @block.scalar
    def _(act):
        fn = nc.scalar.activation

        def step(ins):
            link(act, "act_step", ins)

        def norm_root(s, scale):
            for i in range(HN[s]):
                act.wait_ge(*at("hn_ss", HN_BASE[s] + i + 1))
                if i == 0 and s:
                    act.wait_ge(*at("hn_done", HN_BASE[s]))
                fn(rt[:, i, :], B[4 + i % 4][:, 0:T], ACT.Ln, bias=eps_col, scale=scale).then_inc(sem("hn_rt"), 1)
            act.wait_ge(*at("hn_rt", HN_BASE[s] + HN[s]))
            fn(rt[:, 0:HN[s], :], rt[:, 0:HN[s], :], ACT.Exp, scale=-0.5).then_inc(sem("hn_inv"), 1)

        act.dma_start(xs_nat[0:NB, :], A["x_sample"].rearrange("b l d -> (b l) d")).then_inc(sem("xs_landed"), 16)
        rows = [(LN1, 8, A["ln1_gain"][0].rearrange("(k p) -> k p", p=P)),
                (LN2, 8, A["ln2_gain"][0].rearrange("(k p) -> k p", p=P)),
                (LNM, 8, A["mem_norm"][0].rearrange("(k p) -> k p", p=P)),
                (C_GDN, 1, A["gdn_norm"]), (C_QM, 1, A["q_norm_mem"]),
                (C_CONV, 48, A["conv_w"][0].rearrange("j (c p) -> (j c) p", p=P))]
        for r, n, src in rows:
            act.dma_start(prm[r:r + n, :], src).then_inc(sem("prm_landed"), 16)
        for half in range(2):
            act.dma_start(prm[C_QS:C_QS + 1, 64 * half:64 * half + 64], A["q_norm_swa"]).then_inc(sem("prm_landed"), 16)
            act.dma_start(prm[C_KS:C_KS + 1, 64 * half:64 * half + 64], A["k_norm_swa"]).then_inc(sem("prm_landed"), 16)
        act.dma_start(cst_nat[0:24, :], A["state_conv"][0].rearrange("b j n -> (b j) n")).then_inc(sem("cst_landed"), 16)
        def gates_out(*chunks):
            for n in chunks:
                act.wait_ge(*at("gate_ps", n + 1))
                fn(gates[:, n, :], B[GATE_BANKS[n]][:, 0:T], ACT.Copy).then_inc(sem("gate_evac"), 1)

        for i in range(8):
            g = 2 * i
            act.wait_ge(*at("x_T", g + 1))
            dst = xT[:, g, :] if g < 8 else memT[:, g - 8, :]
            fn(dst, B[g % 4][:, 0:T if g < 8 else NP_TOK], ACT.Copy).then_inc(sem("tr_evac_act"), 1)
        act.wait_ge(*at("tr_evac_act", 4))
        act.wait_ge(*at("tr_evac_dve", 4))
        fn(G_flat, xT_flat, ACT.Square).then_inc(sem("ln_sq"), 1)
        act.wait_ge(*at("ln_ss", 1))
        act.wait_ge(*at("eps", 1))
        step(fn(rsx, B[4][:, 0:T], ACT.Ln, bias=eps_col, scale=1.0 / D))
        fn(rsx, rsx, ACT.Exp, scale=-0.5).then_inc(sem("ln_rt"), 1)
        act.wait_ge(*at("tr_evac_act", 8))
        act.wait_ge(*at("tr_evac_dve", 8))
        fn(G_flat[:, 0:2048], memT.rearrange("p k n -> p (k n)"), ACT.Square).then_inc(sem("ln_sq"), 1)
        act.wait_ge(*at("ln_ss", 2))
        step(fn(rsm, B[5][:, 0:NP_TOK], ACT.Ln, bias=eps_col, scale=1.0 / D))
        fn(rsm, rsm, ACT.Exp, scale=-0.5).then_inc(sem("ln_rt"), 1)
        act.wait_ge(*at("memTn_ready", 8))
        act.wait_ge(*at("hT_ready", 8))
        for n in range(8):
            i, c = n // 2, n % 2
            act.wait_ge(*at("proj", n + 1))
            dst = (Kn if i < 2 else Vm)[:, c, 256 * (i % 2):256 * (i % 2) + 256]
            fn(dst, B[n % 4][:, 0:256], ACT.Copy).then_inc(sem("proj_evac"), 1)
        act.wait_ge(*at("proj_evac", 8))
        fn(G_flat[:, 0:1024], Kn_flat, ACT.Square).then_inc(sem("kn_sq"), 1)
        act.wait_ge(*at("kn_ss", 1))
        fn(stat[:, 8:16], stat[:, 0:8], ACT.Sqrt, bias=eps_col, scale=1.0 / HD_M).then_inc(sem("kn_rt"), 1)
        for n in range(8, 12):
            act.wait_ge(*at("proj", n + 1))
            fn(qm[:, n - 8, :], B[n % 4][:, 0:T], ACT.Copy).then_inc(sem("proj_evac"), 1)
        act.wait_ge(*at("proj_evac", 12))
        fn(G_flat[:, 0:4 * T], qm_flat, ACT.Square).then_inc(sem("hn_sq"), 1)
        norm_root(0, 1.0 / HD_M)
        act.wait_ge(*at("cin_ready", 1))
        for n in range(12, 34):
            act.wait_ge(*at("proj", n + 1))
            j = n - 12
            if j < 5:
                dst = qsk[:, j, :]
            elif j == 5:
                dst = vsT
            elif j < 18:
                c = j - 6
                fn(cin[:, c, 3:3 + NP_TOK], B[n % 4][:, 0:NP_TOK], ACT.Copy)
                fn(cin[:, c, 3 + NP_TOK:CONV_FLAT].rearrange("p (b j) -> p b j", j=4)[:, :, 3],
                   B[n % 4][:, NP_TOK:T], ACT.Copy).then_inc(sem("proj_evac"), 1)
            else:
                dst = zT[:, j - 18, :]
            if not 6 <= j < 18:
                fn(dst, B[n % 4][:, 0:T], ACT.Copy).then_inc(sem("proj_evac"), 1)
            c = j - 8
            if 0 <= c < 12:
                act.wait_ge(*at("conv_y", c + 1))
                if c >= 2:
                    act.wait_ge(*at("conv_done", c - 1))
                fn(conv_sg[:, c % 2, :], conv_y[:, c % 2, :], ACT.Sigmoid).then_inc(sem("conv_sg"), 1)
        act.wait_ge(*at("ab_ps", 1))
        fn(ab_T[0:8, :], B[4][0:8, 0:T], ACT.Copy).then_inc(sem("ab_T"), 1)
        act.wait_ge(*at("hn_done", 4))
        act.wait_ge(*at("proj_evac", 34))
        fn(G_flat[:, 0:5 * T], qsk_flat, ACT.Square).then_inc(sem("hn_sq"), 1)
        gates_out(0, 1)
        norm_root(1, 1.0 / HD_S)
        act.wait_ge(*at("conv_done", 12))
        act.wait_ge(*at("hn_ss", HN_BASE[2]))
        fn(G_flat, cv_flat[:, 0:KD * T], ACT.Square).then_inc(sem("hn_sq"), 1)
        gates_out(2, 3)
        norm_root(2, 1.0)
        act.wait_ge(*at("hn_ss", HN_BASE[3]))
        fn(G_flat[:, 0:4 * T], zT_flat, ACT.Sigmoid).then_inc(sem("z_sg"), 1)
        act.wait_ge(*at("dc", 1))
        step(fn(gt1, gt1, ACT.Exp))
        step(fn(gt1, gt1, ACT.Ln, bias=1.0))
        step(fn(beta_n, ab_n[:, :, 4:8], ACT.Exp, scale=-1.0))
        fn(alog_b, alog_b, ACT.Exp).then_inc(sem("dc_act"), 1)
        for c in range(2):
            act.wait_ge(*at("kmT_ps", c + 1))
            fn(KmT[:, :, P * c:P * c + P], grid(B[6 + c][:, :], P), ACT.Copy).then_inc(sem("KmT_ready"), 1)
        for c in range(3):
            act.wait_ge(*at("conv_rows_ps", c + 1))
            act.wait_ge(*at("conv_done", 12))
            fn(cso[0:27, 512 * c:512 * c + 512], B[c][0:27, :], ACT.Copy).then_inc(sem("conv_rows_ready"), 1)

        gates_out(4, 5, 6)
        gates_out(7)
        act.wait_ge(*at("mm_m", 1))
        for i in range(8):
            ins = fn(mm_s[:, i, :], mm_s[:, i, :], ACT.Exp, bias=stat[:, 8 + i:9 + i], scale=HD_M ** -0.5,
                     accum_out=stat[:, 16 + i:17 + i])
        ins.then_inc(sem("mm_e"), 1)
        gates_out(8)
        for i in range(8):
            act.wait_ge(*at("mm_pT_ps", i + 1))
            if i >= 2:
                act.wait_ge(*at("mm_o_ps", i - 1))
            fn(mm_pT[:, i % 2, :], B[2 + i % 2][:, 0:2 * P], ACT.Copy).then_inc(sem("mm_pT"), 1)
        gates_out(9, 10)
        act.wait_ge(*at("sw_m", 1))
        for i in range(8):
            fn(sw_s3[:, i, 0:P], sw_s3[:, i, 0:P], ACT.Exp, bias=stat[:, 16 + i:17 + i], accum_out=stat[:, 32 + i:33 + i])
            fn(sw_s3[:, i, P:3 * P], sw_s3[:, i, P:3 * P], ACT.Exp, bias=stat[:, 24 + i:25 + i],
               accum_out=stat[:, 40 + i:41 + i])
        fn(stat[:, 48:64], stat[:, 48:64], ACT.Exp).then_inc(sem("sw_e"), 1)
        gates_out(11, 12)
        for i in range(8):
            act.wait_ge(*at("sw_pT_ps", i + 1))
            if i >= 2:
                act.wait_ge(*at("sw_o_ps", i - 1))
            fn(sw_pT[:, i % 2, :], B[2 + i % 2][:, 0:3 * P], ACT.Copy).then_inc(sem("sw_pT"), 1)
        act.wait_ge(*at("sw_o", 4))
        for j in range(2):
            act.wait_ge(*at("ss_kT_ps", j + 1))
            fn(grid(cols(scr, 512 * j, 512), P), grid(B[j][:, :], P), ACT.Copy).then_inc(sem("ss_kT"), 1)
        act.wait_ge(*at("ss_m", 1))
        fn(ss[0:64, :], ss[0:64, :], ACT.Exp, bias=stat[0:64, 1:2], accum_out=stat[0:64, 2:3])
        fn(stat[0:64, 3:4], stat[0:64, 5:6], ACT.Exp, bias=stat[0:64, 1:2]).then_inc(sem("ss_e"), 1)
        gates_out(13, 14)
        act.wait_ge(*at("gd_small", 1))
        fn(g_sm[:, 16:40], g_sm[:, 16:40], ACT.Exp).then_inc(sem("gd_exp"), 1)
        fn(gt1[0:NB, 2, :], g_n[0:NB, 2, :], ACT.Exp).then_inc(sem("gs_eg"), 1)
        act.wait_ge(*at("gd_row", 2))
        act.wait_ge(*at("ss_done", 1))
        act.wait_ge(*at("gd_min", 1))
        fn(e_row.rearrange("p k n -> p (k n)"), B[2][:, :], ACT.Exp).then_inc(sem("gd_erow"), 1)
        fn(dec_flat, dec_flat, ACT.Exp).then_inc(sem("gd_dec_e"), 1)
        act.wait_ge(*at("memkv_stored", 1))
        act.wait_ge(*at("gd_exp", 1))
        for c in range(2):
            act.wait_ge(*at("gd_kn", c + 1))
            for h in range(H_G):
                ins = fn(k_dec[:, 4 * c + h, :], B[1 + c][:, P * h:P * h + P], ACT.Copy, scale=g_sm[:, 32 + 4 * c + h:33 + 4 * c + h])
            ins.then_inc(sem("gd_kdec"), 1)
        for c in range(2):
            act.wait_ge(*at("gd_vn", c + 1))
            for h in range(H_G):
                ins = fn(v_beta[:, 4 * c + h, :], B[3 + c][:, P * h:P * h + P], ACT.Copy, scale=beta_n[:, c, h:h + 1])
            ins.then_inc(sem("gd_vbeta"), 1)
        for s, (_, _, _, what) in enumerate(INVERSE):
            if what[0] == "copy":
                act.wait_ge(*at("inv_ps", 2 * s + 2))
                fn(inv_flat[what[1]][:, 512:1024], B[(6, 0)[s % 2]][:, :], ACT.Copy).then_inc(sem("inv_act"), 1)
            if s % 4 == 3:
                gates_out(15 + s // 4)
        act.wait_ge(*at("gd_v0", 1))
        act.wait_ge(*at("gd_kdec", 2))
        fn(cols(KmT_flat, 0, 512), B[1][:, :], ACT.Copy).then_inc(sem("gd_v0_evac"), 1)
        act.wait_ge(*at("gd_v1", 1))
        act.wait_ge(*at("gd_s1", 1))
        act.wait_ge(*at("gd_o0", 1))
        fn(cols(KmT_flat, 0, 512), B[1][:, :], ACT.Copy).then_inc(sem("gd_v1_evac"), 1)
        gates_out(20, 21)
        for i in range(2):
            own = gates_flat[:, 8 * i * T:8 * (i + 1) * T]
            act.wait_ge(*at("gate_evac", 8 * i + 8))
            fn(own, own, ACT.Sigmoid).then_inc(sem("gates"), 1)
            gates_out(22 + i)
        act.wait_ge(*at("ms_m", 1))
        fn(ms[0:32, :], ms[0:32, :], ACT.Exp, bias=stat[0:32, 1:2], scale=HD_M ** -0.5,
           accum_out=stat[0:32, 2:3]).then_inc(sem("ms_e"), 1)
        for j in range(2):
            act.wait_ge(*at("ms_o_ps", 4 * j + 4))
            fn(ms_pv[:, j, :], B[5 + j][:, :], ACT.Copy).then_inc(sem("ms_o_evac"), 1)
        act.wait_ge(*at("gate_evac", 24))
        own = gates_flat[:, 16 * T:24 * T]
        fn(own, own, ACT.Sigmoid).then_inc(sem("gates"), 1)
        act.wait_ge(*at("ms_done", 1))
        fn(G_flat[:, 0:4 * T], oT_flat[:, 4 * T:8 * T], ACT.Square).then_inc(sem("hn_sq"), 1)
        norm_root(3, 1.0 / HD_G)
        for k in range(KD):
            act.wait_ge(*at("x1", k + 1))
            fn(G[:, k, :], xT[:, k, :], ACT.Square).then_inc(sem("ln_sq"), 1)
        act.wait_ge(*at("ln_ss", 3))
        step(fn(rr[:, 0:T], B[4][:, 0:T], ACT.Ln, bias=eps_col, scale=1.0 / D))
        fn(rr[:, 0:T], rr[:, 0:T], ACT.Exp, scale=-0.5).then_inc(sem("ln_rt"), 1)
        act.wait_ge(*at("lg_ps", 1))
        fn(lgT[0:32, :], B[5][0:32, 0:T], ACT.Copy).then_inc(sem("lgT"), 1)
        for c, (a, n) in enumerate(TOK):
            for j in range(2):
                act.wait_ge(*at("h2_nat_ps", 2 * c + j + 1))
                ins = fn(h2_nat[0:n, c, 512 * j:512 * j + 512], B[(0, 2, 6)[c] + j][0:n, :], ACT.Copy)
                ins.then_inc(sem("h2_nat"), 1)
            act.wait_ge(*at("h2_nat", 2 * c + 2))
            fn(h2_parts[0:n, 0, c, :], h2_nat[0:n, c, :], ACT.Copy).then_inc(sem("h2_hi"), 1)
            if c == 0:
                act.wait_ge(*at("top", 1))
                fn(top_p, top_p, ACT.Exp).then_inc(sem("top_e"), 1)
        act.wait_ge(*at("b1_ps", 1))
        act.wait_ge(*at("moe_ready", 1))
        fn(b1_e.rearrange("p e f -> p f e"), grid(B[4][:, :], N_EXP), ACT.Copy).then_inc(sem("b1_done"), 1)
        act.wait_ge(*at("gateT_ps", 1))
        fn(gateT[0:32, :], B[0][0:32, 0:T], ACT.Copy).then_inc(sem("gateT"), 1)

        act.wait_ge(*at("xg_ps", 1))
        fn(xg.rearrange("p k n -> p (k n)"), B[6][:, :], ACT.Copy).then_inc(sem("xg"), 1)
        act.wait_ge(*at("items_ready", 1))
        n_items = act.value_load(item_count[0:1, 0:1], min_val=N_EXP, max_val=N_EXP + EXTRA)
        for name in ("part_ready", "put", "y_evac"):
            act.nop().then_inc(sem(name), 1)
        with act.Fori(0, n_items) as item:
            fn(stat[:, 101:102], eps_col, ACT.Sigmoid)
            act.wait_ge(*at("h_sum", item * 4))
            for n in range(4):
                act.wait_ge(*at("mm1", item * 7 + (n + 4)))
                fn(h_odd[0:BLK, 512 * n:512 * n + 512], B[n][64:64 + BLK, :], ACT.Copy).then_inc(sem("h_odd"), 1)
            act.wait_ge(*at("xg_ps", item + 2))
            fn(xg.rearrange("p k n -> p (k n)"), B[6][:, :], ACT.Copy).then_inc(sem("xg"), 1)
            act.wait_ge(*at("acc_done", item))
            for d in range(KD):
                if d == 2:
                    act.wait_ge(*at("glu", item + 1))
                    fn(sg, glu, ACT.Sigmoid, scale=ALPHA).then_inc(sem("sg"), 1)
                act.wait_ge(*at("scat_ps", item * 8 + (d + 1)))
                fn(part[:, d, :], B[6 + d % 2][:, 0:T], ACT.Copy).then_inc(sem("part_ready"), 1)
            act.wait_ge(*at("put_ps", item + 1))
            fn(put, B[7][:, 0:T], ACT.Copy).then_inc(sem("put"), 1)
            act.wait_ge(*at("mm2", item * 4 + 4))
            for n in range(2):
                fn(y_e[:, 512 * n:512 * n + 512], B[4 + n][:, :], ACT.Copy).then_inc(sem("y_evac"), 1)
        act.wait_ge(*at("acc_done", n_items))
        for d in range(KD):
            act.wait_ge(*at("scat_ps", n_items * 8 + (d + 1)))
            fn(part[:, d, :], B[6 + d % 2][:, 0:T], ACT.Copy).then_inc(sem("part_ready"), 1)
        for c, (a, n) in enumerate(TOK):
            act.wait_ge(*at("y_ps", 2 * c + 1))
            fn(y_out[0:n, c, 0:512], B[2 * c][0:n, :], ACT.Copy).then_inc(sem("y_half"), 1)

    @block.vector
    def _(dve):
        v = nc.vector

        def step(ins):
            link(dve, "dve_step", ins)

        def norm_scale(s, dst, gains):
            dve.wait_ge(*at("hn_inv", s + 1))
            for i in range(HN[s]):
                v.scalar_tensor_tensor(dst(i), dst(i), gains(i), rt[:, i, :], ALU.mult, ALU.mult).then_inc(sem("hn_done"), 1)

        def column(i):
            return colp[:, i:i + 1]

        v.memset(eps_col, EPS).then_inc(sem("eps"), 1)
        v.memset(ab_n, 0.0)
        v.memset(stat, 0.0)
        for r in range(4):
            v.memset(thr_col[32 * r:32 * r + 32, :], float(BLK * (r + 1)))
        for i in range(8):
            g = 2 * i + 1
            dve.wait_ge(*at("x_T", g + 1))
            dst = xT[:, g, :] if g < 8 else memT[:, g - 8, :]
            v.tensor_copy(dst, B[g % 4][:, 0:T if g < 8 else NP_TOK]).then_inc(sem("tr_evac_dve"), 1)
        dve.wait_ge(*at("prm_T", 1))
        v.tensor_copy(colp[:, 0:76], B[7][:, 0:76]).then_inc(sem("colp_ready"), 1)
        dve.wait_ge(*at("colp_ready", 1))
        step(v.tensor_scalar(column(C_QS), column(C_QS), HD_S ** -0.5, None, ALU.mult))
        dve.wait_ge(*at("const_ready", 3))
        step(v.scalar_tensor_tensor(e_col, thr_col, -0.5, e_col, ALU.mult, ALU.add))
        step(v.tensor_scalar(e_col, e_col, 32.0, None, ALU.add))
        dve.wait_ge(*at("x_T", 16))
        v.memset(cin[:, :, 0:3], 0.0)
        dve.wait_ge(*at("cst_T", 1))
        for c in range(12):
            dst = cin[:, c, 3 + NP_TOK:CONV_FLAT].rearrange("p (b j) -> p b j", j=4)[:, :, 0:3]
            ins = v.tensor_copy(dst, B[6][:, 24 * c:24 * c + 24].rearrange("p (b j) -> p b j", j=3))
        ins.then_inc(sem("cst_done"), 1)
        dve.wait_ge(*at("cst_done", 1))
        v.tensor_scalar(stat[:, 100:101], eps_col, 0.0, None, ALU.mult).then_inc(sem("cin_ready"), 1)
        dve.wait_ge(*at("ln_rt", 1))
        for k in range(KD):
            v.scalar_tensor_tensor(hT[:, k, :], xT[:, k, :], column(LN1 + k), rsx, ALU.mult, ALU.mult).then_inc(sem("hT_ready"), 1)
        dve.wait_ge(*at("ln_rt", 2))
        for k in range(KD):
            v.scalar_tensor_tensor(memTn[:, k, :], memT[:, k, :], column(LNM + k), rsm, ALU.mult, ALU.mult).then_inc(sem("memTn_ready"), 1)
        dve.wait_ge(*at("rowp_landed", 80))
        dve.wait_ge(*at("kn_sq", 1))
        v.reduce_sum(stat[:, 0:8], grid(G_flat[:, 0:1024], P), AX).then_inc(sem("kn_ss"), 1)
        dve.wait_ge(*at("kn_rt", 1))
        step(v.reciprocal(stat[:, 8:16], stat[:, 8:16]))
        kn8 = grid(Kn_flat, P)
        step(v.tensor_tensor(kn8, kn8, bc(stat[:, 8:16], P), ALU.mult))
        dve.wait_ge(*at("proj_evac", 8))
        v.tensor_tensor(kn8, kn8, mid(knorm_b, 8), ALU.mult).then_inc(sem("memkv_ready"), 1)
        norm_scale(0, lambda i: qm[:, i, :], lambda i: column(C_QM))
        for c in range(13):
            if c < 12:
                dve.wait_ge(*at("proj_evac", 19 + c))
                if c >= 2:
                    dve.wait_ge(*at("conv_done", c - 1))
                y = conv_y[:, c % 2, :]
                step(v.tensor_scalar(y, cin[:, c, 0:288], column(C_CONV + c), None, ALU.mult))
                for j in range(1, 4):
                    ins = v.scalar_tensor_tensor(y, cin[:, c, j:j + 288], column(C_CONV + 12 * j + c), y, ALU.mult, ALU.add)
                    if j < 3:
                        step(ins)
                    else:
                        ins.then_inc(sem("conv_y"), 1)
            if c:
                i = c - 1
                dve.wait_ge(*at("conv_sg", i + 1))
                y, s = conv_y[:, i % 2, :], conv_sg[:, i % 2, :]
                v.tensor_tensor(cv[:, i, 0:NP_TOK], y[:, 0:NP_TOK], s[:, 0:NP_TOK], ALU.mult)
                ys, s_s = (u[:, 256:288].rearrange("p (b j) -> p b j", j=4)[:, :, 3] for u in (y, s))
                v.tensor_tensor(cv[:, i, NP_TOK:T], ys, s_s, ALU.mult).then_inc(sem("conv_done"), 1)
        cs = grid(conv_save, 27)
        v.tensor_copy(cs[:, :, 0:3], cin[:, :, NP_TOK:NP_TOK + 3])
        for c in range(12):
            src = cin[:, c, 3 + NP_TOK:CONV_FLAT].rearrange("p (b j) -> p b j", j=4)[:, :, 1:4]
            ins = v.tensor_copy(cs[:, c, 3:27].rearrange("p (b j) -> p b j", j=3), src)
        ins.then_inc(sem("conv_saved"), 1)
        dve.wait_ge(*at("ab_nT", 1))
        for c, (a, n) in enumerate(TOK):
            ins = v.tensor_copy(ab_n[0:n, c, :], B[5][0:n, 8 * c:8 * c + 8])
        ins.then_inc(sem("ab_done"), 1)
        dve.wait_ge(*at("ab_done", 1))
        step(v.tensor_tensor(gt0, ab_n[:, :, 0:4], mid(dt_b, 3), ALU.add))
        step(v.tensor_scalar(gt1, gt0, -1.0, None, ALU.mult))
        v.tensor_tensor(gt1, gt0, gt1, ALU.min).then_inc(sem("dc"), 1)
        norm_scale(1, lambda i: qsk[:, i, :], lambda i: column(C_QS if i < 4 else C_KS))
        norm_scale(2, lambda i: cv[:, i, :], lambda i: HD_G ** -0.5 if i < 4 else 1.0)
        dve.wait_ge(*at("z_sg", 1))
        step(v.tensor_tensor(zT_flat, zT_flat, G_flat[:, 0:4 * T], ALU.mult))
        dve.wait_ge(*at("dc_act", 1))
        step(v.scalar_tensor_tensor(gt0, gt0, 0.0, gt1, ALU.max, ALU.add))
        step(v.tensor_tensor(gt0, gt0, mid(alog_b, 3), ALU.mult))
        step(v.tensor_scalar(g_n, gt0, -1.0, None, ALU.mult))
        step(v.tensor_scalar(beta_n, beta_n, 1.0, None, ALU.add))
        v.reciprocal(beta_n, beta_n).then_inc(sem("decay_ready"), 1)

        dve.wait_ge(*at("hn_done", HN_BASE[3]))
        for i in range(8):
            dve.wait_ge(*at("mm_s", i + 1))
            v.tensor_copy(mm_s[:, i, :], B[i % 2][:, 0:256]).then_inc(sem("mm_s_evac"), 1)
        dve.wait_ge(*at("mm_s_evac", 8))
        step(v.tensor_reduce(stat[:, 0:8], mm_s, AX, ALU.max))
        v.tensor_scalar(stat[:, 8:16], stat[:, 0:8], -(HD_M ** -0.5), None, ALU.mult).then_inc(sem("mm_m"), 1)
        dve.wait_ge(*at("mm_e", 1))
        step(v.reciprocal(stat[:, 16:24], stat[:, 16:24]))
        v.tensor_tensor(mm_s, mm_s, bc(stat[:, 16:24], NP_TOK), ALU.mult).then_inc(sem("mm_p"), 1)
        dve.wait_ge(*at("conv_stored", 1))
        for h in range(H_M):
            dve.wait_ge(*at("mm_o_ps", 2 * h + 2))
            v.tensor_copy(oT[:, 8 + h, 0:NP_TOK], B[4 + h % 2][:, 0:256]).then_inc(sem("mm_o"), 1)
        dve.wait_ge(*at("mm_o_ps", 8))
        for kv in range(2):
            for half in range(2):
                ins = v.tensor_copy(k_dup[64 * half:64 * half + 64, kv, :], qsk[64 * kv:64 * kv + 64, 4, :])
        ins.then_inc(sem("k_dup"), 1)
        dve.wait_ge(*at("swa_nat", 1))
        v.tensor_copy(kv_nat, B[6][:, 0:3 * P]).then_inc(sem("swa_rows_ready"), 1)
        dve.wait_ge(*at("swa_nat", 2))
        v.tensor_copy(kv_s[0:NB, :], B[7][0:NB, 0:2 * P]).then_inc(sem("swa_rows_ready"), 1)
        for h in range(H_S):
            dve.wait_ge(*at("sw_s", h + 1))
            v.scalar_tensor_tensor(sw_s3[:, h, :], neg_dist, 2.0 ** -(h + 1), B[h % 2][:, 0:3 * P], ALU.mult,
                                   ALU.add).then_inc(sem("sw_s_evac"), 1)
        dve.wait_ge(*at("sw_s_evac", 8))
        v.tensor_reduce(stat[:, 0:8], sw_s3[:, :, 0:P], AX, ALU.max)
        step(v.tensor_reduce(stat[:, 8:16], sw_s3[:, :, P:3 * P], AX, ALU.max))
        two = stat[:, 0:16].rearrange("p (c h) -> p c h", h=8)
        step(v.tensor_tensor(two, two, mid(sink_b, 2), ALU.max))
        v.tensor_scalar(stat[:, 16:32], stat[:, 0:16], -1.0, None, ALU.mult)
        v.tensor_tensor(stat[:, 48:64].rearrange("p (c h) -> p c h", h=8), mid(sink_b, 2), two,
                        ALU.subtract).then_inc(sem("sw_m"), 1)
        dve.wait_ge(*at("sw_e", 1))
        step(v.tensor_tensor(stat[:, 32:48], stat[:, 32:48], stat[:, 48:64], ALU.add))
        step(v.reciprocal(stat[:, 32:48], stat[:, 32:48]))
        v.tensor_tensor(sw_s3[:, :, 0:P], sw_s3[:, :, 0:P], bc(stat[:, 32:40], P), ALU.mult)
        v.tensor_tensor(sw_s3[:, :, P:3 * P], sw_s3[:, :, P:3 * P], bc(stat[:, 40:48], 2 * P),
                        ALU.mult).then_inc(sem("sw_p"), 1)
        for i in range(4):
            dve.wait_ge(*at("sw_o_ps", 2 * i + 2))
            v.tensor_copy(oT[:, i, 0:NP_TOK], B[4 + i % 2][:, 0:256]).then_inc(sem("sw_o"), 1)

        dve.wait_ge(*at("sw_o", 4))
        step(v.memset(q_bd, 0.0))
        for h in range(H_S):
            a, b = 64 * (h // 4), 64 * (h % 2)
            ins = v.tensor_copy(q_bd3[a:a + 64, :, h], qsk[b:b + 64, h // 2, NP_TOK:T])
            v.memset(rows64[0:1, h:64:8], 2.0 ** -(h + 1))
        step(v.tensor_copy(rows64[0:1, 64:128].rearrange("p (b h) -> p b h", h=8), mid(sink_b[0:1, :], 8)))
        v.tensor_tensor(ss_prod3, q_bd3, bc(qsk[:, 4, NP_TOK:T], 8), ALU.mult).then_inc(sem("ss_q"), 1)
        dve.wait_ge(*at("ss_new", 1))
        step(v.tensor_copy(stat[0:64, 4:7], B[3][0:64, 0:3]))
        step(v.tensor_copy(stat[0:64, 7:8], stat[0:64, 5:6]))
        step(v.tensor_copy(stat[0:64, 5:6], stat[0:64, 6:7]))
        dve.wait_ge(*at("ss_s", 1))
        v.tensor_copy(ss_T, B[2][:, 0:64]).then_inc(sem("ss_sT"), 1)
        dve.wait_ge(*at("ss_rows", 1))
        v.tensor_copy(ss[0:64, P:P + 1], stat[0:64, 4:5])
        step(v.scalar_tensor_tensor(ss[0:64, 0:P], neg_dist_s[0:64, :], stat[0:64, 7:8], B[4][0:64, 0:P], ALU.mult, ALU.add))
        step(v.tensor_reduce(stat[0:64, 0:1], ss[0:64, :], AX, ALU.max))
        step(v.tensor_tensor(stat[0:64, 0:1], stat[0:64, 0:1], stat[0:64, 5:6], ALU.max))
        v.tensor_scalar(stat[0:64, 1:2], stat[0:64, 0:1], -1.0, None, ALU.mult).then_inc(sem("ss_m"), 1)
        dve.wait_ge(*at("ss_e", 1))
        step(v.tensor_tensor(stat[0:64, 2:3], stat[0:64, 2:3], stat[0:64, 3:4], ALU.add))
        step(v.reciprocal(stat[0:64, 2:3], stat[0:64, 2:3]))
        step(v.tensor_scalar(ss[0:64, :], ss[0:64, :], stat[0:64, 2:3], None, ALU.mult))
        v.tensor_copy(ss_pb[0:64, :], ss[0:64, P:P + 1].broadcast_to([64, P])).then_inc(sem("ss_p"), 1)
        dve.wait_ge(*at("ss_pT_ps", 1))
        v.tensor_copy(ss_pT, B[5][:, 0:64]).then_inc(sem("ss_pT"), 1)
        step(v.tensor_tensor(ss_o3, grid(B[3][:, 0:64], 8), bc(vsT[:, NP_TOK:T], 8), ALU.mult))
        dve.wait_ge(*at("ss_o_ps", 1))
        step(v.tensor_tensor(ss_o, ss_o, B[2][:, 0:64], ALU.add))
        for h in range(H_S):
            a, b = 64 * (h // 4), 64 * (h % 2)
            ins = v.tensor_copy(oT[b:b + 64, h // 2, NP_TOK:T], ss_o3[a:a + 64, :, h])
        ins.then_inc(sem("ss_done"), 1)

        dve.wait_ge(*at("ss_done", 1))
        dve.wait_ge(*at("gd_cum", 1))
        step(v.tensor_copy(g_sm[:, 0:16], B[0][:, 0:16]))
        v.tensor_copy(g_sm[:, 16:32], g_sm[:, 0:16]).then_inc(sem("gd_cum_evac"), 1)
        v.tensor_tensor(g_sm[:, 32:40], g_sm[:, 8:16], g_sm[:, 0:8], ALU.subtract).then_inc(sem("gd_small"), 1)
        dve.wait_ge(*at("gd_row", 2))
        for m in range(8):
            h = m % 4
            ins = v.tensor_scalar(dec[:, m, :], B[1 + m // 4][:, P * h:P * h + P], g_sm[:, m:m + 1], 0.0, ALU.subtract, ALU.min)
        ins.then_inc(sem("gd_min"), 1)
        dve.wait_ge(*at("gd_erow", 1))
        step(v.tensor_tensor(q_dec, cv[:, 0:4, P:2 * P], e_row, ALU.mult))
        dve.wait_ge(*at("gd_exp", 1))
        step(v.tensor_tensor(g_sm[:, 40:48].rearrange("p (c h) -> p c h", h=4), g_sm[:, 16:24].rearrange("p (c h) -> p c h", h=4),
                             beta_n[:, 0:2, :], ALU.mult))
        step(v.tensor_scalar(g_sm[:, 40:48], g_sm[:, 40:48], -1.0, None, ALU.mult))
        dve.wait_ge(*at("gd_dec_e", 1))
        dve.wait_ge(*at("swa_stored", 1))
        v.tensor_tensor(inv[5], dec, mid(tri_strict, 8), ALU.mult).then_inc(sem("gd_dec"), 1)
        v.tensor_tensor(dec, dec, mid(tri_incl, 8), ALU.mult).then_inc(sem("gd_dec"), 1)
        dve.wait_ge(*at("gd_dec", 2))
        for c in range(2):
            dve.wait_ge(*at("gd_kk", c + 1))
            part_a = inv_flat[0][:, 512 * c:512 * c + 512]
            step(v.tensor_tensor(part_a, B[5 + c][:, :], inv_flat[5][:, 512 * c:512 * c + 512], ALU.mult))
            dve.wait_ge(*at("gd_brow", c + 1))
            v.tensor_tensor(part_a, part_a, B[3 + c][:, :], ALU.mult).then_inc(sem("gd_at"), 1)
        for c in range(2):
            dve.wait_ge(*at("gd_qk", c + 1))
            v.tensor_tensor(intra_flat[:, 512 * c:512 * c + 512], B[7 if c == 0 else 0][:, :],
                            dec_flat[:, 512 * c:512 * c + 512], ALU.mult).then_inc(sem("gd_qk_done"), 1)
        for s, (kind, a, b, what) in enumerate(INVERSE):
            for c in range(1 if what[0] == "copy" else 2):
                dve.wait_ge(*at("inv_ps", 2 * s + c + 1))
                bank = B[(5, 6, 7, 0)[2 * (s % 2) + c]]
                own = slice(512 * c, 512 * c + 512)
                ps = bank[:, :]
                if what[0] == "parts":
                    g4 = slice(4 * c, 4 * c + 4)
                    step(v.tensor_tensor(inv[1][:, g4, :], grid(ps, P), mid(diag16, 4), ALU.mult))
                    step(v.tensor_tensor(inv_flat[2][:, own], ps, inv_flat[1][:, own], ALU.subtract))
                    step(v.tensor_tensor(inv[3][:, g4, :], mid(ident, 4), inv[1][:, g4, :], ALU.subtract))
                    ins = v.tensor_tensor(inv[0][:, g4, :], inv[0][:, g4, :], mid(diag16, 4), ALU.mult)
                elif what[0] == "copy":
                    ins = v.tensor_copy(inv_flat[what[1]][:, own], ps)
                elif what[0] == "add":
                    ins = v.tensor_tensor(inv_flat[what[1]][:, own], inv_flat[what[1]][:, own], ps, ALU.add)
                else:
                    ins = v.tensor_tensor(inv_flat[what[1]][:, own], inv_flat[what[1]][:, own], ps, ALU.subtract)
                ins.then_inc(sem("inv"), 1)
        dve.wait_ge(*at("gd_s1", 1))
        v.tensor_copy(s_one.rearrange("p k n -> p (k n)"), B[2][:, :]).then_inc(sem("gd_s1_evac"), 1)
        dve.wait_ge(*at("gd_o0", 1))
        v.tensor_copy(oT[:, 4:8, 0:P], grid(B[3][:, :], P))
        dve.wait_ge(*at("gd_ks", 1))
        dve.wait_ge(*at("gd_vbeta", 2))
        for h in range(H_G):
            ins = v.scalar_tensor_tensor(r_new[:, h, :], B[4][:, P * h:P * h + P], g_sm[:, 44 + h:45 + h], v_beta[:, 4 + h, :],
                                         ALU.mult, ALU.add)
        ins.then_inc(sem("gd_r"), 1)
        dve.wait_ge(*at("gd_o1", 1))
        step(v.tensor_copy(oT[:, 4:8, P:2 * P], grid(B[5][:, :], P)))
        dve.wait_ge(*at("gd_s2", 1))
        for h in range(H_G):
            ins = v.scalar_tensor_tensor(s_one[:, h, :], s_one[:, h, :], g_sm[:, 28 + h:29 + h], B[2][:, P * h:P * h + P],
                                         ALU.mult, ALU.add)
        ins.then_inc(sem("gdn_state_ready"), 1)

        def by_bh(u):
            return u.rearrange("p h b -> p b h")

        kq4 = gs_kq.rearrange("p (b h) c -> p b h c", h=4)
        ks_, qs_ = cv[:, 4:8, NP_TOK:T], cv[:, 0:4, NP_TOK:T]
        bh = lambda u: u.rearrange("p (b h) -> p b h", h=4)
        dve.wait_ge(*at("gdn_state_ready", 1))
        v.tensor_copy(kq4[:, :, :, 0], by_bh(ks_))
        v.tensor_copy(kq4[:, :, :, 1], by_bh(qs_))
        v.tensor_tensor(bh(gs_qk), by_bh(ks_), by_bh(qs_), ALU.mult)
        dve.wait_ge(*at("gd_v1", 1))
        dg = gs_dg[0:8, :].rearrange("p (s b h) -> p s b h", s=2, h=4)
        v.tensor_tensor(dg[:, 0], bc(ident[0:8, 0:8], 4), mid(beta_n[0:8, 2, :], 8), ALU.mult)
        dve.wait_ge(*at("gs_eg", 1))
        v.tensor_tensor(dg[:, 1], bc(ident[0:8, 0:8], 4), mid(gt1[0:8, 2, :], 8), ALU.mult).then_inc(sem("gs_kq"), 1)
        dve.wait_ge(*at("gs_ps", 1))
        step(v.tensor_copy(gs_bc, B[1][:, 0:96]))
        sq = B[0][:, 0:64].rearrange("p (n c) -> p n c", c=2)
        step(v.tensor_tensor(gs_t, sq[:, :, 0], gs_bc[:, 64:96], ALU.mult))
        step(v.tensor_tensor(bh(gs_t), by_bh(cv[:, 8:12, NP_TOK:T]), bh(gs_t), ALU.subtract))
        step(v.tensor_tensor(gs_vn, gs_t, gs_bc[:, 32:64], ALU.mult))
        step(v.tensor_tensor(gs_bc[:, 0:32], gs_bc[:, 0:32], gs_vn, ALU.mult))
        step(v.tensor_tensor(gs_qk, sq[:, :, 1], gs_bc[:, 64:96], ALU.mult))
        v.tensor_tensor(by_bh(oT[:, 4:8, NP_TOK:T]), bh(gs_qk), bh(gs_bc[:, 0:32]), ALU.add)
        v.tensor_copy(gs_t, gs_kq[:, :, 0]).then_inc(sem("gs_v"), 1)
        for j in range(2):
            i = PC_STATE + j
            has_landed(dve, i)
            v.tensor_tensor(s_out3[:, 16 * j:16 * j + 16, :], grid(slot(i), P), bc(gs_bc[:, 64 + 16 * j:80 + 16 * j], P),
                            ALU.mult).then_inc(sem("state_used"), 1)
        dve.wait_ge(*at("gs_rows", 1))
        step(v.tensor_copy(gs_nat[0:32, :], B[2][0:32, 0:2 * P]))
        for j in range(8):
            if j % 2 == 0:
                if j >= 4:
                    dve.wait_ge(*at("gs_outer", j - 2))
                q = j // 2
                v.tensor_tensor(vn_mask[q % 2][0:32, :, :], mid(gs_nat[0:32, 0:P], 8), bc(ident[0:32, 8 * q:8 * q + 8], P),
                                ALU.mult).then_inc(sem("gs_mask"), 1)
            dve.wait_ge(*at("gs_outer", j + 1))
            dst = s_out[:, 512 * j:512 * j + 512]
            v.tensor_tensor(dst, dst, B[4 + j % 4][:, :], ALU.add).then_inc(sem("gs_state_ready"), 1)

        def merge(j, chunks=range(8)):
            n = BRANCHES[j]
            for d in chunks:
                dve.wait_ge(*at("branch", 8 * j + d + 1))
                ps = B[4 + d % 4][:, 0:T]
                if j == 0:
                    v.tensor_tensor(mT[:, d, :], ps, gates[:, 8 * n + d, :], ALU.mult).then_inc(sem("merged"), 1)
                else:
                    step(v.tensor_tensor(mtmp[:, d % 2, :], ps, gates[:, 8 * n + d, :], ALU.mult))
                    v.tensor_tensor(mT[:, d, :], mT[:, d, :], mtmp[:, d % 2, :], ALU.add).then_inc(sem("merged"), 1)

        dve.wait_ge(*at("gd_s2", 1))
        v.tensor_copy(pick8[0:8, :, :], bc(ident[0:8, 0:8], P))
        dve.wait_ge(*at("ms_q_ps", 1))
        v.tensor_copy(q_nat8[0:8, :], B[0][0:8, :]).then_inc(sem("ms_q"), 1)
        ms_T4 = ms_T.rearrange("p (c b h) -> p c b h", c=2, h=4)
        for b in range(NB):
            i = PC_MK + b // 2
            has_landed(dve, i)
            dve.wait_ge(*at("ms_qb", b + 1))
            kb = grid(slot(i)[:, 1024 * (b % 2):1024 * (b % 2) + 1024], 512)
            v.tensor_tensor(mk_prod.rearrange("p (c h) d -> p c (h d)", c=2), kb, mid(B[1 + b % 2][:, :], 2),
                            ALU.mult).then_inc(sem("ms_mul"), 1)
            dve.wait_ge(*at("ms_mul", b + 1))
            v.reduce_sum(ms_T4[:, :, b, :], mk_prod.rearrange("p (c h) d -> p c h d", c=2), AX).then_inc(sem("ms_s"), 1)
            if b == 0:
                dve.wait_ge(*at("gates", 1))
            merge(0, [b])
            dve.wait_ge(*at("ms_s", b + 1))
        dve.wait_ge(*at("ms_rows", 1))
        step(v.tensor_copy(ms[0:32, :], B[3][0:32, 0:256]))
        step(v.tensor_reduce(stat[0:32, 0:1], ms[0:32, :], AX, ALU.max))
        v.tensor_scalar(stat[0:32, 1:2], stat[0:32, 0:1], -(HD_M ** -0.5), None, ALU.mult).then_inc(sem("ms_m"), 1)
        dve.wait_ge(*at("ms_e", 1))
        step(v.reciprocal(stat[0:32, 2:3], stat[0:32, 2:3]))
        v.tensor_scalar(ms[0:32, :], ms[0:32, :], stat[0:32, 2:3], None, ALU.mult).then_inc(sem("ms_p"), 1)
        dve.wait_ge(*at("ms_pT_ps", 1))
        v.tensor_copy(ms_pT, B[4][:, 0:64]).then_inc(sem("ms_pT"), 1)
        for j in range(2):
            dve.wait_ge(*at("ms_oT", j + 1))
            for h in range(H_M):
                a = P * h + 16 * j + h
                ins = v.tensor_copy(oT[:, 8 + h, NP_TOK + 4 * j:NP_TOK + 4 * j + 4], B[(0, 7)[j]][:, a:a + 109:36])
        ins.then_inc(sem("ms_done"), 1)
        norm_scale(3, lambda i: oT[:, 4 + i, :], lambda i: column(C_GDN))
        dve.wait_ge(*at("hn_done", 21))
        v.tensor_tensor(oT_flat[:, 4 * T:8 * T], oT_flat[:, 4 * T:8 * T], zT_flat, ALU.mult).then_inc(sem("o_ready"), 1)

        dve.wait_ge(*at("gates", 3))
        dve.wait_ge(*at("gdn_stored", 1))
        merge(1)
        merge(2)
        for d in range(8):
            dve.wait_ge(*at("out_ps", d + 1))
            v.tensor_tensor(xT[:, d, :], xT[:, d, :], B[d % 4][:, 0:T], ALU.add).then_inc(sem("x1"), 1)
        dve.wait_ge(*at("ln_rt", 3))
        for k in range(KD):
            v.scalar_tensor_tensor(hT[:, k, :], xT[:, k, :], column(LN2 + k), rr[:, 0:T], ALU.mult, ALU.mult).then_inc(sem("h2_ready"), 1)
        step(v.memset(lg_n, 0.0))
        v.memset(top_flat, 0.0)
        step(v.memset(top_i, 0))
        dve.wait_ge(*at("lg_nat", 1))
        v.tensor_tensor(lg_n[:, 0:2, :], grid(B[5][:, 0:64], 32), mid(brow_b, 2), ALU.add)
        step(v.tensor_tensor(lg_n[0:NB, 2, :], B[5][0:NB, 64:96], brow_b[0:NB, :], ALU.add))
        for c, (a, n) in enumerate(TOK):
            ins = v.max(top_v[0:n, c, :], lg_n[0:n, c, :])
        step(ins)
        for c, (a, n) in enumerate(TOK):
            v.max_index(top_i[0:n, c, :], top_v[0:n, c, :], lg_n[0:n, c, :])
        v.tensor_tensor(top_p, top_v[:, :, 0:4], top_v[:, :, 0:1].broadcast_to([P, 3, 4]), ALU.subtract).then_inc(sem("top"), 1)
        dve.wait_ge(*at("top", 1))
        step(v.tensor_copy(top_f, top_i))
        step(v.tensor_tensor(hot4, iota32.unsqueeze(1).unsqueeze(1).broadcast_to([P, 3, 4, 32]), bc(top_f[:, :, 0:4], 32), ALU.is_equal))
        step(v.tensor_reduce(sel_n, hot4.rearrange("p c k e -> p c e k"), AX, ALU.add))
        v.tensor_copy(sel4, sel_n.unsqueeze(2).broadcast_to([P, 3, 4, 32])).then_inc(sem("sel"), 1)
        dve.wait_ge(*at("top_e", 1))
        dve.wait_ge(*at("moe_ready", 1))
        step(v.tensor_reduce(top_s, top_p, AX, ALU.add))
        step(v.reciprocal(top_s, top_s))
        step(v.tensor_tensor(top_p, top_p, bc(top_s, 4), ALU.mult))
        step(v.tensor_tensor(hot4, hot4, bc(top_p, 32), ALU.mult))
        v.tensor_reduce(gate_n, hot4.rearrange("p c k e -> p c e k"), AX, ALU.add).then_inc(sem("gate_ready"), 1)
        dve.wait_ge(*at("rank", 1))
        v.scalar_tensor_tensor(pos_n[:, 0:2, :], grid(B[5][:, 0:64], 32), 1.0, sel_n[:, 0:2, :], ALU.add, ALU.mult)
        step(v.scalar_tensor_tensor(pos_n[0:NB, 2, :], B[5][0:NB, 64:96], 1.0, sel_n[0:NB, 2, :], ALU.add, ALU.mult))
        v.tensor_scalar(pos_n[:, 0:2, :], pos_n[:, 0:2, :], -1.0, None, ALU.add)
        step(v.tensor_scalar(pos_n[0:NB, 2, :], pos_n[0:NB, 2, :], -1.0, None, ALU.add))

        def build_pick(e, first):
            for c, (a, n) in enumerate(TOK):
                at_e = pos_n[0:n, c, bass.ds(e, 1)]
                ins = v.tensor_scalar(pick[0:n, c, :], places[0:n, bass.ds(first, BLK)], at_e, None, ALU.is_equal)
            ins.then_inc(sem("picks"), 1)

        for c, (a, n) in enumerate(TOK):
            ins = v.tensor_scalar(pick_0[0:n, c, :], places[0:n, 0:BLK], pos_n[0:n, c, 0:1], None, ALU.is_equal)
        ins.then_inc(sem("pick_0"), 1)
        dve.wait_ge(*at("counts", 1))
        v.tensor_tensor(more_f, B[7][:, 0:1], thr_col, ALU.is_gt).then_inc(sem("more"), 1)
        dve.wait_ge(*at("more_ps", 1))
        step(v.tensor_copy(more_pos, B[7][:, 8:9]))
        step(v.tensor_scalar(item_f[0:1, 0:1], B[7][0:1, 12:13], float(N_EXP), None, ALU.add))
        v.tensor_scalar(item_hot, iota32[:, 0:16], more_pos, more_f, ALU.is_equal, ALU.mult).then_inc(sem("hot"), 1)
        v.tensor_copy(item_expert[0:1, 0:N_EXP], iota32[0:1, :])
        v.tensor_copy(item_count[0:1, :], item_f[0:1, :])
        dve.wait_ge(*at("hot_ps", 1))
        v.tensor_copy(item_expert[0:1, N_EXP:N_EXP + EXTRA], B[7][0:1, 16:32])
        step(v.tensor_scalar(item_first[0:1, N_EXP:N_EXP + EXTRA], B[7][0:1, 32:48], 2.0, None, ALU.mult))
        dve.nop().then_inc(sem("items_ready"), 1)
        for d in range(8):
            dve.wait_ge(*at("b2_ps", d + 1))
            v.tensor_tensor(xT[:, d, :], xT[:, d, :], B[2 + d % 2][:, 0:T], ALU.add).then_inc(sem("acc_ready"), 1)

        dve.wait_ge(*at("h2_hi", 3))
        dve.wait_ge(*at("xg_ps", 1))
        for c, (a, n) in enumerate(TOK):
            t0 = h2_nat[0:n, c, :]
            step(v.tensor_tensor(t0, t0, h2_parts[0:n, 0, c, :], ALU.subtract))
            step(v.tensor_copy(h2_parts[0:n, 1, c, :], t0))
            v.tensor_tensor(h2_parts[0:n, 2, c, :], t0, h2_parts[0:n, 1, c, :], ALU.subtract).then_inc(sem("h2_split"), 1)

        dve.wait_ge(*at("b1_done", 1))
        dve.wait_ge(*at("items_ready", 1))
        n_items = dve.value_load(item_count[0:1, 0:1], min_val=N_EXP, max_val=N_EXP + EXTRA)
        dve.nop().then_inc(sem("h_sum"), 1)
        with dve.Fori(0, n_items) as item:
            dve.wait_ge(*at("xg_ps", item + 1))
            build_pick(dve.value_load(item_expert[0:1, bass.ds(item + 1, 1)], min_val=0, max_val=N_EXP - 1),
                       dve.value_load(item_first[0:1, bass.ds(item + 1, 1)], min_val=0, max_val=P * (N_BLK - 1)))
            e = dve.value_load(item_expert[0:1, bass.ds(item, 1)], min_val=0, max_val=N_EXP - 1)
            first = dve.value_load(item_first[0:1, bass.ds(item, 1)], min_val=0, max_val=P * (N_BLK - 1))
            dve.wait_ge(*at("put_ps", item))
            for c, (a, n) in enumerate(TOK):
                ins = v.tensor_scalar(gpick[0:n, c, :], places[0:n, bass.ds(first, P)], pos_n[0:n, c, bass.ds(e, 1)],
                                      gate_n[0:n, c, bass.ds(e, 1)], ALU.is_equal, ALU.mult)
            ins.then_inc(sem("gpicks"), 1)
            for n in range(4):
                dve.wait_ge(*at("h_odd", item * 4 + (n + 1)))
                own = slice(512 * n, 512 * n + 512)
                v.tensor_tensor(h_sum[0:BLK, own], B[n][0:BLK, :], h_odd[0:BLK, own], ALU.add).then_inc(sem("h_sum"), 1)
            b1 = b1_e[:, bass.ds(e, 1), :].rearrange("p i f -> p (i f)")
            dve.wait_ge(*at("hT_ps", item * 2 + 1))
            v.tensor_tensor(grid(glu, BLK), grid(B[0][:, :], BLK), bc(b1[:, 0:8], BLK), ALU.add).then_inc(sem("e_step"), 1)
            dve.wait_ge(*at("e_step", item * 4 + 1))
            v.tensor_scalar(glu, glu, LIMIT, None, ALU.min).then_inc(sem("glu"), 1)
            dve.wait_ge(*at("hT_ps", item * 2 + 2))
            v.tensor_tensor(grid(lin, BLK), grid(B[1][:, :], BLK), bc(b1[:, 8:16], BLK), ALU.add).then_inc(sem("e_step"), 1)
            dve.wait_ge(*at("e_step", item * 4 + 2))
            v.tensor_scalar(lin, lin, LIMIT, -LIMIT, ALU.min, ALU.max).then_inc(sem("e_step"), 1)
            dve.wait_ge(*at("e_step", item * 4 + 3))
            dve.wait_ge(*at("glu", item + 1))
            v.scalar_tensor_tensor(lin, lin, 1.0, glu, ALU.add, ALU.mult).then_inc(sem("e_step"), 1)
            dve.wait_ge(*at("e_step", item * 4 + 4))
            dve.wait_ge(*at("sg", item + 1))
            v.tensor_tensor(act_e, lin, sg, ALU.mult).then_inc(sem("act"), 1)
        for c, (a, n) in enumerate(TOK):
            dve.wait_ge(*at("y_ps", 2 * c + 2))
            dve.wait_ge(*at("y_half", c + 1))
            v.tensor_copy(y_out[0:n, c, 512:1024], B[2 * c + 1][0:n, :]).then_inc(sem("y_ready"), 1)


_INS = ['x_prompt', 'x_sample', 'cache_swa_k', 'cache_swa_v', 'state_gdn', 'state_conv', 'cache_mem_k', 'cache_mem_v',
        'mem_prompt', 'ln1_gain', 'w_in', 'q_norm_swa', 'k_norm_swa', 'swa_sinks', 'conv_w', 'a_log', 'dt_bias',
        'gdn_norm', 'q_norm_mem', 'k_norm_mem', 'mem_norm', 'w_mem_kv', 'w_branch', 'w_out', 'ln2_gain', 'w_router',
        'b_router', 'w_mlp1', 'b_mlp1', 'w_mlp2', 'b_mlp2']
_OUTS = [('y_p', (1, 256, 1024)), ('y_s', (8, 1, 1024)), ('swa_kp', (1, 1, 128, 2, 64)), ('swa_vp', (1, 1, 128, 2, 64)),
         ('swa_ks', (1, 8, 128, 2, 64)), ('swa_vs', (1, 8, 128, 2, 64)), ('gdn_p', (1, 1, 4, 128, 128)),
         ('gdn_s', (1, 8, 4, 128, 128)), ('conv_p', (1, 1, 3, 1536)), ('conv_s', (1, 8, 3, 1536)),
         ('mem_k', (1, 1, 256, 4, 128)), ('mem_v', (1, 1, 256, 4, 128))]


def kernel(**inputs):
    import numpy as _np
    import concourse.bacc as _bacc
    from concourse import mybir as _mybir
    from concourse.bass_utils import run_bass_kernel_spmd as _run

    nc = _bacc.Bacc("TRN2", target_bir_lowering=False, num_devices=1)
    arrays, A, O = {}, {}, {}
    for name in _INS:
        a = _np.ascontiguousarray(inputs[name])
        arrays[f"in_{name}"] = a
        A[name] = nc.dram_tensor(f"in_{name}", a.shape, _mybir.dt.from_np(a.dtype), kind="ExternalInput").ap()
    for name, shape in _OUTS:
        O[name] = nc.dram_tensor(f"out_{name}", shape, _mybir.dt.float32, kind="ExternalOutput").ap()
    build_layer(nc, A, O)
    r = _run(nc, [arrays], core_ids=[0])
    return tuple(r.results[0][f"out_{name}"] for name, _ in _OUTS)
```

```python
from contextlib import ExitStack

import concourse.bass as bass
from concourse import mybir

F32 = mybir.dt.float32
BF16 = mybir.dt.bfloat16
I32 = mybir.dt.int32
U32 = mybir.dt.uint32
ALU = mybir.AluOpType
ACT = mybir.ActivationFunctionType
AX = mybir.AxisListType.X

P = 128
D = 1024
KD = D // P
NP_TOK = 256
NB = 8
T = NP_TOK + NB
EPS = 1e-6
NEG = -1e30
HD_S, H_S, KV_S, WIN = 64, 8, 2, 128
HD_G, H_G = 128, 4
HD_M, H_M, MEM = 128, 4, 256
N_EXP, TOP_K = 32, 4
LIMIT, ALPHA = 7.0, 1.702
SLOTS, SLOT = 12, 2048
PRE_SLOTS = 8
BLK = 64
EXTRA = 16
N_ITEM = N_EXP + EXTRA + 1
N_BLK = -(-T // BLK)
CONV_FLAT = 3 + NP_TOK + 4 * NB
OFF_Z, OFF_AB, OFF_QM, OFF_GATE = 2304, 2816, 2824, 3336
BRANCHES = (0, 1, 2)
TOK = [(0, P), (P, P), (2 * P, NB)]


INVERSE = [
    ("turn", 0, None, ("parts",)),
    ("mult", 0, 1, ("copy", 4)),
    ("turn", 4, None, ("copy", 5)),
    ("mult", 5, 4, ("copy", 0)),
    ("turn", 0, None, ("copy", 1)),
    ("mult", 1, 0, ("copy", 4)),
    ("turn", 4, None, ("copy", 4)),
    ("mult", 5, 3, ("add", 3)),
    ("mult", 1, 3, ("add", 3)),
    ("mult", 4, 3, ("add", 3)),
    ("turn", 3, None, ("copy", 4)),
    ("mult", 4, 2, ("copy", 0)),
    ("turn", 0, None, ("copy", 1)),
    ("mult", 1, 0, ("copy", 2)),
    ("turn", 2, None, ("copy", 4)),
    ("mult", 4, 2, ("copy", 5)),
    ("turn", 5, None, ("copy", 5)),
    ("mult", 5, 3, ("add", 3)),
    ("mult", 4, 3, ("add", 3)),
    ("mult", 1, 3, ("subtract", 3)),
    ("turn", 3, None, ("copy", 3)),
]


INV_COPIES = sum(step[3][0] == "copy" for step in INVERSE)


def inverse_out(s, c):
    copies = sum(step[3][0] == "copy" for step in INVERSE[:s])
    if INVERSE[s][3][0] == "copy":
        return ("inv_act", copies + 1) if c else ("inv", 2 * s - copies + 1)
    return "inv", 2 * s - copies + 1 + c


CHAINS = {
    "pe_load": [("x_T", 16), ("prm_T", 1), ("cst_T", 1)],
    "pe_small": [("ab_ps", 1), ("ab_nT", 1), ("kmT_ps", 2), ("conv_rows_ps", 3)],
    "pe_scores": [("mm_s", 8), ("swa_nat", 2), ("sw_s", 8)],
    "pe_turned": [("mm_pT_ps", 8), ("sw_pT_ps", 8)],
    "pe_outputs": [("mm_o_ps", 8), ("sw_o_ps", 8)],
    "pe_window": [("ss_kT_ps", 2), ("ss_new", 1), ("ss_s", 1), ("ss_rows", 1), ("ss_pT_ps", 1), ("ss_o_ps", 1)],
    "pe_delta": [("gd_cum", 1), ("gd_row", 2), ("gd_brow", 2), ("gd_kk", 2), ("gd_qk", 2), ("gd_kn", 2), ("gd_vn", 2),
                 ("inv_ps", 2 * len(INVERSE)), ("gd_v0", 1), ("gd_s1", 1), ("gd_o0", 1), ("gd_ks", 1), ("gd_v1", 1),
                 ("gd_o1", 1), ("gd_s2", 1), ("gs_ps", 1), ("gs_rows", 1), ("gs_outer", 8)],
    "pe_memory": [("ms_q_ps", 1), ("ms_qb", 8), ("ms_rows", 1), ("ms_pT_ps", 1), ("ms_o_ps", 8), ("ms_oT", 2)],
    "pe_router": [("out_ps", 8), ("b1_ps", 1), ("lg_ps", 1), ("h2_nat_ps", 6), ("rank", 1), ("counts", 1),
                  ("gateT_ps", 1), ("more_ps", 1), ("hot_ps", 1)],
    "act_small": [("tr_evac_act", 4), ("kn_sq", 1), ("kn_rt", 1), ("ab_T", 1), ("z_sg", 1), ("dc_act", 1),
                  ("KmT_ready", 2), ("conv_rows_ready", 3)],
    "act_attend": [("mm_e", 1), ("mm_pT", 8), ("sw_e", 1), ("sw_pT", 8), ("ss_kT", 2), ("ss_e", 1)],
    "act_delta": [("gd_exp", 1), ("gs_eg", 1), ("gd_erow", 1), ("gd_dec_e", 1), ("gd_kdec", 2), ("gd_vbeta", 2),
                  ("inv_act", INV_COPIES), ("gd_v0_evac", 1), ("gd_v1_evac", 1)],
    "act_late": [("ms_e", 1), ("ms_o_evac", 2), ("b1_done", 1), ("lgT", 1), ("top_e", 1), ("gateT", 1)],
    "dve_load": [("eps", 1), ("tr_evac_dve", 12), ("colp_ready", 1), ("cst_done", 1), ("cin_ready", 1),
                 ("hT_ready", 8), ("memTn_ready", 8), ("kn_ss", 1), ("memkv_ready", 1)],
    "dve_small": [("conv_saved", 1), ("ab_done", 1), ("dc", 1), ("decay_ready", 1)],
    "dve_attend": [("mm_s_evac", 8), ("mm_m", 1), ("mm_p", 1), ("mm_o", 4), ("k_dup", 1), ("swa_rows_ready", 2),
                   ("sw_s_evac", 8), ("sw_m", 1), ("sw_p", 1), ("sw_o", 4)],
    "dve_window": [("ss_q", 1), ("ss_sT", 1), ("ss_m", 1), ("ss_p", 1), ("ss_pT", 1), ("ss_done", 1)],
    "dve_delta": [("gd_cum_evac", 1), ("gd_small", 1), ("gd_min", 1), ("gd_dec", 2), ("gd_at", 2), ("gd_qk_done", 2),
                  ("inv", 2 * len(INVERSE) - INV_COPIES), ("gd_s1_evac", 1), ("gd_r", 1), ("gdn_state_ready", 1), ("gs_kq", 1),
                  ("gs_v", 1)],
    "dve_memory": [("ms_q", 1), ("o_ready", 1), ("ms_m", 1), ("ms_p", 1), ("ms_pT", 1), ("ms_done", 1)],
    "dve_router": [("x1", 8), ("h2_ready", 8), ("top", 1), ("sel", 1), ("gate_ready", 1), ("pick_0", 1), ("more", 1), ("hot", 1),
                   ("items_ready", 1)],
}


PRIMED = ("put_ps", "part_ready", "put", "y_evac", "h_sum", "acc_done")


def build_layer(nc, A, O):
    with ExitStack() as ctx:
        build_program(nc, ctx, A, O)


def build_program(nc, ctx, A, O):
    sems, signalled = {}, {}
    where = {name: (chain, i) for chain, steps in CHAINS.items() for i, (name, _) in enumerate(steps)}

    def handle(name):
        if name not in sems:
            sems[name] = ctx.enter_context(nc.semaphore(name))
        return sems[name]

    def sem(name):
        if name not in where:
            return handle(name)
        chain, i = where[name]
        signalled[name] = signalled.get(name, 0) + 1
        for before_it, count in CHAINS[chain][:i]:
            assert signalled.get(before_it, 0) == count, (name, before_it)
        assert signalled[name] <= CHAINS[chain][i][1], name
        return handle(chain)

    def at(name, n):
        if name not in where:
            return handle(name), n + (name in PRIMED)
        chain, i = where[name]
        return handle(chain), sum(count for _, count in CHAINS[chain][:i]) + n

    made = {}

    def link(eng, name, ins):
        made[name] = made.get(name, 0) + 1
        ins.then_inc(sem(name), 1)
        eng.wait_ge(*at(name, made[name]))

    ring = ctx.enter_context(nc.sbuf_tensor("ring", [P, SLOTS, SLOT], F32))
    ARENA = 28600
    arena = ctx.enter_context(nc.sbuf_tensor("arena", [P, ARENA], F32))
    top = [0]

    def take(n):
        top[0] += n
        assert top[0] <= ARENA, top[0]
        return arena[:, top[0] - n:top[0]]

    def cols(region, a, n):
        return region[:, a:a + n]

    def grid(v, n):
        return v.rearrange("p (k n) -> p k n", n=n)

    ident, ones, blk64 = take(P), take(P), take(P)
    tri_incl, tri_strict, diag16 = take(P), take(P), take(P)
    neg_dist = take(3 * P)
    neg_dist_s = take(P)
    slot_iota = take(P)
    iota32 = take(32)
    colp = take(80)
    sink_b, alog_b, dt_b, brow_b = take(8), take(4), take(4), take(32)
    eps_col, thr_col, e_col = take(1), take(1), take(1)
    w_ab = grid(take(64), 8)
    w_rt = grid(take(256), 32)
    ab_T = take(T)
    ab_n = grid(take(24), 8)
    g_n, beta_n, gt0, gt1 = (grid(take(12), 4) for _ in range(4))
    conv_save = take(12 * 27)
    stat = take(160)
    xT_flat, hT_flat = take(KD * T), take(KD * T)
    xT, hT = grid(xT_flat, T), grid(hT_flat, T)
    at_qsk = top[0]
    qsk_flat = take(5 * T)
    vsT = take(T)
    qsk = grid(qsk_flat, T)
    region_q = arena[:, at_qsk:at_qsk + 6 * T]
    at_cv = top[0]
    cv_flat, zT_flat, qm_flat = take(12 * T), take(4 * T), take(4 * T)
    cv, zT, qm = grid(cv_flat, T), grid(zT_flat, T), grid(qm_flat, T)
    int_tmp, prm = cols(zT_flat, 0, 3 * P).bitcast(I32), cols(zT_flat, 3 * P, P)
    region_cv = arena[:, at_cv:at_cv + 20 * T]
    G_flat = take(KD * T)
    G = grid(G_flat, T)
    oT_flat = take(12 * T)
    oT = grid(oT_flat, T)
    at_mem = top[0]
    Kn_flat, Vm_flat, KmT_flat = take(1024), take(1024), take(1024)
    knorm_b = cols(KmT_flat, 0, P)
    region_mem = arena[:, at_mem:at_mem + 3072]
    scr = take(6400)

    x_nat = grid(cols(scr, 0, 2048), D)
    xs_nat = cols(scr, 2048, 1024)
    mem_nat = grid(cols(scr, 3072, 2048), D)
    memT = grid(cols(oT_flat, 0, 2048), NP_TOK)
    memTn = grid(cols(cv_flat, 0, 2048), NP_TOK)
    rsx, rsm = cols(Kn_flat, 0, T), cols(Kn_flat, 512, NP_TOK)
    cst_nat = cols(region_q, 0, 1536)
    cin = grid(cols(scr, 0, 12 * CONV_FLAT), CONV_FLAT)
    conv_y = grid(cols(scr, 3492, 576), 288)
    conv_sg = grid(cols(oT_flat, 2112, 576), 288)
    rt = grid(cols(scr, 4288, KD * T), T)
    cso = cols(oT_flat, 0, 1536)
    Kn, Vm = grid(Kn_flat, 512), grid(Vm_flat, 512)
    KmT = grid(KmT_flat, NP_TOK)

    gates_flat = cols(ring[:, PRE_SLOTS:SLOTS, :].rearrange("p s n -> p (s n)"), 0, 24 * T)
    gates = grid(gates_flat, T)

    B = [ctx.enter_context(nc.psum_tensor(f"bank{i}", [P, 512], F32)) for i in range(8)]

    LN1, LN2, LNM, C_GDN, C_QM, C_QS, C_KS, C_CONV = 0, 8, 16, 24, 25, 26, 27, 28

    w_in, w_mkv, w_br, w_out = A["w_in"][0], A["w_mem_kv"][0], A["w_branch"][0], A["w_out"][0]

    def columns(w, a):
        return [(0, SLOT, 256, w[:, a:a + 256].rearrange("(k p) n -> p k n", p=P))]

    pieces = [columns(w_in, OFF_QM + 256 * i) for i in range(2)]
    PC_MKV = len(pieces)
    pieces += [columns(w_mkv, 256 * i) for i in range(4)]
    PC_IN = len(pieces)
    pieces += [columns(w_in, 256 * i) for i in range(OFF_Z // 256)]
    N_PROJ = len(pieces)
    PC_LATE = {}

    def late_pieces(first, end):
        for i in range(first, end):
            PC_LATE[i] = len(pieces)
            pieces.append(columns(w_in, OFF_Z + 256 * i if i < 2 else OFF_GATE + 256 * (i - 2)))

    late_pieces(0, 8)
    PC_SWA = len(pieces)
    pieces.append([(0, 1024, P, A["cache_swa_k"][0].rearrange("b w k d -> w b (k d)")),
                   (1024, 1024, P, A["cache_swa_v"][0].rearrange("b w k d -> w b (k d)"))])
    late_pieces(8, 12)
    PC_STATE = len(pieces)
    state = A["state_gdn"][0].rearrange("b h k v -> k (b h) v")
    pieces += [[(0, SLOT, HD_G, state[:, 16 * i:16 * i + 16, :])] for i in range(2)]
    late_pieces(12, 14)
    PC_BR = {}

    def branch_pieces(n):
        PC_BR[n] = len(pieces)
        v = w_br[n].rearrange("(c p) d -> p c d", p=P)
        return [[(0, SLOT, 512, v[:, :, 512 * i:512 * i + 512])] for i in range(2)]

    pieces += branch_pieces(BRANCHES[0])
    mk, mv = (A[name][0].rearrange("b (c m) h d -> m (b c) (h d)", m=P) for name in ("cache_mem_k", "cache_mem_v"))
    PC_MK = len(pieces)
    pieces += [[(0, SLOT, 512, mk[:, 4 * i:4 * i + 4, :])] for i in range(4)]
    pieces += branch_pieces(BRANCHES[1])
    PC_MV = len(pieces)
    pieces += [[(0, SLOT, 512, mv[:, 4 * i:4 * i + 4, :])] for i in range(4)]
    pieces += branch_pieces(BRANCHES[2])
    PC_OUT = len(pieces)
    pieces += [columns(w_out, 256 * i) for i in range(4)]
    N_PRE = len(pieces)
    landed_at, landed_pre = [], [0] * SLOTS
    for i, dmas in enumerate(pieces):
        landed_pre[i % PRE_SLOTS] += 16 * len(dmas)
        landed_at.append(landed_pre[i % PRE_SLOTS])
    landed = [sem(f"landed{s}") for s in range(SLOTS)]
    release = {i: ("proj", 2 * i + 2) for i in range(N_PROJ)}
    release.update({PC_LATE[i]: ("late_ps", 2 * i + 2) for i in range(14)})
    release.update({PC_SWA: ("ss_o_ps", 1), PC_STATE: ("state_used", 1), PC_STATE + 1: ("state_used", 2)})
    for i in range(4):
        release[PC_MK + i], release[PC_MV + i] = ("ms_mul", 2 * i + 2), ("ms_o_ps", 2 * i + 2)
        release[PC_OUT + i] = ("out_ps", 2 * i + 2)
    for j, n in enumerate(BRANCHES):
        for i in range(2):
            release[PC_BR[n] + i] = ("branch", 8 * j + 4 * i + 4)

    def slot(i):
        return ring[:, i % PRE_SLOTS, :]

    def has_landed(eng, i):
        eng.wait_ge(landed[i % PRE_SLOTS], landed_at[i])

    def expert_slot(p):
        return (N_PRE + p) % PRE_SLOTS if p < PRE_SLOTS else p

    LATE_BANKS = [2, 3, 0, 1, 3, 4, 5] + [6 + n % 2 for n in range(7, 17)] + [1 + (n + 1) % 2 for n in range(17, 23)] + [7, 3, 3, 3, 3]

    n_store = [0]

    HN = [4, 5, 8, 4]
    HN_BASE = [0, 4, 9, 17]

    block = ctx.enter_context(nc.Block())

    sw_s = cols(scr, 0, H_S * 3 * P)
    sw_s3 = grid(sw_s, 3 * P)
    sw_pT = grid(cols(scr, 3072, 2 * 3 * P), 3 * P)
    k_dup = grid(cols(scr, 3840, 2 * T), T)
    kv_nat = cols(scr, 4368, 3 * P)
    kv_s = cols(scr, 4752, 2 * P)
    mm_s = grid(cols(scr, 0, 8 * NP_TOK), NP_TOK)
    mm_pT = grid(cols(scr, 2048, 2 * NP_TOK), NP_TOK)
    sw_kT = grid(cols(scr, 0, 1024), P)
    q_bd = cols(scr, 1024, 64)
    q_bd3 = q_bd.rearrange("p (b h) -> p b h", h=H_S)
    ss_prod = cols(scr, 1088, 64)
    ss_prod3 = ss_prod.rearrange("p (b h) -> p b h", h=H_S)
    rows64 = cols(scr, 1664, 128)
    ss_T = cols(scr, 1152, 64)
    ss = cols(scr, 1216, P + 1)
    ss_pT = cols(scr, 1408, 64)
    ss_pb = cols(scr, 1472, P)
    ss_o = cols(scr, 1600, 64)
    ss_o3 = ss_o.rearrange("p (b h) -> p b h", h=H_S)
    inv = [grid(cols(scr, 1024 * i, 1024), P) for i in range(6)]
    inv_flat = [cols(scr, 1024 * i, 1024) for i in range(6)]
    dec_flat, intra_flat = cols(G_flat, 0, 1024), cols(G_flat, 1024, 1024)
    dec, intra = grid(dec_flat, P), grid(intra_flat, P)
    k_dec, v_beta = grid(Kn_flat, P), grid(Vm_flat, P)
    v_new = grid(cols(KmT_flat, 0, 512), P)
    s_one = grid(cols(KmT_flat, 512, 512), P)
    q_dec, r_new, e_row = (grid(cols(region_q, 512 * i, 512), P) for i in range(3))
    g_sm = cols(scr, 6144, 64)
    s_out = cols(scr, 0, 4096)
    s_out3 = grid(s_out, P)
    vn_mask = [grid(cols(scr, 4096 + 1024 * i, 1024), P) for i in range(2)]
    gs = cols(scr, 6144, 256)
    gs_kq = gs[:, 0:64].rearrange("p (n c) -> p n c", c=2)
    gs_qk, gs_bc = gs[:, 64:96], gs[:, 96:192]
    gs_vn, gs_t = gs[:, 192:224], gs[:, 224:256]
    gs_nat = cols(region_q, 0, 2 * P)
    gs_dg = cols(region_q, 256, 64)
    pick8 = grid(Kn_flat, P)
    q_nat8 = cols(Vm_flat, 0, 512)
    ms_T = cols(Vm_flat, 512, 64)
    ms = cols(Vm_flat, 576, NP_TOK)
    ms_pT = cols(Vm_flat, 832, 64)
    mk_prod = grid(cols(G_flat, 0, 1024), P)
    ms_pv = grid(cols(G_flat, 1024, 1024), 512)
    mT = grid(cols(cv_flat, 0, KD * T), T)
    mtmp = grid(cols(region_q, 320, 2 * T), T)
    sq3 = cols(region_q, 320, 4 * T)
    h2_nat = grid(cols(oT_flat, 0, 3 * D), D)
    h2_parts = cols(region_cv, 0, 4608).bitcast(BF16).rearrange("p (s c d) -> p s c d", s=3, d=D)
    b1_nat = cols(scr, 0, 2048)
    b2_nat, gateT = cols(G_flat, 0, D), cols(G_flat, D, T)
    rr, lgT = (cols(scr, 3072 + T * i, T) for i in range(2))
    used_scr = [4096]

    def tmp(n):
        used_scr[0] += n
        return cols(scr, used_scr[0] - n, n)

    lg_n, sel_n = grid(tmp(96), 32), grid(tmp(96), 32)
    top_flat = tmp(3 * (8 + 8 + 4 + 1))
    top_v, top_f, top_p = (grid(cols(top_flat, a, n), n // 3) for a, n in ((0, 24), (24, 24), (48, 12)))
    top_s = cols(top_flat, 60, 3)
    top_i = tmp(24).bitcast(U32).rearrange("p (c n) -> p c n", n=8)
    hot4, sel4 = (tmp(384).rearrange("p (c r e) -> p c r e", c=3, r=4) for _ in range(2))
    pick_0 = grid(tmp(3 * BLK), BLK)
    more_f, more_pos, item_hot, item_f = tmp(1), tmp(1), tmp(16), tmp(1)
    used_cols = [0]

    def moe(n):
        used_cols[0] += n
        assert used_cols[0] <= 3072
        return cols(region_mem, used_cols[0] - n, n)

    pos_n, gate_n = grid(moe(96), 32), grid(moe(96), 32)
    b1_e = grid(moe(16 * N_EXP), 16)
    item_list = moe(2 + 2 * N_ITEM)
    item_int = item_list.bitcast(I32)
    item_count, item_expert, item_first = item_int[:, 0:1], item_int[:, 1:1 + N_ITEM], item_int[:, 1 + N_ITEM:1 + 2 * N_ITEM]
    places = moe(P * N_BLK)
    pick = moe(96).bitcast(BF16).rearrange("p (c n) -> p c n", n=BLK)
    gpick = grid(moe(3 * P), P)
    xg = grid(moe(512), BLK)
    put = moe(T)
    h_odd, h_sum = cols(scr, 0, 2048), cols(scr, 2048, 2048)
    glu, lin, sg, act_e = (cols(scr, 4096 + 512 * i, 512) for i in range(4))
    y_e = cols(region_q, 0, 1024)
    part_flat = hT_flat
    part = hT
    y_out = h2_nat

    def bc(v, n):
        return v.unsqueeze(len(v.shape)).broadcast_to([*v.shape, n])

    def mid(v, n):
        return v.unsqueeze(1).broadcast_to([v.shape[0], n, v.shape[1]])

    @block.sync
    def _(sp):
        sp.dma_start(x_nat, A["x_prompt"][0].rearrange("(c p) d -> p c d", p=P)).then_inc(sem("x_landed"), 16)
        sp.dma_start(mem_nat, A["mem_prompt"][0].rearrange("(c p) d -> p c d", p=P)).then_inc(sem("mem_landed"), 16)
        sp.wait_ge(*at("prm_landed", 160))
        sp.wait_ge(*at("cst_landed", 16))
        for i, dmas in enumerate(pieces):
            if i >= PRE_SLOTS:
                sp.wait_ge(*at(*release[i - PRE_SLOTS]))
            for a, n, w, src in dmas:
                sp.dma_start(grid(slot(i)[:, a:a + n], w), src).then_inc(landed[i % PRE_SLOTS], 16)

        w1 = A["w_mlp1"][0].rearrange("e (k p) n -> e k p n", p=P)
        w2 = A["w_mlp2"][0].rearrange("e (j k p) n -> e j p k n", p=P, k=2)

        def load_expert(e, item):
            for p in range(SLOTS):
                s = expert_slot(p)
                if item is None:
                    sp.wait_ge(*at(*(release[N_PRE - PRE_SLOTS + p] if p < PRE_SLOTS else ("merged", 24))))
                elif p < 8:
                    sp.wait_ge(*at("mm1", item * 7 - 7 + (p // 2 + 1 if p < 6 else 7)))
                else:
                    sp.wait_ge(*at("mm2", item * 4 - 4 + (p - 7)))
                if p < 8:
                    src = w1[bass.ds(e, 1), p, :, :].rearrange("e p n -> p (e n)")
                    dst = ring[:, s, :]
                else:
                    src = w2[bass.ds(e, 1), p - 8, :, :, :].rearrange("e p k n -> p (e k) n")
                    dst = grid(ring[:, s, :], D)
                sp.dma_start(dst, src).then_inc(landed[s], 16)

        load_expert(0, None)
        with sp.Fori(1, N_EXP) as e:
            load_expert(e, e)
        sp.wait_ge(*at("items_ready", 1))
        n_items = sp.value_load(item_count[0:1, 0:1], min_val=N_EXP, max_val=N_EXP + EXTRA)
        with sp.If(n_items > N_EXP):
            with sp.Fori(N_EXP, n_items) as item:
                e = sp.value_load(item_expert[0:1, bass.ds(item, 1)], min_val=0, max_val=N_EXP - 1)
                load_expert(e, item)
        y_p = O["y_p"][0].rearrange("(c p) d -> p c d", p=P)
        sp.wait_ge(*at("y_act", 2))
        sp.dma_start(y_p[:, :, 0:512], y_out[:, 0:2, 0:512]).then_inc(sem("y_stored"), 16)
        sp.wait_ge(*at("y_act", 4))
        sp.wait_ge(*at("y_dve", 1))
        sp.dma_start(y_p[:, :, 512:1024], y_out[:, 0:2, 512:1024]).then_inc(sem("y_stored"), 16)
        sp.wait_ge(*at("y_dve", 2))
        sp.dma_start(O["y_s"].rearrange("b l d -> (b l) d"), y_out[0:NB, 2, :]).then_inc(sem("y_stored"), 16)
        sp.wait_ge(*at("y_stored", 48))

    @block.gpsimd
    def _(pool):
        def step(ins):
            link(pool, "pool_step", ins)

        step(pool.memset(arena[:, 0:6 * P], 1.0))
        step(pool.affine_select(out=ident, in_=ident, compare_op=ALU.is_equal, fill=0.0, base=0,
                                pattern=[[-1, P]], channel_multiplier=1))
        pool.nop().then_inc(sem("const_ready"), 1)
        step(pool.affine_select(out=tri_incl, in_=tri_incl, compare_op=ALU.is_ge, fill=0.0, base=0,
                                pattern=[[1, P]], channel_multiplier=-1))
        step(pool.affine_select(out=tri_strict, in_=tri_strict, compare_op=ALU.is_gt, fill=0.0, base=0,
                                pattern=[[1, P]], channel_multiplier=-1))
        d16 = diag16.rearrange("p (a b) -> p a b", b=16)
        step(pool.affine_select(out=d16, in_=d16, compare_op=ALU.is_ge, fill=0.0, base=0,
                                pattern=[[-16, 8], [0, 16]], channel_multiplier=1))
        step(pool.affine_select(out=d16, in_=d16, compare_op=ALU.is_ge, fill=0.0, base=15,
                                pattern=[[16, 8], [0, 16]], channel_multiplier=-1))
        b64 = blk64.rearrange("p (a b) -> p a b", b=64)
        step(pool.affine_select(out=b64, in_=b64, compare_op=ALU.is_ge, fill=0.0, base=0,
                                pattern=[[-64, 2], [0, 64]], channel_multiplier=1))
        pool.affine_select(out=b64, in_=b64, compare_op=ALU.is_ge, fill=0.0, base=63,
                           pattern=[[64, 2], [0, 64]], channel_multiplier=-1).then_inc(sem("const_ready"), 1)

        step(pool.iota(int_tmp[:, 0:P], pattern=[[1, P]], base=0, channel_multiplier=-1))
        step(pool.iota(int_tmp[:, P:3 * P], pattern=[[1, 2 * P]], base=-P, channel_multiplier=-1))
        step(pool.tensor_copy(neg_dist, int_tmp))
        step(pool.affine_select(out=neg_dist[:, 0:P], in_=neg_dist[:, 0:P], compare_op=ALU.is_ge, fill=NEG, base=0,
                                pattern=[[-1, P]], channel_multiplier=1))
        step(pool.affine_select(out=neg_dist[:, P:3 * P], in_=neg_dist[:, P:3 * P], compare_op=ALU.is_ge, fill=NEG,
                                base=P, pattern=[[-1, 2 * P]], channel_multiplier=1))
        step(pool.affine_select(out=neg_dist[:, P:3 * P], in_=neg_dist[:, P:3 * P], compare_op=ALU.is_ge, fill=NEG,
                                base=0, pattern=[[1, 2 * P]], channel_multiplier=-1))
        step(pool.iota(int_tmp[:, 0:P], pattern=[[1, P]], base=-P, channel_multiplier=0))
        step(pool.iota(int_tmp[:, P:2 * P], pattern=[[0, 2], [1, BLK]], base=0, channel_multiplier=0))
        step(pool.iota(int_tmp[:, 2 * P:2 * P + 32], pattern=[[1, 32]], base=0, channel_multiplier=0))
        step(pool.iota(int_tmp[:, 2 * P + 32:2 * P + 33], pattern=[[0, 1]], base=0, channel_multiplier=1))
        step(pool.tensor_copy(neg_dist_s, int_tmp[:, 0:P]))
        step(pool.tensor_copy(slot_iota, int_tmp[:, P:2 * P]))
        step(pool.tensor_copy(iota32, int_tmp[:, 2 * P:2 * P + 32]))
        pool.tensor_copy(e_col, int_tmp[:, 2 * P + 32:2 * P + 33]).then_inc(sem("const_ready"), 1)

        def spread(v, n):
            return v.broadcast_to([P, n])
        pool.dma_start(knorm_b, spread(A["k_norm_mem"], P)).then_inc(sem("rowp_landed"), 16)
        pool.dma_start(sink_b, spread(A["swa_sinks"], 8)).then_inc(sem("rowp_landed"), 16)
        pool.dma_start(alog_b, spread(A["a_log"], 4)).then_inc(sem("rowp_landed"), 16)
        pool.dma_start(dt_b, spread(A["dt_bias"], 4)).then_inc(sem("rowp_landed"), 16)
        pool.dma_start(brow_b, spread(A["b_router"], 32)).then_inc(sem("rowp_landed"), 16)
        pool.dma_start(w_ab, w_in[:, OFF_AB:OFF_AB + 8].rearrange("(k p) n -> p k n", p=P)).then_inc(sem("wab_landed"), 16)
        pool.dma_start(w_rt, A["w_router"][0].rearrange("(k p) n -> p k n", p=P)).then_inc(sem("wrt_landed"), 16)

        def store(dst, src):
            pool.dma_start(dst, src).then_inc(sem("stored"), 16)
            n_store[0] += 1

        store(O["swa_ks"][0, :, 0:WIN - 1].rearrange("b w k d -> b w (k d)"),
              A["cache_swa_k"][0, :, 1:WIN].rearrange("b w k d -> b w (k d)"))
        store(O["swa_vs"][0, :, 0:WIN - 1].rearrange("b w k d -> b w (k d)"),
              A["cache_swa_v"][0, :, 1:WIN].rearrange("b w k d -> b w (k d)"))
        pool.wait_ge(*at("memkv_ready", 1))
        store(O["mem_k"][0, 0].rearrange("(c m) h d -> m c (h d)", m=P), Kn)
        store(O["mem_v"][0, 0].rearrange("(c m) h d -> m c (h d)", m=P), Vm)
        pool.wait_ge(*at("stored", 16 * n_store[0]))
        pool.nop().then_inc(sem("memkv_stored"), 1)
        pool.wait_ge(*at("conv_rows_ready", 3))
        store(O["conv_p"][0, 0], cso[0:3, :])
        store(O["conv_s"][0].rearrange("b j n -> (b j) n"), cso[3:27, :])
        pool.wait_ge(*at("stored", 16 * n_store[0]))
        pool.nop().then_inc(sem("conv_stored"), 1)
        pool.wait_ge(*at("swa_rows_ready", 2))
        store(O["swa_kp"][0, 0].rearrange("w k d -> w (k d)"), kv_nat[:, 2 * P:3 * P])
        store(O["swa_vp"][0, 0].rearrange("w k d -> w (k d)"), kv_nat[:, P:2 * P])
        store(O["swa_ks"][0, :, WIN - 1].rearrange("b k d -> b (k d)"), kv_s[0:NB, 0:P])
        store(O["swa_vs"][0, :, WIN - 1].rearrange("b k d -> b (k d)"), kv_s[0:NB, P:2 * P])
        pool.wait_ge(*at("stored", 16 * n_store[0]))
        pool.nop().then_inc(sem("swa_stored"), 1)
        pool.wait_ge(*at("gdn_state_ready", 1))
        store(O["gdn_p"][0, 0].rearrange("h k v -> k h v"), s_one)
        pool.wait_ge(*at("gs_state_ready", 8))
        for j in range(2):
            store(O["gdn_s"][0].rearrange("b h k v -> k (b h) v")[:, 16 * j:16 * j + 16, :], s_out3[:, 16 * j:16 * j + 16, :])
        pool.wait_ge(*at("stored", 16 * n_store[0]))
        pool.nop().then_inc(sem("gdn_stored"), 1)
        pool.wait_ge(*at("merged", 24))
        pool.dma_start(b1_nat[0:N_EXP, :], A["b_mlp1"][0]).then_inc(sem("b_landed"), 16)
        for r in range(N_BLK):
            pool.tensor_scalar(places[:, P * r:P * r + P], slot_iota, float(BLK * r), None, ALU.add)
        pool.memset(put, 0.0)
        pool.memset(item_list, 0.0)
        pool.memset(y_e, 0.0).then_inc(sem("moe_ready"), 1)
        pool.wait_ge(*at("ln_ss", 3))
        pool.dma_start(b2_nat[0:N_EXP, :], A["b_mlp2"][0]).then_inc(sem("b2_landed"), 16)

        pool.wait_ge(*at("items_ready", 1))
        n_items = pool.value_load(item_count[0:1, 0:1], min_val=N_EXP, max_val=N_EXP + EXTRA)
        pool.nop().then_inc(sem("acc_done"), 1)
        with pool.Fori(0, n_items) as item:
            pool.wait_ge(*at("part_ready", (item + 1) * 8))
            pool.tensor_tensor(xT_flat, xT_flat, part_flat, ALU.add).then_inc(sem("acc_done"), 1)
            pool.wait_ge(*at("acc_done", item + 1))

    @block.tensor
    def _(pe):
        def mm(out, lhsT, rhs, start=True, stop=True):
            return nc.tensor.matmul(out, lhsT, rhs, start=start, stop=stop, skip_group_check=True)

        def tr(out, in_):
            n = in_.shape[0]
            return nc.tensor.transpose(out, in_, ident[0:n, 0:n])

        pe.wait_ge(*at("const_ready", 1))
        pe.wait_ge(*at("x_landed", 16))
        pe.wait_ge(*at("xs_landed", 16))
        for g in range(16):
            k = g % 8
            if g == 8:
                pe.wait_ge(*at("mem_landed", 16))
            if g >= 4:
                if g - 4 >= 8:
                    pe.wait_ge(*at("tr_evac_dve", 4 + g - 11))
                else:
                    pe.wait_ge(*at("tr_evac_dve" if g % 2 else "tr_evac_act", (g - 4) // 2 + 1))
            src = x_nat if g < 8 else mem_nat
            for c in range(2):
                ins = tr(B[g % 4][:, P * c:P * c + P], src[:, c, P * k:P * k + P])
            if g < 8:
                ins = tr(B[g % 4][:, 2 * P:T], xs_nat[0:NB, P * k:P * k + P])
            ins.then_inc(sem("x_T"), 1)
        def layer_sums(i, n, squares):
            pe.wait_ge(*at("ln_sq", i + 1))
            for k in range(KD):
                ins = mm(B[4 + i][:, 0:n], ones, squares[:, n * k:n * k + n], start=(k == 0), stop=(k == KD - 1))
            ins.then_inc(sem("ln_ss"), 1)

        layer_sums(0, T, G_flat)
        pe.wait_ge(*at("prm_landed", 160))
        tr(B[7][:, 0:76], prm[0:76, :]).then_inc(sem("prm_T"), 1)
        pe.wait_ge(*at("cst_landed", 16))
        for c in range(12):
            ins = tr(B[6][:, 24 * c:24 * c + 24], cst_nat[0:24, P * c:P * c + P])
        ins.then_inc(sem("cst_T"), 1)
        layer_sums(1, NP_TOK, cv_flat)

        def project(i, half, n, rhs):
            if half == 0:
                has_landed(pe, i)
            if n >= 4:
                pe.wait_ge(*at("proj_evac", n - 3))
            w = grid(slot(i), 256)
            for k in range(KD):
                if n == 0:
                    pe.wait_ge(*at("hT_ready", k + 1))
                ins = mm(B[n % 4][:, 0:T], w[:, k, P * half:P * half + P], rhs[:, k, :], start=(k == 0), stop=(k == KD - 1))
            ins.then_inc(sem("proj"), 1)

        def late(n, after=None, blocks=range(KD)):
            if blocks[0] == 0:
                has_landed(pe, PC_LATE[n // 2])
                if after is not None:
                    pe.wait_ge(*at("late_out", after + 1))
            w = grid(slot(PC_LATE[n // 2]), 256)
            a = P * (n % 2)
            for k in blocks:
                ins = mm(B[LATE_BANKS[n]][:, 0:T], w[:, k, a:a + P], hT[:, k, :], start=(k == 0), stop=(k == KD - 1))
            if blocks[-1] == KD - 1:
                ins.then_inc(sem("late_ps"), 1)

        def branch(j, chunks=range(8)):
            for d in chunks:
                i = PC_BR[BRANCHES[j]] + d // 4
                has_landed(pe, i)
                w = grid(slot(i), 512)
                m = 8 * j + d
                if m >= 4:
                    pe.wait_ge(*at("merged", m - 3))
                for c in range(4):
                    ins = mm(B[4 + m % 4][:, 0:T], w[:, c, P * (d % 4):P * (d % 4) + P], oT[:, 4 * BRANCHES[j] + c, :],
                             start=(c == 0), stop=(c == 3))
                ins.then_inc(sem("branch"), 1)

        def norm_sums(s, lhsT, squares=G_flat):
            pe.wait_ge(*at("hn_sq", s + 1))
            for i in range(HN[s]):
                if i >= 4 or s:
                    pe.wait_ge(*at("hn_rt", max(HN_BASE[s], HN_BASE[s] + i - 3) if i >= 4 else HN_BASE[s]))
                mm(B[4 + i % 4][:, 0:T], lhsT, squares[:, T * i:T * i + T]).then_inc(sem("hn_ss"), 1)

        for n in range(4):
            project(n // 2, n % 2, n, hT)
        pe.wait_ge(*at("memTn_ready", 8))
        for n in range(4, 12):
            i, c = n // 2, n % 2
            has_landed(pe, i)
            pe.wait_ge(*at("proj_evac", n - 3))
            w = grid(slot(i), 256)
            for k in range(KD):
                ins = mm(B[n % 4][:, 0:256], memTn[:, k, P * c:P * c + P], w[:, k, :], start=(k == 0), stop=(k == KD - 1))
            ins.then_inc(sem("proj"), 1)
        pe.wait_ge(*at("const_ready", 3))
        pe.wait_ge(*at("cst_done", 1))
        pe.wait_ge(*at("colp_ready", 1))
        norm_sums(0, ones)
        for n in range(12, 30):
            project(PC_IN + (n - 12) // 2, n % 2, n, hT)
        pe.wait_ge(*at("wab_landed", 16))
        pe.wait_ge(*at("hn_rt", 4))
        for k in range(KD):
            ins = mm(B[4][0:8, 0:T], w_ab[:, k, :], hT[:, k, :], start=(k == 0), stop=(k == KD - 1))
        ins.then_inc(sem("ab_ps"), 1)
        pe.wait_ge(*at("proj_evac", 28))
        late(0)
        late(1)
        pe.wait_ge(*at("ab_T", 1))
        for c, (a, n) in enumerate(TOK):
            ins = tr(B[5][0:n, 8 * c:8 * c + 8], ab_T[0:8, a:a + n])
        ins.then_inc(sem("ab_nT"), 1)
        pe.wait_ge(*at("ab_done", 1))
        norm_sums(1, blk64)
        pe.wait_ge(*at("proj_evac", 30))
        late(2)
        late(3)
        norm_sums(2, ones)
        pe.wait_ge(*at("memkv_ready", 1))
        pe.wait_ge(*at("hn_rt", HN_BASE[3]))
        for c in range(2):
            for h in range(H_M):
                ins = tr(B[6 + c][:, P * h:P * h + P], Kn[:, c, P * h:P * h + P])
            ins.then_inc(sem("kmT_ps"), 1)
        pe.wait_ge(*at("conv_saved", 1))
        pe.wait_ge(*at("late_out", 4))
        cs = grid(conv_save, 27)
        for c in range(12):
            ins = tr(B[c // 4][0:27, P * (c % 4):P * (c % 4) + P], cs[:, c, :])
            if c % 4 == 3:
                ins.then_inc(sem("conv_rows_ps"), 1)

        late(4)
        late(5)
        late(6)

        def attend(tag, n, between, scores, values, part_n):
            if tag == "mm":
                pe.wait_ge(*at("late_out", 7))
            for i in range(n):
                if i >= 2:
                    pe.wait_ge(*at(tag + "_s_evac", i - 1))
                scores(i, B[i % 2]).then_inc(sem(tag + "_s"), 1)
            for i in between:
                late(i, after=i - 2 if i > between[1] else None)
            for i in range(n):
                pe.wait_ge(*at(tag + "_p", 1))
                if i >= 2:
                    pe.wait_ge(*at(tag + "_pT", i - 1))
                part_n(i, B[2 + i % 2]).then_inc(sem(tag + "_pT_ps"), 1)
                if i:
                    values(i - 1)
            values(n - 1)

        pe.wait_ge(*at("hn_done", HN_BASE[3]))
        pe.wait_ge(*at("KmT_ready", 2))
        pe.wait_ge(*at("conv_rows_ready", 3))

        def mm_scores(i, bank):
            h, q = i // 2, i % 2
            return mm(bank[:, 0:256], qm[:, h, P * q:P * q + P], KmT[:, h, :])

        def mm_turn(i, bank):
            tr(bank[:, 0:P], mm_s[:, i, 0:P])
            return tr(bank[:, P:2 * P], mm_s[:, i, P:2 * P])

        def mm_values(i):
            h, q = i // 2, i % 2
            pe.wait_ge(*at("mm_pT", i + 1))
            if q == 0 and h >= 2:
                pe.wait_ge(*at("mm_o", h - 1))
            for c in range(2):
                ins = mm(B[4 + h % 2][:, P * q:P * q + P], Vm[:, c, P * h:P * h + P], mm_pT[:, i % 2, P * c:P * c + P],
                         start=(c == 0), stop=(c == 1))
            ins.then_inc(sem("mm_o_ps"), 1)

        attend("mm", 8, (7, 8, 9), mm_scores, mm_values, mm_turn)

        pe.wait_ge(*at("late_out", 10))
        pe.wait_ge(*at("mm_o", 4))
        for j in range(2):
            tr(B[6][:, P * j:P * j + P], vsT[:, P * j:P * j + P])
        tr(B[6][:, 2 * P:3 * P], qsk[:, 4, P:2 * P]).then_inc(sem("swa_nat"), 1)
        tr(B[7][0:NB, 0:P], qsk[:, 4, 2 * P:T])
        tr(B[7][0:NB, P:2 * P], vsT[:, 2 * P:T]).then_inc(sem("swa_nat"), 1)
        pe.wait_ge(*at("k_dup", 1))
        pe.wait_ge(*at("swa_rows_ready", 2))

        def sw_scores(i, bank):
            r = HD_S * (i % 2)
            q, k = qsk[r:r + HD_S, i // 2, :], k_dup[r:r + HD_S, i // 4, :]
            mm(bank[:, 0:P], q[:, 0:P], k[:, 0:P])
            return mm(bank[:, P:3 * P], q[:, P:2 * P], k[:, 0:2 * P])

        def sw_turn(i, bank):
            for c in range(3):
                ins = tr(bank[:, P * c:P * c + P], sw_s3[:, i, P * c:P * c + P])
            return ins

        def sw_values(i):
            r, v = HD_S * (i % 2), HD_S * (i // 4)
            pe.wait_ge(*at("sw_pT", i + 1))
            if i % 2 == 0 and i >= 4:
                pe.wait_ge(*at("sw_o", i // 2 - 1))
            out = B[4 + (i // 2) % 2][r:r + HD_S, :]
            mm(out[:, 0:P], kv_nat[:, v:v + HD_S], sw_pT[:, i % 2, 0:P])
            mm(out[:, P:2 * P], kv_nat[:, v:v + HD_S], sw_pT[:, i % 2, P:2 * P], stop=False)
            mm(out[:, P:2 * P], kv_nat[:, P + v:P + v + HD_S], sw_pT[:, i % 2, 2 * P:3 * P],
               start=False).then_inc(sem("sw_o_ps"), 1)

        attend("sw", 8, (10, 11, 12, 13, 14), sw_scores, sw_values, sw_turn)

        pe.wait_ge(*at("sw_o", 4))
        has_landed(pe, PC_SWA)
        kc, vc = grid(slot(PC_SWA)[:, 0:1024], P), grid(slot(PC_SWA)[:, 1024:2048], P)
        for b in range(NB):
            ins = tr(B[b // 4][:, P * (b % 4):P * (b % 4) + P], kc[:, b, :])
            if b % 4 == 3:
                ins.then_inc(sem("ss_kT_ps"), 1)
        pe.wait_ge(*at("ss_q", 1))
        mm(B[3][0:64, 0:1], ss_prod, ones[:, 0:1])
        mm(B[3][0:64, 1:2], rows64[0:1, 0:64], ones[0:1, 0:1])
        mm(B[3][0:64, 2:3], rows64[0:1, 64:128], ones[0:1, 0:1]).then_inc(sem("ss_new"), 1)
        for b in range(NB):
            pe.wait_ge(*at("ss_kT", b // 4 + 1))
            ins = mm(B[2][:, 8 * b:8 * b + 8], sw_kT[:, b, :], q_bd[:, 8 * b:8 * b + 8])
        ins.then_inc(sem("ss_s"), 1)
        pe.wait_ge(*at("ss_sT", 1))
        tr(B[4][0:64, 0:P], ss_T).then_inc(sem("ss_rows"), 1)
        late(15, after=13)
        pe.wait_ge(*at("ss_p", 1))
        mm(B[3][:, 0:64], ss_pb[0:64, :], ident[0:64, 0:64])
        tr(B[5][:, 0:64], ss[0:64, 0:P]).then_inc(sem("ss_pT_ps"), 1)
        pe.wait_ge(*at("ss_pT", 1))
        for b in range(NB):
            ins = mm(B[2][:, 8 * b:8 * b + 8], vc[:, b, :], ss_pT[:, 8 * b:8 * b + 8])
        ins.then_inc(sem("ss_o_ps"), 1)

        late(16, after=14)
        pe.wait_ge(*at("ss_done", 1))
        pe.wait_ge(*at("decay_ready", 1))
        for c in range(2):
            mm(B[0][:, 4 * c:4 * c + 4], tri_incl, g_n[:, c, :])
            ins = mm(B[0][:, 8 + 4 * c:12 + 4 * c], ones, g_n[:, c, :])
        ins.then_inc(sem("gd_cum"), 1)
        for c in range(2):
            for h in range(H_G):
                ins = mm(B[1 + c][:, P * h:P * h + P], g_n[:, c, h:h + 1].broadcast_to([P, P]), tri_incl)
            ins.then_inc(sem("gd_row"), 1)
        for c in range(2):
            for h in range(H_G):
                ins = mm(B[3 + c][:, P * h:P * h + P], beta_n[:, c, h:h + 1].broadcast_to([P, P]), ident)
            ins.then_inc(sem("gd_brow"), 1)
        pe.wait_ge(*at("late_out", 17))
        for c in range(2):
            for h in range(H_G):
                k = cv[:, 4 + h, P * c:P * c + P]
                ins = mm(B[5 + c][:, P * h:P * h + P], k, k)
            ins.then_inc(sem("gd_kk"), 1)
        for c in range(2):
            if c:
                pe.wait_ge(*at("gd_cum_evac", 1))
            for h in range(H_G):
                ins = mm(B[7 if c == 0 else 0][:, P * h:P * h + P], cv[:, 4 + h, P * c:P * c + P], cv[:, h, P * c:P * c + P])
            ins.then_inc(sem("gd_qk"), 1)
        pe.wait_ge(*at("gd_dec", 2))
        for c in range(2):
            for h in range(H_G):
                ins = tr(B[1 + c][:, P * h:P * h + P], cv[:, 4 + h, P * c:P * c + P])
            ins.then_inc(sem("gd_kn"), 1)
        pe.wait_ge(*at("gd_at", 2))
        for c in range(2):
            for h in range(H_G):
                ins = tr(B[3 + c][:, P * h:P * h + P], cv[:, 8 + h, P * c:P * c + P])
            ins.then_inc(sem("gd_vn"), 1)

        pe.wait_ge(*at("gd_qk_done", 2))
        for s, (kind, a, b, _) in enumerate(INVERSE):
            for c in range(2):
                if s:
                    pe.wait_ge(*at(*inverse_out(s - 1, c)))
                bank = B[(5, 6, 7, 0)[2 * (s % 2) + c]]
                for h in range(H_G):
                    m = 4 * c + h
                    out = bank[:, P * h:P * h + P]
                    ins = tr(out, inv[a][:, m, :]) if kind == "turn" else mm(out, inv[a][:, m, :], inv[b][:, m, :])
                ins.then_inc(sem("inv_ps"), 1)
            if s == 0:
                pe.wait_ge(*at("gd_kdec", 2))
                late(17)
            else:
                n, q = 18 + (s - 1) // 4, (s - 1) % 4
                late(n, after=n - 2 if n > 18 else None, blocks=range(2 * q, 2 * q + 2))
        for c in range(2):
            pe.wait_ge(*at(*inverse_out(len(INVERSE) - 1, c)))
        pe.wait_ge(*at("gd_vbeta", 2))

        def per_head(bank, left, right, name, **kw):
            for h in range(H_G):
                ins = mm(bank[:, P * h:P * h + P], left(h), right(h), **kw)
            if name:
                ins.then_inc(sem(name), 1)

        pe.wait_ge(*at("late_out", 23))
        T_inv = inv[3]
        per_head(B[1], lambda h: T_inv[:, h, :], lambda h: v_beta[:, h, :], "gd_v0")
        late(23, blocks=range(0, 2))
        pe.wait_ge(*at("gd_v0_evac", 1))
        per_head(B[2], lambda h: k_dec[:, h, :], lambda h: v_new[:, h, :], "gd_s1")
        per_head(B[3], lambda h: v_new[:, h, :], lambda h: intra[:, h, :], "gd_o0")
        late(23, blocks=range(2, 4))
        pe.wait_ge(*at("gd_s1_evac", 1))
        per_head(B[4], lambda h: cv[:, 4 + h, P:2 * P], lambda h: s_one[:, h, :], "gd_ks")
        late(23, blocks=range(4, 6))
        pe.wait_ge(*at("gd_r", 1))
        per_head(B[1], lambda h: T_inv[:, 4 + h, :], lambda h: r_new[:, h, :], "gd_v1")
        late(23, blocks=range(6, 8))
        pe.wait_ge(*at("gd_v1_evac", 1))
        for h in range(H_G):
            mm(B[5][:, P * h:P * h + P], s_one[:, h, :], q_dec[:, h, :], stop=False)
            ins = mm(B[5][:, P * h:P * h + P], v_new[:, h, :], intra[:, 4 + h, :], start=False)
        ins.then_inc(sem("gd_o1"), 1)
        per_head(B[2], lambda h: k_dec[:, 4 + h, :], lambda h: v_new[:, h, :], "gd_s2")

        pe.wait_ge(*at("gdn_state_ready", 1))
        pe.wait_ge(*at("gs_kq", 1))
        for i in range(32):
            if i % 16 == 0:
                has_landed(pe, PC_STATE + i // 16)
            ins = mm(B[0][:, 2 * i:2 * i + 2], slot(PC_STATE + i // 16)[:, P * (i % 16):P * (i % 16) + P], gs_kq[:, i, :])
        mm(B[1][:, 0:32], ones, gs_qk)
        mm(B[1][:, 32:96], ones[0:8, :], gs_dg[0:8, :]).then_inc(sem("gs_ps"), 1)
        late(24)
        pe.wait_ge(*at("gs_v", 1))
        tr(B[2][0:32, 0:P], gs_vn)
        tr(B[2][0:32, P:2 * P], gs_t).then_inc(sem("gs_rows"), 1)
        late(25, after=24)
        for j in range(8):
            if j in (2, 4):
                late(25 + j // 2, after=24 + j // 2)
            pe.wait_ge(*at("gs_mask", j // 2 + 1))
            if j >= 4:
                pe.wait_ge(*at("gs_state_ready", j - 3))
            elif j == 3:
                pe.wait_ge(*at("late_out", 24))
            mm(B[4 + j % 4][:, :], gs_nat[0:32, P:2 * P],
               vn_mask[(j // 2) % 2][0:32, 4 * (j % 2):4 * (j % 2) + 4, :].rearrange("p a b -> p (a b)")).then_inc(sem("gs_outer"), 1)

        pe.wait_ge(*at("gs_state_ready", 8))
        for h in range(H_M):
            ins = tr(B[0][0:NB, P * h:P * h + P], qm[:, h, 2 * P:T])
        ins.then_inc(sem("ms_q_ps"), 1)
        norm_sums(3, ones, sq3)
        pe.wait_ge(*at("hn_rt", 21))
        pe.wait_ge(*at("ms_q", 1))
        for b in range(NB):
            if b >= 2:
                pe.wait_ge(*at("ms_mul", b - 1))
            mm(B[1 + b % 2][:, :], pick8[0:8, b, :], q_nat8[0:8, :]).then_inc(sem("ms_qb"), 1)
            branch(0, [b])
        pe.wait_ge(*at("o_ready", 1))
        branch(1, [0, 1])
        pe.wait_ge(*at("late_out", 28))
        pe.wait_ge(*at("ms_s", 8))
        for c in range(2):
            ins = tr(B[0][0:32, P * c:P * c + P], ms_T[:, 32 * c:32 * c + 32])
        ins.then_inc(sem("ms_rows"), 1)
        branch(1, [2, 3])
        pe.wait_ge(*at("ms_p", 1))
        for c in range(2):
            ins = tr(B[1][:, 32 * c:32 * c + 32], ms[0:32, P * c:P * c + P])
        ins.then_inc(sem("ms_pT_ps"), 1)
        branch(1, [4])
        pe.wait_ge(*at("ms_pT", 1))
        for b in range(NB):
            i = PC_MV + b // 2
            has_landed(pe, i)
            v = grid(slot(i), 512)
            for c in range(2):
                ins = mm(B[2 + b // 4][32 * (b % 4):32 * (b % 4) + 32, :], ms_pT[:, 32 * c:32 * c + 32],
                         v[:, 2 * (b % 2) + c, :], start=(c == 0), stop=(c == 1))
            ins.then_inc(sem("ms_o_ps"), 1)
        branch(1, [5])
        for j in range(2):
            pe.wait_ge(*at("ms_o_evac", j + 1))
            for h in range(H_M):
                ins = tr(B[j][:, P * h:P * h + P], ms_pv[:, j, P * h:P * h + P])
            ins.then_inc(sem("ms_oT"), 1)
        branch(1, [6, 7])
        pe.wait_ge(*at("ms_done", 1))
        branch(2)
        pe.wait_ge(*at("merged", 24))
        for d in range(8):
            i = PC_OUT + d // 2
            has_landed(pe, i)
            w = grid(slot(i), 256)
            if d >= 4:
                pe.wait_ge(*at("x1", d - 3))
            for k in range(KD):
                ins = mm(B[d % 4][:, 0:T], w[:, k, P * (d % 2):P * (d % 2) + P], mT[:, k, :], start=(k == 0), stop=(k == KD - 1))
            ins.then_inc(sem("out_ps"), 1)
        for k in range(KD):
            pe.wait_ge(*at("ln_sq", 3 + k))
            ins = mm(B[4][:, 0:T], ones, G[:, k, :], start=(k == 0), stop=(k == KD - 1))
        ins.then_inc(sem("ln_ss"), 1)
        pe.wait_ge(*at("b_landed", 16))
        for f in range(16):
            ins = tr(B[7][:, 32 * f:32 * f + 32], b1_nat[0:32, P * f:P * f + P])
        ins.then_inc(sem("b1_ps"), 1)
        pe.wait_ge(*at("wrt_landed", 16))
        for k in range(KD):
            pe.wait_ge(*at("h2_ready", k + 1))
            ins = mm(B[5][0:32, 0:T], w_rt[:, k, :], hT[:, k, :], start=(k == 0), stop=(k == KD - 1))
        ins.then_inc(sem("lg_ps"), 1)
        for c, (a, n) in enumerate(TOK):
            if c == 2:
                pe.wait_ge(*at("b1_done", 1))
            for k in range(KD):
                bank = B[(0, 2, 6)[c] + k // 4]
                ins = tr(bank[0:n, P * (k % 4):P * (k % 4) + P], hT[:, k, a:a + n])
                if k % 4 == 3:
                    ins.then_inc(sem("h2_nat_ps"), 1)
            if c == 0:
                pe.wait_ge(*at("lgT", 1))
                for i, (b, m) in enumerate(TOK):
                    ins = tr(B[5][0:m, 32 * i:32 * i + 32], lgT[0:32, b:b + m])
                ins.then_inc(sem("lg_nat"), 1)
        pe.wait_ge(*at("sel", 1))
        for c, (a, n) in enumerate(TOK):
            for i in range(c):
                mm(B[5][0:n, 32 * c:32 * c + 32], ones[:, 0:n], sel_n[:, i, :], start=(i == 0), stop=False)
            ins = mm(B[5][0:n, 32 * c:32 * c + 32], tri_strict[0:n, 0:n], sel_n[0:n, c, :], start=(c == 0), stop=True)
        ins.then_inc(sem("rank"), 1)
        pe.wait_ge(*at("h2_nat", 6))
        for c, (a, n) in enumerate(TOK):
            ins = mm(B[7][:, 0:1], sel4[0:n, c, :, :].rearrange("p r e -> p (r e)"), ones[0:n, 0:1], start=(c == 0), stop=(c == 2))
        ins.then_inc(sem("counts"), 1)
        pe.wait_ge(*at("gate_ready", 1))
        for c, (a, n) in enumerate(TOK):
            ins = tr(B[0][0:32, a:a + n], gate_n[0:n, c, :])
        ins.then_inc(sem("gateT_ps"), 1)

        def gather():
            for k in range(KD):
                for s in range(3):
                    for c, (a, n) in enumerate(TOK):
                        ins = mm(B[6][:, BLK * k:BLK * k + BLK], h2_parts[0:n, s, c, P * k:P * k + P], pick[0:n, c, :],
                                 start=(s == 0 and c == 0), stop=(s == 2 and c == 2))
            ins.then_inc(sem("xg_ps"), 1)

        pe.wait_ge(*at("pick_0", 1))
        for k in range(KD):
            for c, (a, n) in enumerate(TOK):
                ins = mm(B[6][:, BLK * k:BLK * k + BLK], h2_nat[0:n, c, P * k:P * k + P], pick_0[0:n, c, :], start=(c == 0), stop=(c == 2))
            if k == 1:
                pe.wait_ge(*at("more", 1))
                mm(B[7][:, 8:9], tri_strict, more_f)
                mm(B[7][0:1, 12:13], more_f, ones[:, 0:1]).then_inc(sem("more_ps"), 1)
            if k == 5:
                pe.wait_ge(*at("hot", 1))
                mm(B[7][0:1, 16:32], e_col, item_hot)
                mm(B[7][0:1, 32:48], thr_col, item_hot).then_inc(sem("hot_ps"), 1)
        ins.then_inc(sem("xg_ps"), 1)
        pe.wait_ge(*at("gateT", 1))
        pe.wait_ge(*at("b1_done", 1))
        pe.wait_ge(*at("items_ready", 1))
        n_items = pe.value_load(item_count[0:1, 0:1], min_val=N_EXP, max_val=N_EXP + EXTRA)
        pe.nop().then_inc(sem("put_ps"), 1)
        with pe.Fori(0, n_items) as item:
            pe.wait_ge(*at("xg", item + 1))
            for j in range(4):
                for r in range(2):
                    s = expert_slot(2 * j + r)
                    pe.wait_ge(landed[s], (item + 1) * 16 + landed_pre[s])
                for n in range(4):
                    for r in range(2):
                        k = 2 * j + r
                        ins = mm(B[n][64 * r:64 * r + 64, :], xg[:, k, :], ring[:, expert_slot(k), 512 * n:512 * n + 512],
                                 start=(j == 0), stop=(j == 3))
                    if j == 3 or n == 3:
                        ins.then_inc(sem("mm1"), 1)
            pe.wait_ge(*at("h2_split", 3))
            pe.wait_ge(*at("picks", item + 1))
            pe.wait_ge(*at("part_ready", item * 8))
            gather()
            for n in range(4):
                pe.wait_ge(*at("h_sum", item * 4 + (n + 1)))
                pe.nop().then_inc(sem("turning"), 1)
                for i in range(4):
                    f = 4 * n + i
                    ins = tr(B[f // 8][:, BLK * (f % 8):BLK * (f % 8) + BLK], h_sum[0:BLK, P * f:P * f + P])
                if n % 2:
                    ins.then_inc(sem("hT_ps"), 1)
            pe.wait_ge(*at("y_evac", item * 2))
            pe.wait_ge(*at("put", item))
            pe.wait_ge(*at("xg", item + 2))
            for d in range(KD):
                if d >= 2:
                    pe.wait_ge(*at("part_ready", item * 8 + (d - 1)))
                mm(B[6 + d % 2][:, 0:T], y_e[:, P * d:P * d + P], put).then_inc(sem("scat_ps"), 1)
            pe.wait_ge(*at("part_ready", item * 8 + 8))
            pe.wait_ge(*at("gpicks", item + 1))
            for c, (a, n) in enumerate(TOK):
                ins = tr(B[7][:, a:a + n], gpick[0:n, c, :])
            ins.then_inc(sem("put_ps"), 1)
            pe.wait_ge(*at("act", item + 1))
            for j in range(4):
                s = expert_slot(8 + j)
                pe.wait_ge(landed[s], (item + 1) * 16 + landed_pre[s])
                for n in range(2):
                    for r in range(2):
                        k = 2 * j + r
                        ins = mm(B[4 + n][64 * r:64 * r + 64, :], act_e[:, BLK * k:BLK * k + BLK],
                                 ring[:, s, D * r + 512 * n:D * r + 512 * n + 512], start=(j == 0), stop=(j == 3))
                ins.then_inc(sem("mm2"), 1)
        pe.wait_ge(*at("put", n_items))
        pe.wait_ge(*at("part_ready", n_items * 8))
        pe.wait_ge(*at("b2_landed", 16))
        for d in range(KD + 2):
            if d >= 2:
                pe.wait_ge(*at("last_add", d - 1))
            if d < KD:
                mm(B[6 + d % 2][:, 0:T], b2_nat[0:32, P * d:P * d + P], gateT[0:32, :], stop=False)
                if d == 0:
                    pe.wait_ge(*at("y_evac", n_items * 2))
                mm(B[6 + d % 2][:, 0:T], y_e[:, P * d:P * d + P], put, start=False).then_inc(sem("scat_ps"), 1)
            k = d - 2
            for c, (a, n) in enumerate(TOK if k >= 0 else ()):
                ins = tr(B[2 * c + k // 4][0:n, P * (k % 4):P * (k % 4) + P], xT[:, k, a:a + n])
                if k % 4 == 3:
                    ins.then_inc(sem("y_ps"), 1)

    @block.scalar
    def _(act):
        fn = nc.scalar.activation

        def step(ins):
            link(act, "act_step", ins)

        def norm_root(s, scale):
            for i in range(HN[s]):
                act.wait_ge(*at("hn_ss", HN_BASE[s] + i + 1))
                if i == 0 and s:
                    act.wait_ge(*at("hn_done", HN_BASE[s]))
                fn(rt[:, i, :], B[4 + i % 4][:, 0:T], ACT.Ln, bias=eps_col, scale=scale).then_inc(sem("hn_rt"), 1)
            act.wait_ge(*at("hn_rt", HN_BASE[s] + HN[s]))
            fn(rt[:, 0:HN[s], :], rt[:, 0:HN[s], :], ACT.Exp, scale=-0.5).then_inc(sem("hn_inv"), 1)

        act.dma_start(xs_nat[0:NB, :], A["x_sample"].rearrange("b l d -> (b l) d")).then_inc(sem("xs_landed"), 16)
        rows = [(LN1, 8, A["ln1_gain"][0].rearrange("(k p) -> k p", p=P)),
                (LN2, 8, A["ln2_gain"][0].rearrange("(k p) -> k p", p=P)),
                (LNM, 8, A["mem_norm"][0].rearrange("(k p) -> k p", p=P)),
                (C_GDN, 1, A["gdn_norm"]), (C_QM, 1, A["q_norm_mem"]),
                (C_CONV, 48, A["conv_w"][0].rearrange("j (c p) -> (j c) p", p=P))]
        for r, n, src in rows:
            act.dma_start(prm[r:r + n, :], src).then_inc(sem("prm_landed"), 16)
        for half in range(2):
            act.dma_start(prm[C_QS:C_QS + 1, 64 * half:64 * half + 64], A["q_norm_swa"]).then_inc(sem("prm_landed"), 16)
            act.dma_start(prm[C_KS:C_KS + 1, 64 * half:64 * half + 64], A["k_norm_swa"]).then_inc(sem("prm_landed"), 16)
        act.dma_start(cst_nat[0:24, :], A["state_conv"][0].rearrange("b j n -> (b j) n")).then_inc(sem("cst_landed"), 16)
        def late_to_sbuf(*chunks):
            for n in chunks:
                act.wait_ge(*at("late_ps", n + 1))
                dst = zT[:, n, :] if n < 4 else gates[:, n - 4, :]
                fn(dst, B[LATE_BANKS[n]][:, 0:T], ACT.Copy).then_inc(sem("late_out"), 1)

        for g in range(0, 8, 2):
            act.wait_ge(*at("x_T", g + 1))
            fn(xT[:, g, :], B[g % 4][:, 0:T], ACT.Copy).then_inc(sem("tr_evac_act"), 1)
        act.wait_ge(*at("tr_evac_act", 4))
        act.wait_ge(*at("tr_evac_dve", 4))
        fn(G_flat, xT_flat, ACT.Square).then_inc(sem("ln_sq"), 1)
        act.wait_ge(*at("tr_evac_dve", 12))
        fn(cv_flat[:, 0:2048], memT.rearrange("p k n -> p (k n)"), ACT.Square).then_inc(sem("ln_sq"), 1)
        act.wait_ge(*at("ln_ss", 1))
        act.wait_ge(*at("eps", 1))
        step(fn(rsx, B[4][:, 0:T], ACT.Ln, bias=eps_col, scale=1.0 / D))
        fn(rsx, rsx, ACT.Exp, scale=-0.5).then_inc(sem("ln_rt"), 1)
        act.wait_ge(*at("ln_ss", 2))
        step(fn(rsm, B[5][:, 0:NP_TOK], ACT.Ln, bias=eps_col, scale=1.0 / D))
        fn(rsm, rsm, ACT.Exp, scale=-0.5).then_inc(sem("ln_rt"), 1)
        for n in range(4):
            act.wait_ge(*at("proj", n + 1))
            fn(qm[:, n, :], B[n % 4][:, 0:T], ACT.Copy).then_inc(sem("proj_evac"), 1)
        act.wait_ge(*at("proj_evac", 4))
        fn(G_flat[:, 0:4 * T], qm_flat, ACT.Square).then_inc(sem("hn_sq"), 1)
        act.wait_ge(*at("memTn_ready", 8))
        for n in range(4, 12):
            i, c = n // 2 - PC_MKV, n % 2
            act.wait_ge(*at("proj", n + 1))
            dst = (Kn if i < 2 else Vm)[:, c, 256 * (i % 2):256 * (i % 2) + 256]
            fn(dst, B[n % 4][:, 0:256], ACT.Copy).then_inc(sem("proj_evac"), 1)
        norm_root(0, 1.0 / HD_M)
        fn(G_flat[:, 0:1024], Kn_flat, ACT.Square).then_inc(sem("kn_sq"), 1)
        act.wait_ge(*at("kn_ss", 1))
        fn(stat[:, 8:16], stat[:, 0:8], ACT.Sqrt, bias=eps_col, scale=1.0 / HD_M).then_inc(sem("kn_rt"), 1)
        def conv_sigmoid(c):
            act.wait_ge(*at("conv_y", c + 1))
            if c >= 2:
                act.wait_ge(*at("conv_done", c - 1))
            fn(conv_sg[:, c % 2, :], conv_y[:, c % 2, :], ACT.Sigmoid).then_inc(sem("conv_sg"), 1)

        act.wait_ge(*at("cin_ready", 1))
        for n in range(12, 30):
            act.wait_ge(*at("proj", n + 1))
            j = n - 12
            if j < 5:
                dst = qsk[:, j, :]
            elif j == 5:
                dst = vsT
            else:
                c = j - 6
                fn(cin[:, c, 3:3 + NP_TOK], B[n % 4][:, 0:NP_TOK], ACT.Copy)
                fn(cin[:, c, 3 + NP_TOK:CONV_FLAT].rearrange("p (b j) -> p b j", j=4)[:, :, 3],
                   B[n % 4][:, NP_TOK:T], ACT.Copy).then_inc(sem("proj_evac"), 1)
            if j < 6:
                fn(dst, B[n % 4][:, 0:T], ACT.Copy).then_inc(sem("proj_evac"), 1)
            if j >= 8:
                conv_sigmoid(j - 8)
        conv_sigmoid(10)
        act.wait_ge(*at("ab_ps", 1))
        fn(ab_T[0:8, :], B[4][0:8, 0:T], ACT.Copy).then_inc(sem("ab_T"), 1)
        conv_sigmoid(11)
        act.wait_ge(*at("hn_done", 4))
        act.wait_ge(*at("proj_evac", 30))
        fn(G_flat[:, 0:5 * T], qsk_flat, ACT.Square).then_inc(sem("hn_sq"), 1)
        late_to_sbuf(0, 1)
        norm_root(1, 1.0 / HD_S)
        act.wait_ge(*at("conv_done", 12))
        act.wait_ge(*at("hn_ss", HN_BASE[2]))
        fn(G_flat, cv_flat[:, 0:KD * T], ACT.Square).then_inc(sem("hn_sq"), 1)
        late_to_sbuf(2, 3)
        norm_root(2, 1.0)
        act.wait_ge(*at("hn_ss", HN_BASE[3]))
        act.wait_ge(*at("late_out", 4))
        fn(G_flat[:, 0:4 * T], zT_flat, ACT.Sigmoid).then_inc(sem("z_sg"), 1)
        act.wait_ge(*at("dc", 1))
        step(fn(gt1, gt1, ACT.Exp))
        step(fn(gt1, gt1, ACT.Ln, bias=1.0))
        step(fn(beta_n, ab_n[:, :, 4:8], ACT.Exp, scale=-1.0))
        fn(alog_b, alog_b, ACT.Exp).then_inc(sem("dc_act"), 1)
        for c in range(2):
            act.wait_ge(*at("kmT_ps", c + 1))
            fn(KmT[:, :, P * c:P * c + P], grid(B[6 + c][:, :], P), ACT.Copy).then_inc(sem("KmT_ready"), 1)
        for c in range(3):
            act.wait_ge(*at("conv_rows_ps", c + 1))
            act.wait_ge(*at("conv_done", 12))
            fn(cso[0:27, 512 * c:512 * c + 512], B[c][0:27, :], ACT.Copy).then_inc(sem("conv_rows_ready"), 1)

        late_to_sbuf(4, 5, 6)
        late_to_sbuf(7)
        act.wait_ge(*at("mm_m", 1))
        for i in range(8):
            ins = fn(mm_s[:, i, :], mm_s[:, i, :], ACT.Exp, bias=stat[:, 8 + i:9 + i], scale=HD_M ** -0.5,
                     accum_out=stat[:, 16 + i:17 + i])
        ins.then_inc(sem("mm_e"), 1)
        late_to_sbuf(8, 9)
        for i in range(8):
            act.wait_ge(*at("mm_pT_ps", i + 1))
            if i >= 2:
                act.wait_ge(*at("mm_o_ps", i - 1))
            fn(mm_pT[:, i % 2, :], B[2 + i % 2][:, 0:2 * P], ACT.Copy).then_inc(sem("mm_pT"), 1)
        late_to_sbuf(10, 11)
        act.wait_ge(*at("sw_m", 1))
        for i in range(8):
            fn(sw_s3[:, i, 0:P], sw_s3[:, i, 0:P], ACT.Exp, bias=stat[:, 16 + i:17 + i], accum_out=stat[:, 32 + i:33 + i])
            fn(sw_s3[:, i, P:3 * P], sw_s3[:, i, P:3 * P], ACT.Exp, bias=stat[:, 24 + i:25 + i],
               accum_out=stat[:, 40 + i:41 + i])
        fn(stat[:, 48:64], stat[:, 48:64], ACT.Exp).then_inc(sem("sw_e"), 1)
        late_to_sbuf(12, 13, 14)
        for i in range(8):
            act.wait_ge(*at("sw_pT_ps", i + 1))
            if i >= 2:
                act.wait_ge(*at("sw_o_ps", i - 1))
            fn(sw_pT[:, i % 2, :], B[2 + i % 2][:, 0:3 * P], ACT.Copy).then_inc(sem("sw_pT"), 1)
        act.wait_ge(*at("sw_o", 4))
        for j in range(2):
            act.wait_ge(*at("ss_kT_ps", j + 1))
            fn(grid(cols(scr, 512 * j, 512), P), grid(B[j][:, :], P), ACT.Copy).then_inc(sem("ss_kT"), 1)
        act.wait_ge(*at("ss_m", 1))
        fn(ss[0:64, :], ss[0:64, :], ACT.Exp, bias=stat[0:64, 1:2], accum_out=stat[0:64, 2:3])
        fn(stat[0:64, 3:4], stat[0:64, 5:6], ACT.Exp, bias=stat[0:64, 1:2]).then_inc(sem("ss_e"), 1)
        late_to_sbuf(15, 16)
        act.wait_ge(*at("gd_small", 1))
        fn(g_sm[:, 16:40], g_sm[:, 16:40], ACT.Exp).then_inc(sem("gd_exp"), 1)
        fn(gt1[0:NB, 2, :], g_n[0:NB, 2, :], ACT.Exp).then_inc(sem("gs_eg"), 1)
        act.wait_ge(*at("gd_row", 2))
        act.wait_ge(*at("ss_done", 1))
        act.wait_ge(*at("gd_min", 1))
        fn(e_row.rearrange("p k n -> p (k n)"), B[2][:, :], ACT.Exp).then_inc(sem("gd_erow"), 1)
        fn(dec_flat, dec_flat, ACT.Exp).then_inc(sem("gd_dec_e"), 1)
        act.wait_ge(*at("memkv_stored", 1))
        act.wait_ge(*at("gd_exp", 1))
        for c in range(2):
            act.wait_ge(*at("gd_kn", c + 1))
            for h in range(H_G):
                ins = fn(k_dec[:, 4 * c + h, :], B[1 + c][:, P * h:P * h + P], ACT.Copy, scale=g_sm[:, 32 + 4 * c + h:33 + 4 * c + h])
            ins.then_inc(sem("gd_kdec"), 1)
        for c in range(2):
            act.wait_ge(*at("gd_vn", c + 1))
            for h in range(H_G):
                ins = fn(v_beta[:, 4 * c + h, :], B[3 + c][:, P * h:P * h + P], ACT.Copy, scale=beta_n[:, c, h:h + 1])
            ins.then_inc(sem("gd_vbeta"), 1)
        for s, (_, _, _, what) in enumerate(INVERSE):
            if what[0] == "copy":
                act.wait_ge(*at("inv_ps", 2 * s + 2))
                fn(inv_flat[what[1]][:, 512:1024], B[(6, 0)[s % 2]][:, :], ACT.Copy).then_inc(sem("inv_act"), 1)
            if s % 4 == 0:
                late_to_sbuf(17 + s // 4)
        act.wait_ge(*at("gd_v0", 1))
        act.wait_ge(*at("gd_kdec", 2))
        fn(cols(KmT_flat, 0, 512), B[1][:, :], ACT.Copy).then_inc(sem("gd_v0_evac"), 1)
        act.wait_ge(*at("gd_v1", 1))
        act.wait_ge(*at("gd_s1", 1))
        act.wait_ge(*at("gd_o0", 1))
        fn(cols(KmT_flat, 0, 512), B[1][:, :], ACT.Copy).then_inc(sem("gd_v1_evac"), 1)
        late_to_sbuf(23, 24)

        def gate_sigmoids(i):
            act.wait_ge(*at("late_out", 8 * i + 12))
            own = gates_flat[:, 8 * i * T:8 * (i + 1) * T]
            fn(own, own, ACT.Sigmoid).then_inc(sem("gates"), 1)

        act.wait_ge(*at("gs_v", 1))
        fn(sq3, oT_flat[:, 4 * T:8 * T], ACT.Square).then_inc(sem("hn_sq"), 1)
        late_to_sbuf(25)
        gate_sigmoids(0)
        late_to_sbuf(26, 27)
        gate_sigmoids(1)
        norm_root(3, 1.0 / HD_G)
        gate_sigmoids(2)
        act.wait_ge(*at("ms_m", 1))
        fn(ms[0:32, :], ms[0:32, :], ACT.Exp, bias=stat[0:32, 1:2], scale=HD_M ** -0.5,
           accum_out=stat[0:32, 2:3]).then_inc(sem("ms_e"), 1)
        for j in range(2):
            act.wait_ge(*at("ms_o_ps", 4 * j + 4))
            fn(ms_pv[:, j, :], B[2 + j][:, :], ACT.Copy).then_inc(sem("ms_o_evac"), 1)
        for k in range(KD):
            act.wait_ge(*at("x1", k + 1))
            fn(G[:, k, :], xT[:, k, :], ACT.Square).then_inc(sem("ln_sq"), 1)
        act.wait_ge(*at("ln_ss", 3))
        act.wait_ge(*at("gdn_stored", 1))
        step(fn(rr[:, 0:T], B[4][:, 0:T], ACT.Ln, bias=eps_col, scale=1.0 / D))
        fn(rr[:, 0:T], rr[:, 0:T], ACT.Exp, scale=-0.5).then_inc(sem("ln_rt"), 1)
        act.wait_ge(*at("b1_ps", 1))
        act.wait_ge(*at("moe_ready", 1))
        fn(b1_e.rearrange("p e f -> p f e"), grid(B[7][:, :], N_EXP), ACT.Copy).then_inc(sem("b1_done"), 1)
        act.wait_ge(*at("lg_ps", 1))
        fn(lgT[0:32, :], B[5][0:32, 0:T], ACT.Copy).then_inc(sem("lgT"), 1)
        for c, (a, n) in enumerate(TOK):
            for j in range(2):
                act.wait_ge(*at("h2_nat_ps", 2 * c + j + 1))
                ins = fn(h2_nat[0:n, c, 512 * j:512 * j + 512], B[(0, 2, 6)[c] + j][0:n, :], ACT.Copy)
                ins.then_inc(sem("h2_nat"), 1)
            act.wait_ge(*at("h2_nat", 2 * c + 2))
            fn(h2_parts[0:n, 0, c, :], h2_nat[0:n, c, :], ACT.Copy).then_inc(sem("h2_hi"), 1)
            if c == 0:
                act.wait_ge(*at("top", 1))
                fn(top_p, top_p, ACT.Exp).then_inc(sem("top_e"), 1)
        act.wait_ge(*at("gateT_ps", 1))
        fn(gateT[0:32, :], B[0][0:32, 0:T], ACT.Copy).then_inc(sem("gateT"), 1)

        act.wait_ge(*at("xg_ps", 1))
        fn(xg.rearrange("p k n -> p (k n)"), B[6][:, :], ACT.Copy).then_inc(sem("xg"), 1)
        act.wait_ge(*at("items_ready", 1))
        n_items = act.value_load(item_count[0:1, 0:1], min_val=N_EXP, max_val=N_EXP + EXTRA)
        for name in ("part_ready", "put", "y_evac"):
            act.nop().then_inc(sem(name), 1)
        with act.Fori(0, n_items) as item:
            fn(stat[:, 101:102], eps_col, ACT.Sigmoid)
            act.wait_ge(*at("h_sum", item * 4))
            for n in range(4):
                act.wait_ge(*at("mm1", item * 7 + (n + 4)))
                fn(h_odd[0:BLK, 512 * n:512 * n + 512], B[n][64:64 + BLK, :], ACT.Copy).then_inc(sem("h_odd"), 1)
            act.wait_ge(*at("xg_ps", item + 2))
            fn(xg.rearrange("p k n -> p (k n)"), B[6][:, :], ACT.Copy).then_inc(sem("xg"), 1)
            act.wait_ge(*at("acc_done", item))
            for d in range(KD):
                if d == 2:
                    act.wait_ge(*at("glu", item + 1))
                    fn(sg, glu, ACT.Sigmoid, scale=ALPHA).then_inc(sem("sg"), 1)
                act.wait_ge(*at("scat_ps", item * 8 + (d + 1)))
                fn(part[:, d, :], B[6 + d % 2][:, 0:T], ACT.Copy).then_inc(sem("part_ready"), 1)
            act.wait_ge(*at("put_ps", item + 1))
            fn(put, B[7][:, 0:T], ACT.Copy).then_inc(sem("put"), 1)
            act.wait_ge(*at("mm2", item * 4 + 4))
            for n in range(2):
                fn(y_e[:, 512 * n:512 * n + 512], B[4 + n][:, :], ACT.Copy).then_inc(sem("y_evac"), 1)
        for c, (a, n) in enumerate(TOK):
            act.wait_ge(*at("y_ps", c + 1))
            fn(y_out[0:n, c, 0:512], B[2 * c][0:n, :], ACT.Copy).then_inc(sem("y_act"), 1)
        act.wait_ge(*at("y_ps", 5))
        fn(y_out[:, 1, 512:1024], B[3][:, :], ACT.Copy).then_inc(sem("y_act"), 1)

    @block.vector
    def _(dve):
        v = nc.vector

        def step(ins):
            link(dve, "dve_step", ins)

        def norm_scale(s, dst, gains):
            dve.wait_ge(*at("hn_inv", s + 1))
            for i in range(HN[s]):
                v.scalar_tensor_tensor(dst(i), dst(i), gains(i), rt[:, i, :], ALU.mult, ALU.mult).then_inc(sem("hn_done"), 1)

        def column(i):
            return colp[:, i:i + 1]

        v.memset(eps_col, EPS).then_inc(sem("eps"), 1)
        v.memset(ab_n, 0.0)
        v.memset(stat, 0.0)
        for r in range(4):
            v.memset(thr_col[32 * r:32 * r + 32, :], float(BLK * (r + 1)))
        for g in (1, 3, 5, 7, *range(8, 16)):
            dve.wait_ge(*at("x_T", g + 1))
            dst = xT[:, g, :] if g < 8 else memT[:, g - 8, :]
            v.tensor_copy(dst, B[g % 4][:, 0:T if g < 8 else NP_TOK]).then_inc(sem("tr_evac_dve"), 1)
        dve.wait_ge(*at("prm_T", 1))
        v.tensor_copy(colp[:, 0:76], B[7][:, 0:76]).then_inc(sem("colp_ready"), 1)
        dve.wait_ge(*at("colp_ready", 1))
        step(v.tensor_scalar(column(C_QS), column(C_QS), HD_S ** -0.5, None, ALU.mult))
        dve.wait_ge(*at("const_ready", 3))
        step(v.scalar_tensor_tensor(e_col, thr_col, -0.5, e_col, ALU.mult, ALU.add))
        step(v.tensor_scalar(e_col, e_col, 32.0, None, ALU.add))
        dve.wait_ge(*at("x_T", 16))
        v.memset(cin[:, :, 0:3], 0.0)
        dve.wait_ge(*at("cst_T", 1))
        for c in range(12):
            dst = cin[:, c, 3 + NP_TOK:CONV_FLAT].rearrange("p (b j) -> p b j", j=4)[:, :, 0:3]
            ins = v.tensor_copy(dst, B[6][:, 24 * c:24 * c + 24].rearrange("p (b j) -> p b j", j=3))
        ins.then_inc(sem("cst_done"), 1)
        dve.wait_ge(*at("cst_done", 1))
        v.tensor_scalar(stat[:, 100:101], eps_col, 0.0, None, ALU.mult).then_inc(sem("cin_ready"), 1)
        dve.wait_ge(*at("ln_rt", 1))
        for k in range(KD):
            v.scalar_tensor_tensor(hT[:, k, :], xT[:, k, :], column(LN1 + k), rsx, ALU.mult, ALU.mult).then_inc(sem("hT_ready"), 1)
        dve.wait_ge(*at("ln_rt", 2))
        for k in range(KD):
            v.scalar_tensor_tensor(memTn[:, k, :], memT[:, k, :], column(LNM + k), rsm, ALU.mult, ALU.mult).then_inc(sem("memTn_ready"), 1)
        norm_scale(0, lambda i: qm[:, i, :], lambda i: column(C_QM))
        dve.wait_ge(*at("rowp_landed", 80))
        dve.wait_ge(*at("kn_sq", 1))
        v.reduce_sum(stat[:, 0:8], grid(G_flat[:, 0:1024], P), AX).then_inc(sem("kn_ss"), 1)
        dve.wait_ge(*at("kn_rt", 1))
        step(v.reciprocal(stat[:, 8:16], stat[:, 8:16]))
        kn8 = grid(Kn_flat, P)
        step(v.tensor_tensor(kn8, kn8, bc(stat[:, 8:16], P), ALU.mult))
        dve.wait_ge(*at("proj_evac", 12))
        v.tensor_tensor(kn8, kn8, mid(knorm_b, 8), ALU.mult).then_inc(sem("memkv_ready"), 1)
        for c in range(13):
            if c < 12:
                dve.wait_ge(*at("proj_evac", 19 + c))
                if c >= 2:
                    dve.wait_ge(*at("conv_done", c - 1))
                y = conv_y[:, c % 2, :]
                step(v.tensor_scalar(y, cin[:, c, 0:288], column(C_CONV + c), None, ALU.mult))
                for j in range(1, 4):
                    ins = v.scalar_tensor_tensor(y, cin[:, c, j:j + 288], column(C_CONV + 12 * j + c), y, ALU.mult, ALU.add)
                    if j < 3:
                        step(ins)
                    else:
                        ins.then_inc(sem("conv_y"), 1)
            if c:
                i = c - 1
                dve.wait_ge(*at("conv_sg", i + 1))
                y, s = conv_y[:, i % 2, :], conv_sg[:, i % 2, :]
                v.tensor_tensor(cv[:, i, 0:NP_TOK], y[:, 0:NP_TOK], s[:, 0:NP_TOK], ALU.mult)
                ys, s_s = (u[:, 256:288].rearrange("p (b j) -> p b j", j=4)[:, :, 3] for u in (y, s))
                v.tensor_tensor(cv[:, i, NP_TOK:T], ys, s_s, ALU.mult).then_inc(sem("conv_done"), 1)
        cs = grid(conv_save, 27)
        v.tensor_copy(cs[:, :, 0:3], cin[:, :, NP_TOK:NP_TOK + 3])
        for c in range(12):
            src = cin[:, c, 3 + NP_TOK:CONV_FLAT].rearrange("p (b j) -> p b j", j=4)[:, :, 1:4]
            ins = v.tensor_copy(cs[:, c, 3:27].rearrange("p (b j) -> p b j", j=3), src)
        ins.then_inc(sem("conv_saved"), 1)
        dve.wait_ge(*at("ab_nT", 1))
        for c, (a, n) in enumerate(TOK):
            ins = v.tensor_copy(ab_n[0:n, c, :], B[5][0:n, 8 * c:8 * c + 8])
        ins.then_inc(sem("ab_done"), 1)
        dve.wait_ge(*at("ab_done", 1))
        step(v.tensor_tensor(gt0, ab_n[:, :, 0:4], mid(dt_b, 3), ALU.add))
        step(v.tensor_scalar(gt1, gt0, -1.0, None, ALU.mult))
        v.tensor_tensor(gt1, gt0, gt1, ALU.min).then_inc(sem("dc"), 1)
        norm_scale(1, lambda i: qsk[:, i, :], lambda i: column(C_QS if i < 4 else C_KS))
        norm_scale(2, lambda i: cv[:, i, :], lambda i: HD_G ** -0.5 if i < 4 else 1.0)
        dve.wait_ge(*at("z_sg", 1))
        step(v.tensor_tensor(zT_flat, zT_flat, G_flat[:, 0:4 * T], ALU.mult))
        dve.wait_ge(*at("dc_act", 1))
        step(v.scalar_tensor_tensor(gt0, gt0, 0.0, gt1, ALU.max, ALU.add))
        step(v.tensor_tensor(gt0, gt0, mid(alog_b, 3), ALU.mult))
        step(v.tensor_scalar(g_n, gt0, -1.0, None, ALU.mult))
        step(v.tensor_scalar(beta_n, beta_n, 1.0, None, ALU.add))
        v.reciprocal(beta_n, beta_n).then_inc(sem("decay_ready"), 1)

        dve.wait_ge(*at("hn_done", HN_BASE[3]))
        for i in range(8):
            dve.wait_ge(*at("mm_s", i + 1))
            v.tensor_copy(mm_s[:, i, :], B[i % 2][:, 0:256]).then_inc(sem("mm_s_evac"), 1)
        dve.wait_ge(*at("mm_s_evac", 8))
        step(v.tensor_reduce(stat[:, 0:8], mm_s, AX, ALU.max))
        v.tensor_scalar(stat[:, 8:16], stat[:, 0:8], -(HD_M ** -0.5), None, ALU.mult).then_inc(sem("mm_m"), 1)
        dve.wait_ge(*at("mm_e", 1))
        step(v.reciprocal(stat[:, 16:24], stat[:, 16:24]))
        v.tensor_tensor(mm_s, mm_s, bc(stat[:, 16:24], NP_TOK), ALU.mult).then_inc(sem("mm_p"), 1)
        dve.wait_ge(*at("conv_stored", 1))
        for h in range(H_M):
            dve.wait_ge(*at("mm_o_ps", 2 * h + 2))
            v.tensor_copy(oT[:, 8 + h, 0:NP_TOK], B[4 + h % 2][:, 0:256]).then_inc(sem("mm_o"), 1)
        dve.wait_ge(*at("mm_o_ps", 8))
        for kv in range(2):
            for half in range(2):
                ins = v.tensor_copy(k_dup[64 * half:64 * half + 64, kv, :], qsk[64 * kv:64 * kv + 64, 4, :])
        ins.then_inc(sem("k_dup"), 1)
        dve.wait_ge(*at("swa_nat", 1))
        v.tensor_copy(kv_nat, B[6][:, 0:3 * P]).then_inc(sem("swa_rows_ready"), 1)
        dve.wait_ge(*at("swa_nat", 2))
        v.tensor_copy(kv_s[0:NB, :], B[7][0:NB, 0:2 * P]).then_inc(sem("swa_rows_ready"), 1)
        for h in range(H_S):
            dve.wait_ge(*at("sw_s", h + 1))
            v.scalar_tensor_tensor(sw_s3[:, h, :], neg_dist, 2.0 ** -(h + 1), B[h % 2][:, 0:3 * P], ALU.mult,
                                   ALU.add).then_inc(sem("sw_s_evac"), 1)
        dve.wait_ge(*at("sw_s_evac", 8))
        v.tensor_reduce(stat[:, 0:8], sw_s3[:, :, 0:P], AX, ALU.max)
        step(v.tensor_reduce(stat[:, 8:16], sw_s3[:, :, P:3 * P], AX, ALU.max))
        two = stat[:, 0:16].rearrange("p (c h) -> p c h", h=8)
        step(v.tensor_tensor(two, two, mid(sink_b, 2), ALU.max))
        v.tensor_scalar(stat[:, 16:32], stat[:, 0:16], -1.0, None, ALU.mult)
        v.tensor_tensor(stat[:, 48:64].rearrange("p (c h) -> p c h", h=8), mid(sink_b, 2), two,
                        ALU.subtract).then_inc(sem("sw_m"), 1)
        dve.wait_ge(*at("sw_e", 1))
        step(v.tensor_tensor(stat[:, 32:48], stat[:, 32:48], stat[:, 48:64], ALU.add))
        step(v.reciprocal(stat[:, 32:48], stat[:, 32:48]))
        v.tensor_tensor(sw_s3[:, :, 0:P], sw_s3[:, :, 0:P], bc(stat[:, 32:40], P), ALU.mult)
        v.tensor_tensor(sw_s3[:, :, P:3 * P], sw_s3[:, :, P:3 * P], bc(stat[:, 40:48], 2 * P),
                        ALU.mult).then_inc(sem("sw_p"), 1)
        for i in range(4):
            dve.wait_ge(*at("sw_o_ps", 2 * i + 2))
            v.tensor_copy(oT[:, i, 0:NP_TOK], B[4 + i % 2][:, 0:256]).then_inc(sem("sw_o"), 1)

        dve.wait_ge(*at("sw_o", 4))
        step(v.memset(q_bd, 0.0))
        for h in range(H_S):
            a, b = 64 * (h // 4), 64 * (h % 2)
            ins = v.tensor_copy(q_bd3[a:a + 64, :, h], qsk[b:b + 64, h // 2, NP_TOK:T])
            v.memset(rows64[0:1, h:64:8], 2.0 ** -(h + 1))
        step(v.tensor_copy(rows64[0:1, 64:128].rearrange("p (b h) -> p b h", h=8), mid(sink_b[0:1, :], 8)))
        v.tensor_tensor(ss_prod3, q_bd3, bc(qsk[:, 4, NP_TOK:T], 8), ALU.mult).then_inc(sem("ss_q"), 1)
        dve.wait_ge(*at("ss_new", 1))
        step(v.tensor_copy(stat[0:64, 4:7], B[3][0:64, 0:3]))
        step(v.tensor_copy(stat[0:64, 7:8], stat[0:64, 5:6]))
        step(v.tensor_copy(stat[0:64, 5:6], stat[0:64, 6:7]))
        dve.wait_ge(*at("ss_s", 1))
        v.tensor_copy(ss_T, B[2][:, 0:64]).then_inc(sem("ss_sT"), 1)
        dve.wait_ge(*at("ss_rows", 1))
        v.tensor_copy(ss[0:64, P:P + 1], stat[0:64, 4:5])
        step(v.scalar_tensor_tensor(ss[0:64, 0:P], neg_dist_s[0:64, :], stat[0:64, 7:8], B[4][0:64, 0:P], ALU.mult, ALU.add))
        step(v.tensor_reduce(stat[0:64, 0:1], ss[0:64, :], AX, ALU.max))
        step(v.tensor_tensor(stat[0:64, 0:1], stat[0:64, 0:1], stat[0:64, 5:6], ALU.max))
        v.tensor_scalar(stat[0:64, 1:2], stat[0:64, 0:1], -1.0, None, ALU.mult).then_inc(sem("ss_m"), 1)
        dve.wait_ge(*at("ss_e", 1))
        step(v.tensor_tensor(stat[0:64, 2:3], stat[0:64, 2:3], stat[0:64, 3:4], ALU.add))
        step(v.reciprocal(stat[0:64, 2:3], stat[0:64, 2:3]))
        step(v.tensor_scalar(ss[0:64, :], ss[0:64, :], stat[0:64, 2:3], None, ALU.mult))
        v.tensor_copy(ss_pb[0:64, :], ss[0:64, P:P + 1].broadcast_to([64, P])).then_inc(sem("ss_p"), 1)
        dve.wait_ge(*at("ss_pT_ps", 1))
        v.tensor_copy(ss_pT, B[5][:, 0:64]).then_inc(sem("ss_pT"), 1)
        step(v.tensor_tensor(ss_o3, grid(B[3][:, 0:64], 8), bc(vsT[:, NP_TOK:T], 8), ALU.mult))
        dve.wait_ge(*at("ss_o_ps", 1))
        step(v.tensor_tensor(ss_o, ss_o, B[2][:, 0:64], ALU.add))
        for h in range(H_S):
            a, b = 64 * (h // 4), 64 * (h % 2)
            ins = v.tensor_copy(oT[b:b + 64, h // 2, NP_TOK:T], ss_o3[a:a + 64, :, h])
        ins.then_inc(sem("ss_done"), 1)

        dve.wait_ge(*at("ss_done", 1))
        dve.wait_ge(*at("gd_cum", 1))
        step(v.tensor_copy(g_sm[:, 0:16], B[0][:, 0:16]))
        v.tensor_copy(g_sm[:, 16:32], g_sm[:, 0:16]).then_inc(sem("gd_cum_evac"), 1)
        v.tensor_tensor(g_sm[:, 32:40], g_sm[:, 8:16], g_sm[:, 0:8], ALU.subtract).then_inc(sem("gd_small"), 1)
        dve.wait_ge(*at("gd_row", 2))
        for m in range(8):
            h = m % 4
            ins = v.tensor_scalar(dec[:, m, :], B[1 + m // 4][:, P * h:P * h + P], g_sm[:, m:m + 1], 0.0, ALU.subtract, ALU.min)
        ins.then_inc(sem("gd_min"), 1)
        dve.wait_ge(*at("gd_erow", 1))
        step(v.tensor_tensor(q_dec, cv[:, 0:4, P:2 * P], e_row, ALU.mult))
        dve.wait_ge(*at("gd_exp", 1))
        step(v.tensor_tensor(g_sm[:, 40:48].rearrange("p (c h) -> p c h", h=4), g_sm[:, 16:24].rearrange("p (c h) -> p c h", h=4),
                             beta_n[:, 0:2, :], ALU.mult))
        step(v.tensor_scalar(g_sm[:, 40:48], g_sm[:, 40:48], -1.0, None, ALU.mult))
        dve.wait_ge(*at("gd_dec_e", 1))
        dve.wait_ge(*at("swa_stored", 1))
        v.tensor_tensor(inv[5], dec, mid(tri_strict, 8), ALU.mult).then_inc(sem("gd_dec"), 1)
        v.tensor_tensor(dec, dec, mid(tri_incl, 8), ALU.mult).then_inc(sem("gd_dec"), 1)
        dve.wait_ge(*at("gd_dec", 2))
        for c in range(2):
            dve.wait_ge(*at("gd_kk", c + 1))
            part_a = inv_flat[0][:, 512 * c:512 * c + 512]
            step(v.tensor_tensor(part_a, B[5 + c][:, :], inv_flat[5][:, 512 * c:512 * c + 512], ALU.mult))
            dve.wait_ge(*at("gd_brow", c + 1))
            v.tensor_tensor(part_a, part_a, B[3 + c][:, :], ALU.mult).then_inc(sem("gd_at"), 1)
        for c in range(2):
            dve.wait_ge(*at("gd_qk", c + 1))
            v.tensor_tensor(intra_flat[:, 512 * c:512 * c + 512], B[7 if c == 0 else 0][:, :],
                            dec_flat[:, 512 * c:512 * c + 512], ALU.mult).then_inc(sem("gd_qk_done"), 1)
        for s, (kind, a, b, what) in enumerate(INVERSE):
            for c in range(1 if what[0] == "copy" else 2):
                dve.wait_ge(*at("inv_ps", 2 * s + c + 1))
                bank = B[(5, 6, 7, 0)[2 * (s % 2) + c]]
                own = slice(512 * c, 512 * c + 512)
                ps = bank[:, :]
                if what[0] == "parts":
                    g4 = slice(4 * c, 4 * c + 4)
                    step(v.tensor_tensor(inv[1][:, g4, :], grid(ps, P), mid(diag16, 4), ALU.mult))
                    step(v.tensor_tensor(inv_flat[2][:, own], ps, inv_flat[1][:, own], ALU.subtract))
                    step(v.tensor_tensor(inv[3][:, g4, :], mid(ident, 4), inv[1][:, g4, :], ALU.subtract))
                    ins = v.tensor_tensor(inv[0][:, g4, :], inv[0][:, g4, :], mid(diag16, 4), ALU.mult)
                elif what[0] == "copy":
                    ins = v.tensor_copy(inv_flat[what[1]][:, own], ps)
                elif what[0] == "add":
                    ins = v.tensor_tensor(inv_flat[what[1]][:, own], inv_flat[what[1]][:, own], ps, ALU.add)
                else:
                    ins = v.tensor_tensor(inv_flat[what[1]][:, own], inv_flat[what[1]][:, own], ps, ALU.subtract)
                ins.then_inc(sem("inv"), 1)
        dve.wait_ge(*at("gd_s1", 1))
        v.tensor_copy(s_one.rearrange("p k n -> p (k n)"), B[2][:, :]).then_inc(sem("gd_s1_evac"), 1)
        dve.wait_ge(*at("gd_o0", 1))
        v.tensor_copy(oT[:, 4:8, 0:P], grid(B[3][:, :], P))
        dve.wait_ge(*at("gd_ks", 1))
        dve.wait_ge(*at("gd_vbeta", 2))
        for h in range(H_G):
            ins = v.scalar_tensor_tensor(r_new[:, h, :], B[4][:, P * h:P * h + P], g_sm[:, 44 + h:45 + h], v_beta[:, 4 + h, :],
                                         ALU.mult, ALU.add)
        ins.then_inc(sem("gd_r"), 1)
        dve.wait_ge(*at("gd_o1", 1))
        step(v.tensor_copy(oT[:, 4:8, P:2 * P], grid(B[5][:, :], P)))
        dve.wait_ge(*at("gd_s2", 1))
        for h in range(H_G):
            ins = v.scalar_tensor_tensor(s_one[:, h, :], s_one[:, h, :], g_sm[:, 28 + h:29 + h], B[2][:, P * h:P * h + P],
                                         ALU.mult, ALU.add)
        ins.then_inc(sem("gdn_state_ready"), 1)

        def by_bh(u):
            return u.rearrange("p h b -> p b h")

        kq4 = gs_kq.rearrange("p (b h) c -> p b h c", h=4)
        ks_, qs_ = cv[:, 4:8, NP_TOK:T], cv[:, 0:4, NP_TOK:T]
        bh = lambda u: u.rearrange("p (b h) -> p b h", h=4)
        dve.wait_ge(*at("gdn_state_ready", 1))
        v.tensor_copy(kq4[:, :, :, 0], by_bh(ks_))
        v.tensor_copy(kq4[:, :, :, 1], by_bh(qs_))
        v.tensor_tensor(bh(gs_qk), by_bh(ks_), by_bh(qs_), ALU.mult)
        dve.wait_ge(*at("gd_v1", 1))
        dg = gs_dg[0:8, :].rearrange("p (s b h) -> p s b h", s=2, h=4)
        v.tensor_tensor(dg[:, 0], bc(ident[0:8, 0:8], 4), mid(beta_n[0:8, 2, :], 8), ALU.mult)
        dve.wait_ge(*at("gs_eg", 1))
        v.tensor_tensor(dg[:, 1], bc(ident[0:8, 0:8], 4), mid(gt1[0:8, 2, :], 8), ALU.mult).then_inc(sem("gs_kq"), 1)
        dve.wait_ge(*at("gs_ps", 1))
        step(v.tensor_copy(gs_bc, B[1][:, 0:96]))
        sq = B[0][:, 0:64].rearrange("p (n c) -> p n c", c=2)
        step(v.tensor_tensor(gs_t, sq[:, :, 0], gs_bc[:, 64:96], ALU.mult))
        step(v.tensor_tensor(bh(gs_t), by_bh(cv[:, 8:12, NP_TOK:T]), bh(gs_t), ALU.subtract))
        step(v.tensor_tensor(gs_vn, gs_t, gs_bc[:, 32:64], ALU.mult))
        step(v.tensor_tensor(gs_bc[:, 0:32], gs_bc[:, 0:32], gs_vn, ALU.mult))
        step(v.tensor_tensor(gs_qk, sq[:, :, 1], gs_bc[:, 64:96], ALU.mult))
        v.tensor_tensor(by_bh(oT[:, 4:8, NP_TOK:T]), bh(gs_qk), bh(gs_bc[:, 0:32]), ALU.add)
        v.tensor_copy(gs_t, gs_kq[:, :, 0]).then_inc(sem("gs_v"), 1)
        for j in range(2):
            i = PC_STATE + j
            has_landed(dve, i)
            v.tensor_tensor(s_out3[:, 16 * j:16 * j + 16, :], grid(slot(i), P), bc(gs_bc[:, 64 + 16 * j:80 + 16 * j], P),
                            ALU.mult).then_inc(sem("state_used"), 1)
        dve.wait_ge(*at("gs_rows", 1))
        step(v.tensor_copy(gs_nat[0:32, :], B[2][0:32, 0:2 * P]))
        for j in range(8):
            if j % 2 == 0:
                if j >= 4:
                    dve.wait_ge(*at("gs_outer", j - 2))
                q = j // 2
                v.tensor_tensor(vn_mask[q % 2][0:32, :, :], mid(gs_nat[0:32, 0:P], 8), bc(ident[0:32, 8 * q:8 * q + 8], P),
                                ALU.mult).then_inc(sem("gs_mask"), 1)
            dve.wait_ge(*at("gs_outer", j + 1))
            dst = s_out[:, 512 * j:512 * j + 512]
            v.tensor_tensor(dst, dst, B[4 + j % 4][:, :], ALU.add).then_inc(sem("gs_state_ready"), 1)

        def merge(j, chunks=range(8)):
            n = BRANCHES[j]
            for d in chunks:
                dve.wait_ge(*at("branch", 8 * j + d + 1))
                ps = B[4 + d % 4][:, 0:T]
                if j == 0:
                    v.tensor_tensor(mT[:, d, :], ps, gates[:, 8 * n + d, :], ALU.mult).then_inc(sem("merged"), 1)
                else:
                    step(v.tensor_tensor(mtmp[:, d % 2, :], ps, gates[:, 8 * n + d, :], ALU.mult))
                    v.tensor_tensor(mT[:, d, :], mT[:, d, :], mtmp[:, d % 2, :], ALU.add).then_inc(sem("merged"), 1)

        dve.wait_ge(*at("gd_s2", 1))
        v.tensor_copy(pick8[0:8, :, :], bc(ident[0:8, 0:8], P))
        dve.wait_ge(*at("ms_q_ps", 1))
        v.tensor_copy(q_nat8[0:8, :], B[0][0:8, :]).then_inc(sem("ms_q"), 1)
        ms_T4 = ms_T.rearrange("p (c b h) -> p c b h", c=2, h=4)
        for b in range(NB):
            i = PC_MK + b // 2
            has_landed(dve, i)
            dve.wait_ge(*at("ms_qb", b + 1))
            kb = grid(slot(i)[:, 1024 * (b % 2):1024 * (b % 2) + 1024], 512)
            v.tensor_tensor(mk_prod.rearrange("p (c h) d -> p c (h d)", c=2), kb, mid(B[1 + b % 2][:, :], 2),
                            ALU.mult).then_inc(sem("ms_mul"), 1)
            dve.wait_ge(*at("ms_mul", b + 1))
            v.reduce_sum(ms_T4[:, :, b, :], mk_prod.rearrange("p (c h) d -> p c h d", c=2), AX).then_inc(sem("ms_s"), 1)
            if b == 0:
                dve.wait_ge(*at("gates", 1))
            merge(0, [b])
            dve.wait_ge(*at("ms_s", b + 1))
            if b == 3:
                norm_scale(3, lambda i: oT[:, 4 + i, :], lambda i: column(C_GDN))
                dve.wait_ge(*at("hn_done", 21))
                v.tensor_tensor(oT_flat[:, 4 * T:8 * T], oT_flat[:, 4 * T:8 * T], zT_flat, ALU.mult).then_inc(sem("o_ready"), 1)
        dve.wait_ge(*at("ms_rows", 1))
        step(v.tensor_copy(ms[0:32, :], B[0][0:32, 0:256]))
        step(v.tensor_reduce(stat[0:32, 0:1], ms[0:32, :], AX, ALU.max))
        v.tensor_scalar(stat[0:32, 1:2], stat[0:32, 0:1], -(HD_M ** -0.5), None, ALU.mult).then_inc(sem("ms_m"), 1)
        dve.wait_ge(*at("gates", 2))
        merge(1, [0])
        dve.wait_ge(*at("ms_e", 1))
        step(v.reciprocal(stat[0:32, 2:3], stat[0:32, 2:3]))
        v.tensor_scalar(ms[0:32, :], ms[0:32, :], stat[0:32, 2:3], None, ALU.mult).then_inc(sem("ms_p"), 1)
        merge(1, [1])
        dve.wait_ge(*at("ms_pT_ps", 1))
        v.tensor_copy(ms_pT, B[1][:, 0:64]).then_inc(sem("ms_pT"), 1)
        merge(1, [2, 3, 4])
        for j in range(2):
            dve.wait_ge(*at("ms_oT", j + 1))
            for h in range(H_M):
                a = P * h + 16 * j + h
                ins = v.tensor_copy(oT[:, 8 + h, NP_TOK + 4 * j:NP_TOK + 4 * j + 4], B[j][:, a:a + 109:36])
        ins.then_inc(sem("ms_done"), 1)
        merge(1, range(5, 8))
        dve.wait_ge(*at("gates", 3))
        merge(2)
        for d in range(8):
            dve.wait_ge(*at("out_ps", d + 1))
            v.tensor_tensor(xT[:, d, :], xT[:, d, :], B[d % 4][:, 0:T], ALU.add).then_inc(sem("x1"), 1)
        dve.wait_ge(*at("ln_rt", 3))
        for k in range(KD):
            v.scalar_tensor_tensor(hT[:, k, :], xT[:, k, :], column(LN2 + k), rr[:, 0:T], ALU.mult, ALU.mult).then_inc(sem("h2_ready"), 1)
        step(v.memset(lg_n, 0.0))
        v.memset(top_flat, 0.0)
        step(v.memset(top_i, 0))
        dve.wait_ge(*at("lg_nat", 1))
        v.tensor_tensor(lg_n[:, 0:2, :], grid(B[5][:, 0:64], 32), mid(brow_b, 2), ALU.add)
        step(v.tensor_tensor(lg_n[0:NB, 2, :], B[5][0:NB, 64:96], brow_b[0:NB, :], ALU.add))
        for c, (a, n) in enumerate(TOK):
            ins = v.max(top_v[0:n, c, :], lg_n[0:n, c, :])
        step(ins)
        for c, (a, n) in enumerate(TOK):
            v.max_index(top_i[0:n, c, :], top_v[0:n, c, :], lg_n[0:n, c, :])
        v.tensor_tensor(top_p, top_v[:, :, 0:4], top_v[:, :, 0:1].broadcast_to([P, 3, 4]), ALU.subtract).then_inc(sem("top"), 1)
        dve.wait_ge(*at("top", 1))
        step(v.tensor_copy(top_f, top_i))
        step(v.tensor_tensor(hot4, iota32.unsqueeze(1).unsqueeze(1).broadcast_to([P, 3, 4, 32]), bc(top_f[:, :, 0:4], 32), ALU.is_equal))
        step(v.tensor_reduce(sel_n, hot4.rearrange("p c k e -> p c e k"), AX, ALU.add))
        v.tensor_copy(sel4, sel_n.unsqueeze(2).broadcast_to([P, 3, 4, 32])).then_inc(sem("sel"), 1)
        dve.wait_ge(*at("top_e", 1))
        dve.wait_ge(*at("moe_ready", 1))
        step(v.tensor_reduce(top_s, top_p, AX, ALU.add))
        step(v.reciprocal(top_s, top_s))
        step(v.tensor_tensor(top_p, top_p, bc(top_s, 4), ALU.mult))
        step(v.tensor_tensor(hot4, hot4, bc(top_p, 32), ALU.mult))
        v.tensor_reduce(gate_n, hot4.rearrange("p c k e -> p c e k"), AX, ALU.add).then_inc(sem("gate_ready"), 1)
        dve.wait_ge(*at("rank", 1))
        v.scalar_tensor_tensor(pos_n[:, 0:2, :], grid(B[5][:, 0:64], 32), 1.0, sel_n[:, 0:2, :], ALU.add, ALU.mult)
        step(v.scalar_tensor_tensor(pos_n[0:NB, 2, :], B[5][0:NB, 64:96], 1.0, sel_n[0:NB, 2, :], ALU.add, ALU.mult))
        v.tensor_scalar(pos_n[:, 0:2, :], pos_n[:, 0:2, :], -1.0, None, ALU.add)
        step(v.tensor_scalar(pos_n[0:NB, 2, :], pos_n[0:NB, 2, :], -1.0, None, ALU.add))

        def build_pick(e, first):
            for c, (a, n) in enumerate(TOK):
                at_e = pos_n[0:n, c, bass.ds(e, 1)]
                ins = v.tensor_scalar(pick[0:n, c, :], places[0:n, bass.ds(first, BLK)], at_e, None, ALU.is_equal)
            ins.then_inc(sem("picks"), 1)

        for c, (a, n) in enumerate(TOK):
            ins = v.tensor_scalar(pick_0[0:n, c, :], places[0:n, 0:BLK], pos_n[0:n, c, 0:1], None, ALU.is_equal)
        ins.then_inc(sem("pick_0"), 1)
        dve.wait_ge(*at("counts", 1))
        v.tensor_tensor(more_f, B[7][:, 0:1], thr_col, ALU.is_gt).then_inc(sem("more"), 1)
        dve.wait_ge(*at("more_ps", 1))
        step(v.tensor_copy(more_pos, B[7][:, 8:9]))
        step(v.tensor_scalar(item_f[0:1, 0:1], B[7][0:1, 12:13], float(N_EXP), None, ALU.add))
        v.tensor_scalar(item_hot, iota32[:, 0:16], more_pos, more_f, ALU.is_equal, ALU.mult).then_inc(sem("hot"), 1)
        v.tensor_copy(item_expert[0:1, 0:N_EXP], iota32[0:1, :])
        v.tensor_copy(item_count[0:1, :], item_f[0:1, :])
        dve.wait_ge(*at("hot_ps", 1))
        v.tensor_copy(item_expert[0:1, N_EXP:N_EXP + EXTRA], B[7][0:1, 16:32])
        step(v.tensor_scalar(item_first[0:1, N_EXP:N_EXP + EXTRA], B[7][0:1, 32:48], 2.0, None, ALU.mult))
        dve.nop().then_inc(sem("items_ready"), 1)

        dve.wait_ge(*at("h2_hi", 3))
        dve.wait_ge(*at("xg_ps", 1))
        for c, (a, n) in enumerate(TOK):
            t0 = h2_nat[0:n, c, :]
            step(v.tensor_tensor(t0, t0, h2_parts[0:n, 0, c, :], ALU.subtract))
            step(v.tensor_copy(h2_parts[0:n, 1, c, :], t0))
            v.tensor_tensor(h2_parts[0:n, 2, c, :], t0, h2_parts[0:n, 1, c, :], ALU.subtract).then_inc(sem("h2_split"), 1)

        dve.wait_ge(*at("b1_done", 1))
        dve.wait_ge(*at("items_ready", 1))
        n_items = dve.value_load(item_count[0:1, 0:1], min_val=N_EXP, max_val=N_EXP + EXTRA)
        dve.nop().then_inc(sem("h_sum"), 1)
        with dve.Fori(0, n_items) as item:
            dve.wait_ge(*at("xg_ps", item + 1))
            build_pick(dve.value_load(item_expert[0:1, bass.ds(item + 1, 1)], min_val=0, max_val=N_EXP - 1),
                       dve.value_load(item_first[0:1, bass.ds(item + 1, 1)], min_val=0, max_val=P * (N_BLK - 1)))
            e = dve.value_load(item_expert[0:1, bass.ds(item, 1)], min_val=0, max_val=N_EXP - 1)
            first = dve.value_load(item_first[0:1, bass.ds(item, 1)], min_val=0, max_val=P * (N_BLK - 1))
            dve.wait_ge(*at("put_ps", item))
            for c, (a, n) in enumerate(TOK):
                ins = v.tensor_scalar(gpick[0:n, c, :], places[0:n, bass.ds(first, P)], pos_n[0:n, c, bass.ds(e, 1)],
                                      gate_n[0:n, c, bass.ds(e, 1)], ALU.is_equal, ALU.mult)
            ins.then_inc(sem("gpicks"), 1)
            for n in range(4):
                dve.wait_ge(*at("h_odd", item * 4 + (n + 1)))
                own = slice(512 * n, 512 * n + 512)
                v.tensor_tensor(h_sum[0:BLK, own], B[n][0:BLK, :], h_odd[0:BLK, own], ALU.add).then_inc(sem("h_sum"), 1)
            b1 = b1_e[:, bass.ds(e, 1), :].rearrange("p i f -> p (i f)")
            dve.wait_ge(*at("hT_ps", item * 2 + 1))
            v.tensor_tensor(grid(glu, BLK), grid(B[0][:, :], BLK), bc(b1[:, 0:8], BLK), ALU.add).then_inc(sem("e_step"), 1)
            dve.wait_ge(*at("e_step", item * 4 + 1))
            v.tensor_scalar(glu, glu, LIMIT, None, ALU.min).then_inc(sem("glu"), 1)
            dve.wait_ge(*at("hT_ps", item * 2 + 2))
            v.tensor_tensor(grid(lin, BLK), grid(B[1][:, :], BLK), bc(b1[:, 8:16], BLK), ALU.add).then_inc(sem("e_step"), 1)
            dve.wait_ge(*at("e_step", item * 4 + 2))
            v.tensor_scalar(lin, lin, LIMIT, -LIMIT, ALU.min, ALU.max).then_inc(sem("e_step"), 1)
            dve.wait_ge(*at("e_step", item * 4 + 3))
            dve.wait_ge(*at("glu", item + 1))
            v.scalar_tensor_tensor(lin, lin, 1.0, glu, ALU.add, ALU.mult).then_inc(sem("e_step"), 1)
            dve.wait_ge(*at("e_step", item * 4 + 4))
            dve.wait_ge(*at("sg", item + 1))
            v.tensor_tensor(act_e, lin, sg, ALU.mult).then_inc(sem("act"), 1)
        dve.wait_ge(*at("acc_done", n_items))
        for d in range(KD):
            dve.wait_ge(*at("scat_ps", n_items * 8 + (d + 1)))
            v.tensor_tensor(xT[:, d, :], xT[:, d, :], B[6 + d % 2][:, 0:T], ALU.add).then_inc(sem("last_add"), 1)
        for c in (0, 2):
            n = TOK[c][1]
            dve.wait_ge(*at("y_ps", 4 + c))
            v.tensor_copy(y_out[0:n, c, 512:1024], B[2 * c + 1][0:n, :]).then_inc(sem("y_dve"), 1)


_INS = ['x_prompt', 'x_sample', 'cache_swa_k', 'cache_swa_v', 'state_gdn', 'state_conv', 'cache_mem_k', 'cache_mem_v',
        'mem_prompt', 'ln1_gain', 'w_in', 'q_norm_swa', 'k_norm_swa', 'swa_sinks', 'conv_w', 'a_log', 'dt_bias',
        'gdn_norm', 'q_norm_mem', 'k_norm_mem', 'mem_norm', 'w_mem_kv', 'w_branch', 'w_out', 'ln2_gain', 'w_router',
        'b_router', 'w_mlp1', 'b_mlp1', 'w_mlp2', 'b_mlp2']
_OUTS = [('y_p', (1, 256, 1024)), ('y_s', (8, 1, 1024)), ('swa_kp', (1, 1, 128, 2, 64)), ('swa_vp', (1, 1, 128, 2, 64)),
         ('swa_ks', (1, 8, 128, 2, 64)), ('swa_vs', (1, 8, 128, 2, 64)), ('gdn_p', (1, 1, 4, 128, 128)),
         ('gdn_s', (1, 8, 4, 128, 128)), ('conv_p', (1, 1, 3, 1536)), ('conv_s', (1, 8, 3, 1536)),
         ('mem_k', (1, 1, 256, 4, 128)), ('mem_v', (1, 1, 256, 4, 128))]


def kernel(**inputs):
    import numpy as _np
    import concourse.bacc as _bacc
    from concourse import mybir as _mybir
    from concourse.bass_utils import run_bass_kernel_spmd as _run

    nc = _bacc.Bacc("TRN2", target_bir_lowering=False, num_devices=1)
    arrays, A, O = {}, {}, {}
    for name in _INS:
        a = _np.ascontiguousarray(inputs[name])
        arrays[f"in_{name}"] = a
        A[name] = nc.dram_tensor(f"in_{name}", a.shape, _mybir.dt.from_np(a.dtype), kind="ExternalInput").ap()
    for name, shape in _OUTS:
        O[name] = nc.dram_tensor(f"out_{name}", shape, _mybir.dt.float32, kind="ExternalOutput").ap()
    build_layer(nc, A, O)
    r = _run(nc, [arrays], core_ids=[0])
    return tuple(r.results[0][f"out_{name}"] for name, _ in _OUTS)
```
